# Optimizing a Trainium2 kernel written in Bass

```python
import math
import jax, jax.numpy as jnp
from jax import lax
import numpy as np

D_MODEL = 1024
BATCH = 1
SEQ = 1024
DEPTH = 1

D_MIX = 2 * D_MODEL
D_CONV = D_MIX // 2
D_LRU = D_MIX - D_CONV
CONV_GROUPS = 8
LRU_HEADS = 8
LRU_HEAD_DIM = D_LRU // LRU_HEADS
CONV_KERNEL = 31
SHORT_CONV = 4
LRU_C = 8.0
D_IN = 3 * D_CONV + 2 * D_LRU
EPS = 1e-6


def rmsnorm(x, g):
    xf = x.astype(jnp.float32)
    y = xf * lax.rsqrt(jnp.mean(xf * xf, axis=-1, keepdims=True) + EPS)
    return (y * g.astype(jnp.float32)).astype(x.dtype)

def layernorm(x, g, b):
    xf = x.astype(jnp.float32)
    mu = jnp.mean(xf, axis=-1, keepdims=True)
    var = jnp.mean(jnp.square(xf - mu), axis=-1, keepdims=True)
    y = (xf - mu) * lax.rsqrt(var + EPS)
    return (y * g.astype(jnp.float32) + b.astype(jnp.float32)).astype(x.dtype)

def causal_depthwise_conv(v, w, b):
    k, ch = w.shape
    y = lax.conv_general_dilated(
        v, w.astype(v.dtype)[:, None, :], window_strides=(1,),
        padding=[(k - 1, 0)], dimension_numbers=("NWC", "WIO", "NWC"),
        feature_group_count=ch)
    return y + b.astype(v.dtype)

def linear_scan(a, bx):
    def step(h, inp):
        a_t, b_t = inp
        h = a_t * h + b_t
        return h, h
    h0 = jnp.zeros((a.shape[0], a.shape[2]), jnp.float32)
    _, hs = lax.scan(step, h0, (jnp.swapaxes(a, 0, 1), jnp.swapaxes(bx, 0, 1)))
    return jnp.swapaxes(hs, 0, 1)

def first_inputs(seed: int = 0) -> dict:
    key = jax.random.key(seed)
    ks = jax.random.split(key, 24)
    f32 = jnp.float32
    nrm = lambda k, s, sc: (jax.random.normal(k, s, f32) * sc)
    x = jax.random.normal(ks[0], (BATCH, SEQ, D_MODEL), f32)
    c = jax.random.normal(ks[1], (BATCH, D_MODEL), f32)
    norm_g = 1.0 + nrm(ks[2], (DEPTH, D_MODEL), 0.05)
    mod_w = nrm(ks[3], (DEPTH, D_MODEL, 3 * D_MODEL), 0.5 * D_MODEL ** -0.5)
    mod_b = nrm(ks[4], (DEPTH, 3 * D_MODEL), 0.02)
    w_in = nrm(ks[5], (DEPTH, D_MODEL, D_IN), D_MODEL ** -0.5)
    dw_w = nrm(ks[6], (DEPTH, CONV_KERNEL, D_CONV), CONV_KERNEL ** -0.5)
    dw_b = nrm(ks[7], (DEPTH, D_CONV), 0.02)
    cln_g = 1.0 + nrm(ks[8], (DEPTH, D_CONV), 0.05)
    cln_b = nrm(ks[9], (DEPTH, D_CONV), 0.02)
    pw2_w = nrm(ks[10], (DEPTH, D_CONV, D_CONV), D_CONV ** -0.5)
    pw2_b = nrm(ks[11], (DEPTH, D_CONV), 0.02)
    sc_w = nrm(ks[12], (DEPTH, SHORT_CONV, D_LRU), SHORT_CONV ** -0.5)
    sc_b = nrm(ks[13], (DEPTH, D_LRU), 0.02)
    wr = nrm(ks[14], (DEPTH, LRU_HEADS, LRU_HEAD_DIM, LRU_HEAD_DIM), LRU_HEAD_DIM ** -0.5)
    br = nrm(ks[15], (DEPTH, D_LRU), 0.02)
    wi = nrm(ks[16], (DEPTH, LRU_HEADS, LRU_HEAD_DIM, LRU_HEAD_DIM), LRU_HEAD_DIM ** -0.5)
    bi = nrm(ks[17], (DEPTH, D_LRU), 0.02)
    a0 = jax.random.uniform(ks[18], (DEPTH, D_LRU), f32, 0.9, 0.999)
    s = a0 ** (1.0 / LRU_C)
    lam = jnp.log(s) - jnp.log1p(-s)
    w_out = nrm(ks[19], (DEPTH, D_MIX, D_MODEL), D_MIX ** -0.5)
    final_g = 1.0 + nrm(ks[20], (D_MODEL,), 0.05)
    return {"x": x, "c": c, "norm_g": norm_g, "mod_w": mod_w, "mod_b": mod_b,
            "w_in": w_in, "dw_w": dw_w, "dw_b": dw_b, "cln_g": cln_g, "cln_b": cln_b,
            "pw2_w": pw2_w, "pw2_b": pw2_b, "sc_w": sc_w, "sc_b": sc_b,
            "wr": wr, "br": br, "wi": wi, "bi": bi, "lam": lam,
            "w_out": w_out, "final_g": final_g}

def first_block(x, c, norm_g, mod_w, mod_b, w_in, dw_w, dw_b, cln_g, cln_b,
              pw2_w, pw2_b, sc_w, sc_b, wr, br, wi, bi, lam, w_out, final_g):
    bsz, seq, _ = x.shape
    c_act = jax.nn.silu(c)
    for l in range(DEPTH):
        mod = c_act @ mod_w[l] + mod_b[l]
        shift, scale, gate = jnp.split(mod, 3, axis=-1)
        h = rmsnorm(x, norm_g[l]) * (1.0 + scale[:, None, :]) + shift[:, None, :]

        u = h @ w_in[l]
        cv, cg, cs, lx, ls = jnp.split(
            u, [D_CONV, 2 * D_CONV, 3 * D_CONV, 3 * D_CONV + D_LRU], axis=-1)

        v = cv * jax.nn.sigmoid(cg)
        v = causal_depthwise_conv(v, dw_w[l], dw_b[l])
        v = jax.nn.silu(layernorm(v, cln_g[l], cln_b[l]))
        v = v @ pw2_w[l] + pw2_b[l]
        y_conv = v * jax.nn.silu(cs)

        xs = causal_depthwise_conv(lx, sc_w[l], sc_b[l])
        xh = xs.reshape(bsz, seq, LRU_HEADS, LRU_HEAD_DIM)
        r = jax.nn.sigmoid(jnp.einsum("bshd,hde->bshe", xh, wr[l]).reshape(bsz, seq, D_LRU) + br[l])
        i = jax.nn.sigmoid(jnp.einsum("bshd,hde->bshe", xh, wi[l]).reshape(bsz, seq, D_LRU) + bi[l])
        log_a = (-LRU_C * r.astype(jnp.float32)
                 * jax.nn.softplus(-lam[l].astype(jnp.float32)))
        a = jnp.exp(log_a)
        mult = jnp.sqrt(-jnp.expm1(2.0 * log_a))
        bx = mult * (i * xs).astype(jnp.float32)
        hs = linear_scan(a, bx).astype(x.dtype)
        y_lru = hs * jax.nn.silu(ls)

        y = jnp.concatenate([y_conv, y_lru], axis=-1) @ w_out[l]
        x = x + (1.0 + gate[:, None, :]) * y
    return rmsnorm(x, final_g)


GRID_W = 64
CTX_LEN = 256
N_MIXERS = 2
M_HEADS = 4
M_DV = D_MODEL // M_HEADS
M_DK = M_DV // 2
M_CHUNK = 128
M_PROJ = 2 * M_HEADS * M_DK + 2 * M_HEADS * M_DV + 4 * M_HEADS
F_GROUPS = 8
F_GROUP_DIM = D_MODEL // F_GROUPS
FFN_DIM = 2816
CONV_W = 3


def rmsnorm_2(x, g):
    x32 = x.astype(jnp.float32)
    y = x32 * lax.rsqrt(jnp.mean(x32 * x32, axis=-1, keepdims=True) + EPS)
    return (y * g.astype(jnp.float32)).astype(x.dtype)

def modulate(h, shift, scale):
    return h * (1 + scale[..., None, :]) + shift[..., None, :]

def _ctx_stream_needed(layer):
    return any(j % N_MIXERS == 0 for j in range(layer + 1, DEPTH))

def mlstm_project(h, w_in, b_in):
    B, T, _ = h.shape
    hk, hv = M_HEADS * M_DK, M_HEADS * M_DV
    p = h @ w_in + b_in
    q, k, v, o, gates = jnp.split(p, [hk, 2 * hk, 2 * hk + hv, 2 * hk + 2 * hv], axis=-1)

    def heads(t, d):
        return t.reshape(B, T, M_HEADS, d).transpose(0, 2, 1, 3).astype(jnp.float32)

    q = heads(q, M_DK)
    k = heads(k, M_DK) * (M_DK ** -0.5)
    v = heads(v, M_DV)
    g = gates.astype(jnp.float32).reshape(B, T, 4, M_HEADS).transpose(2, 0, 3, 1)
    fwd = (g[0], jax.nn.log_sigmoid(g[1]))
    bwd = (g[2], jax.nn.log_sigmoid(g[3]))
    return q, k, v, o, fwd, bwd

def mlstm_zero_state(B):
    return (jnp.zeros((B, M_HEADS, M_DK, M_DV), jnp.float32),
            jnp.zeros((B, M_HEADS, M_DK), jnp.float32),
            jnp.zeros((B, M_HEADS), jnp.float32))

def mlstm_chunk_scan(q, k, v, logi, logf, state0, with_outputs):
    B, H, T, _ = q.shape
    L = M_CHUNK
    nc = T // L

    def chunks(t):
        return jnp.moveaxis(t.reshape((B, H, nc, L) + t.shape[3:]), 2, 0)

    tri = jnp.tril(jnp.ones((L, L), dtype=bool))

    def step(carry, inp):
        C, n, m = carry
        qc, kc, vc, li, lf = inp
        b = jnp.cumsum(lf, axis=-1)
        bL = b[..., -1]
        g_s = bL[..., None] - b + li
        m_new = jnp.maximum(bL + m, jnp.max(g_s, axis=-1))
        a = jnp.exp(bL + m - m_new)
        ws = jnp.exp(g_s - m_new[..., None])
        C_new = a[..., None, None] * C + jnp.einsum('bhs,bhsd,bhse->bhde', ws, kc, vc)
        n_new = a[..., None] * n + jnp.einsum('bhs,bhsd->bhd', ws, kc)
        if not with_outputs:
            return (C_new, n_new, m_new), None
        dmat = jnp.where(tri, b[..., :, None] - b[..., None, :] + li[..., None, :], -jnp.inf)
        inter = b + m[..., None]
        m_t = jnp.maximum(inter, jnp.max(dmat, axis=-1))
        w_inter = jnp.exp(inter - m_t)
        s = jnp.einsum('bhtd,bhsd->bhts', qc, kc) * jnp.exp(dmat - m_t[..., None])
        num = w_inter[..., None] * jnp.einsum('bhtd,bhde->bhte', qc, C) + jnp.einsum('bhts,bhse->bhte', s, vc)
        den = w_inter * jnp.einsum('bhtd,bhd->bht', qc, n) + jnp.sum(s, axis=-1)
        h = num / jnp.maximum(jnp.abs(den), jnp.exp(-m_t))[..., None]
        return (C_new, n_new, m_new), h

    state, hs = lax.scan(step, state0, (chunks(q), chunks(k), chunks(v), chunks(logi), chunks(logf)))
    if with_outputs:
        hs = jnp.moveaxis(hs, 0, 2).reshape(B, H, T, M_DV)
    return hs, state

def mlstm_direction(q, k, v, gates, state0, reverse, with_outputs):
    logi, logf = gates
    if reverse:
        q, k, v = q[:, :, ::-1], k[:, :, ::-1], v[:, :, ::-1]
        logi, logf = logi[..., ::-1], logf[..., ::-1]
    h, state = mlstm_chunk_scan(q, k, v, logi, logf, state0, with_outputs)
    if reverse and with_outputs:
        h = h[:, :, ::-1]
    return h, state

def mlstm_readout(h, o, norm_g, w_out):
    B, H, T, _ = h.shape
    hn = h * lax.rsqrt(jnp.mean(h * h, axis=-1, keepdims=True) + EPS)
    hn = hn * norm_g.astype(jnp.float32).reshape(H, 1, M_DV)
    hn = hn.transpose(0, 2, 1, 3).reshape(B, T, H * M_DV)
    y = (hn * jax.nn.sigmoid(o.astype(jnp.float32))).astype(o.dtype)
    return y @ w_out

def mlstm_mixer(hx, hc, w_in, b_in, norm_g, w_out, ctx_outputs):
    B = hx.shape[0]
    s0 = mlstm_zero_state(B)
    qc, kc, vc, oc, gfc, gbc = mlstm_project(hc, w_in, b_in)
    hcf, st_f = mlstm_direction(qc, kc, vc, gfc, s0, False, ctx_outputs)
    hcb, st_b = mlstm_direction(qc, kc, vc, gbc, s0, True, ctx_outputs)
    qx, kx, vx, ox, gfx, gbx = mlstm_project(hx, w_in, b_in)
    hxf, _ = mlstm_direction(qx, kx, vx, gfx, st_f, False, True)
    hxb, _ = mlstm_direction(qx, kx, vx, gbx, st_b, True, True)
    yx = mlstm_readout(hxf + hxb, ox, norm_g, w_out)
    yc = mlstm_readout(hcf + hcb, oc, norm_g, w_out) if ctx_outputs else None
    return yx, yc

def fourier_mixer(h, w_out, b_out):
    B, T, D = h.shape
    hg = h.astype(jnp.float32).reshape(B, T, F_GROUPS, F_GROUP_DIM)
    y = jnp.real(jnp.fft.fft2(hg, axes=(1, 3), norm="ortho")).reshape(B, T, D).astype(h.dtype)
    return y @ w_out + b_out

def dwconv3(g, w, b, axis):
    n = g.shape[axis]
    pad = [(0, 0)] * g.ndim
    pad[axis] = (1, 1)
    gp = jnp.pad(g, pad)
    return (lax.slice_in_dim(gp, 0, n, axis=axis) * w[0]
            + lax.slice_in_dim(gp, 1, n + 1, axis=axis) * w[1]
            + lax.slice_in_dim(gp, 2, n + 2, axis=axis) * w[2] + b)

def conv_ffn(h, up_w, conv_w, conv_b, down_w, on_grid):
    u, g = jnp.split(h @ up_w, 2, axis=-1)
    if on_grid:
        B, T, F = g.shape
        rows = T // GRID_W
        g = dwconv3(g.reshape(B, rows, GRID_W, F), conv_w, conv_b, axis=2).reshape(B, T, F)
    else:
        g = dwconv3(g, conv_w, conv_b, axis=1)
    return (jax.nn.silu(g) * u) @ down_w

def second_inputs(seed: int = 0) -> dict:
    key = jax.random.key(seed)
    ks = jax.random.split(key, 24)
    D, F = D_MODEL, FFN_DIM
    NA = (DEPTH + N_MIXERS - 1) // N_MIXERS
    NB = DEPTH // N_MIXERS
    nrm = jax.random.normal
    x = nrm(ks[0], (BATCH, SEQ, D), jnp.float32)
    c = nrm(ks[1], (BATCH, D), jnp.float32)
    ctx = nrm(ks[2], (BATCH, CTX_LEN, D), jnp.float32)
    c_ctx = nrm(ks[3], (D,), jnp.float32)
    ada_w = nrm(ks[4], (DEPTH, D, 6 * D), jnp.float32) * D ** -0.5
    ada_b = 0.02 * nrm(ks[5], (DEPTH, 6 * D), jnp.float32)
    pre_mix_g = 1.0 + 0.05 * nrm(ks[6], (DEPTH, D), jnp.float32)
    post_mix_g = 1.0 + 0.05 * nrm(ks[7], (DEPTH, D), jnp.float32)
    pre_ffn_g = 1.0 + 0.05 * nrm(ks[8], (DEPTH, D), jnp.float32)
    post_ffn_g = 1.0 + 0.05 * nrm(ks[9], (DEPTH, D), jnp.float32)
    ffn_up_w = nrm(ks[10], (DEPTH, D, 2 * F), jnp.float32) * D ** -0.5
    ffn_conv_w = nrm(ks[11], (DEPTH, CONV_W, F), jnp.float32) * CONV_W ** -0.5
    ffn_conv_b = 0.02 * nrm(ks[12], (DEPTH, F), jnp.float32)
    ffn_down_w = nrm(ks[13], (DEPTH, F, D), jnp.float32) * F ** -0.5
    m_in_w = nrm(ks[14], (NA, D, M_PROJ), jnp.float32) * D ** -0.5
    lin_b = 0.02 * nrm(ks[15], (NA, M_PROJ - 4 * M_HEADS), jnp.float32)
    f_base = jnp.linspace(3.0, 6.0, M_HEADS, dtype=jnp.float32)
    gn = 0.1 * nrm(ks[16], (NA, 4, M_HEADS), jnp.float32)
    gate_b = gn + jnp.stack([jnp.zeros_like(f_base), f_base, jnp.zeros_like(f_base), f_base])[None]
    m_in_b = jnp.concatenate([lin_b, gate_b.reshape(NA, 4 * M_HEADS)], axis=-1)
    m_norm_g = 1.0 + 0.05 * nrm(ks[17], (NA, M_HEADS * M_DV), jnp.float32)
    m_out_w = nrm(ks[18], (NA, M_HEADS * M_DV, D), jnp.float32) * (M_HEADS * M_DV) ** -0.5
    f_out_w = nrm(ks[19], (NB, D, D), jnp.float32) * D ** -0.5
    f_out_b = 0.02 * nrm(ks[20], (NB, D), jnp.float32)
    return {"x": x, "c": c, "ctx": ctx, "c_ctx": c_ctx,
            "ada_w": ada_w, "ada_b": ada_b,
            "pre_mix_g": pre_mix_g, "post_mix_g": post_mix_g,
            "pre_ffn_g": pre_ffn_g, "post_ffn_g": post_ffn_g,
            "ffn_up_w": ffn_up_w, "ffn_conv_w": ffn_conv_w, "ffn_conv_b": ffn_conv_b,
            "ffn_down_w": ffn_down_w,
            "m_in_w": m_in_w, "m_in_b": m_in_b, "m_norm_g": m_norm_g, "m_out_w": m_out_w,
            "f_out_w": f_out_w, "f_out_b": f_out_b}

def second_block(x, c, ctx, c_ctx, ada_w, ada_b, pre_mix_g, post_mix_g, pre_ffn_g, post_ffn_g,
              ffn_up_w, ffn_conv_w, ffn_conv_b, ffn_down_w,
              m_in_w, m_in_b, m_norm_g, m_out_w, f_out_w, f_out_b):
    cx = jax.nn.silu(c)
    cc = jax.nn.silu(c_ctx)
    h_ctx = ctx
    for i in range(DEPTH):
        is_mlstm = (i % N_MIXERS) == 0
        j = i // N_MIXERS
        ctx_out = _ctx_stream_needed(i)
        sh1, sc1, g1, sh2, sc2, g2 = jnp.split(cx @ ada_w[i] + ada_b[i], 6, axis=-1)
        if is_mlstm or ctx_out:
            csh1, csc1, cg1, csh2, csc2, cg2 = jnp.split(cc @ ada_w[i] + ada_b[i], 6, axis=-1)
        hx = modulate(rmsnorm_2(x, pre_mix_g[i]), sh1, sc1)
        if is_mlstm:
            hc = modulate(rmsnorm_2(h_ctx, pre_mix_g[i]), csh1, csc1)
            yx, yc = mlstm_mixer(hx, hc, m_in_w[j], m_in_b[j], m_norm_g[j], m_out_w[j], ctx_out)
        else:
            yx = fourier_mixer(hx, f_out_w[j], f_out_b[j])
            if ctx_out:
                hc = modulate(rmsnorm_2(h_ctx, pre_mix_g[i]), csh1, csc1)
                yc = fourier_mixer(hc, f_out_w[j], f_out_b[j])
        x = x + g1[..., None, :] * rmsnorm_2(yx, post_mix_g[i])
        if ctx_out:
            h_ctx = h_ctx + cg1[..., None, :] * rmsnorm_2(yc, post_mix_g[i])
        hx = modulate(rmsnorm_2(x, pre_ffn_g[i]), sh2, sc2)
        yx = conv_ffn(hx, ffn_up_w[i], ffn_conv_w[i], ffn_conv_b[i], ffn_down_w[i], True)
        x = x + g2[..., None, :] * rmsnorm_2(yx, post_ffn_g[i])
        if ctx_out:
            hc = modulate(rmsnorm_2(h_ctx, pre_ffn_g[i]), csh2, csc2)
            yc = conv_ffn(hc, ffn_up_w[i], ffn_conv_w[i], ffn_conv_b[i], ffn_down_w[i], False)
            h_ctx = h_ctx + cg2[..., None, :] * rmsnorm_2(yc, post_ffn_g[i])
    return x


def setup_inputs(seed=0):
    out = dict(first_inputs(seed))
    for name, value in second_inputs(seed + 1).items():
        if name != "x":
            out[name + "_2"] = value
    return out


def reference(
    x, c, norm_g, mod_w, mod_b, w_in, dw_w, dw_b, cln_g, cln_b, pw2_w, pw2_b, sc_w, sc_b, wr,
    br, wi, bi, lam, w_out, final_g, c_2, ctx_2, c_ctx_2, ada_w_2, ada_b_2, pre_mix_g_2,
    post_mix_g_2, pre_ffn_g_2, post_ffn_g_2, ffn_up_w_2, ffn_conv_w_2, ffn_conv_b_2,
    ffn_down_w_2, m_in_w_2, m_in_b_2, m_norm_g_2, m_out_w_2, f_out_w_2, f_out_b_2,
):
    x = first_block(
        x, c, norm_g, mod_w, mod_b, w_in, dw_w, dw_b, cln_g, cln_b, pw2_w, pw2_b, sc_w, sc_b,
        wr, br, wi, bi, lam, w_out, final_g,
    )
    return second_block(
        x, c_2, ctx_2, c_ctx_2, ada_w_2, ada_b_2, pre_mix_g_2, post_mix_g_2, pre_ffn_g_2,
        post_ffn_g_2, ffn_up_w_2, ffn_conv_w_2, ffn_conv_b_2, ffn_down_w_2, m_in_w_2, m_in_b_2,
        m_norm_g_2, m_out_w_2, f_out_w_2, f_out_b_2,
    )


_drawn_inputs = setup_inputs


def setup_inputs(seed=0):
    import zlib

    import numpy as np

    out = dict(_drawn_inputs(seed))
    spreads = {}
    factors = {'dw_b': 3.961,
     'cln_b': 6.651,
     'pw2_b': 3.675,
     'br': 8.0,
     'bi': 5.924,
     'ffn_conv_b_2': 7.823}
    for name, (base, spread) in spreads.items():
        noise = np.random.default_rng([zlib.crc32(name.encode()), seed]).standard_normal(out[name].shape)
        drawn = base * np.exp(spread * noise) if base else spread * noise
        out[name] = __import__('jax').numpy.asarray(drawn.astype(out[name].dtype))
    for name, factor in factors.items():
        out[name] = (out[name] * factor).astype(out[name].dtype)
    return out
```

```python
from contextlib import ExitStack

import concourse.bass as bass
from concourse import mybir

F32 = mybir.dt.float32
F32R = mybir.dt.float32r
ALU = mybir.AluOpType
ACT = mybir.ActivationFunctionType
ds = bass.ds

P = 128
EPS = 1e-6
BIG = 1e30
GRID = 64


def block_pair_kernel(nc, A, out):
    x, ctx = A["x"][0], A["ctx_2"][0]
    SEQ, D = x.shape
    CTX = ctx.shape[0]
    KD = D // P
    NT = SEQ // P
    NC = CTX // P
    TAPS = A["dw_w"].shape[1]
    SHORT = A["sc_w"].shape[1]
    FFN = A["ffn_down_w_2"].shape[1]
    KF = FFN // P
    HEADS, DK, DV = 4, P, D // 4
    ALL = CTX + SEQ
    NCH = ALL // P
    HQ = HEADS * DK
    MP = A["m_in_w_2"].shape[2]
    GATE_ROW = MP - 4 * HEADS
    LRU_C = 8.0
    LOG1P_TERMS = 9
    VW = DV + 1

    mod_w, w_in, pw2_w, w_out = A["mod_w"][0], A["w_in"][0], A["pw2_w"][0], A["w_out"][0]
    ada_w, m_in_w, m_out_w = A["ada_w_2"][0], A["m_in_w_2"][0], A["m_out_w_2"][0]
    up_w, down_w = A["ffn_up_w_2"][0], A["ffn_down_w_2"][0]

    def dram(name, shape):
        return nc.dram_tensor(name, shape, F32).ap()

    xT_d = dram("xT_d", [D, SEQ])
    ctxT_d = dram("ctxT_d", [D, CTX])
    lru_d = dram("lru_d", [D, SEQ])
    cs_d = dram("cs_d", [D, SEQ])
    x2_d = dram("x2_d", [D, SEQ])
    proj_d = dram("proj_d", [MP, ALL])
    lf_d = dram("lf_d", [2 * HEADS, ALL])
    rows_d = dram("rows_d", [5 * 2 * HEADS, ALL])
    h_d = dram("h_d", [2, SEQ, D])
    act_d = dram("act_d", [FFN, SEQ])

    stage_rows, col, fill = [], {}, [0]

    def place(name, src, n):
        if fill[0] % P + n > P:
            fill[0] += P - fill[0] % P
        col[name] = fill[0]
        stage_rows.append((fill[0] // P, fill[0] % P, n, src))
        fill[0] += n

    def vec(a):
        return a.rearrange("(k p) -> k p", p=P)

    for name in ("norm_g", "mod_b", "dw_b", "cln_g", "cln_b", "pw2_b", "sc_b", "br", "bi", "lam"):
        place(name, vec(A[name][0]), A[name].shape[1] // P)
    place("c", vec(A["c"][0]), KD)
    place("sc_w", A["sc_w"][0].rearrange("t (k p) -> (t k) p", p=P), SHORT * KD)
    for name in ("pre_mix_g_2", "post_mix_g_2", "pre_ffn_g_2", "post_ffn_g_2", "m_norm_g_2", "ffn_conv_b_2", "ada_b_2"):
        place(name, vec(A[name][0]), A[name].shape[1] // P)
    place("c_2", vec(A["c_2"][0]), KD)
    place("final_g", vec(A["final_g"]), KD)
    dw = A["dw_w"][0].rearrange("t (k p) -> (t k) p", p=P)
    for t0 in range(0, TAPS, P // KD):
        n = min(P // KD, TAPS - t0) * KD
        place(f"dw_w{t0}", dw[t0 * KD:t0 * KD + n, :], n)
    place("ffn_conv_w", A["ffn_conv_w_2"][0].rearrange("t (k p) -> (t k) p", p=P), 3 * KF)
    place("m_in_b", vec(A["m_in_b_2"][0][0:GATE_ROW]), GATE_ROW // P)
    place("gate_b", vec(A["m_in_b_2"][0][MP - P:MP]), 1)
    place("c_ctx", vec(A["c_ctx_2"]), KD)
    NST = (fill[0] + P - 1) // P

    with ExitStack() as ctxs:
        def sb(name, shape, dt=F32):
            return ctxs.enter_context(nc.sbuf_tensor(name, shape, dt))

        def sem(name):
            return ctxs.enter_context(nc.semaphore(name))

        sems = {}

        shared = {}

        def share(total, *events):
            at_count = 0
            for name, n in events:
                shared[name] = (total, at_count)
                at_count += n

        share("x_high", ("xh_L1", KD), ("xh_G1", KD), ("xh_G2", KD), ("xh_G3", KD), ("xh_c", KD), ("xh_r", NT), ("xh_G6", KD), ("xh_G7", KF))
        share("x_low", ("xl_L1", KD), ("xl_G1", KD), ("xl_G2", KD), ("xl_G3", KD), ("xl_c", KD), ("xl_Gx", KD), ("xl_r", NT), ("xl_G6", KD), ("xl_G7", KF))
        share("dve_stage", *((n, 1) for n in ("stage_zero", "pv", "pj", "mod_ok", "sc_ok", "var_ok", "n1_ms", "x1_used", "lf_sb", "rows_sb", "rec_zero", "n2_done")))
        share("pe_stage", *((n, 1) for n in ("stage_ps", "mean_ps", "var_ps", "stat1_ps", "stat1_ps2", "stat2_ps", "stat3_ps", "stat4_ps")))
        share("act_stage", *((n, 1) for n in ("lam_e", "ln_sd", "n1_sd1", "n1_sd2", "f_e", "n2_sd", "n3_sd", "n4_sd")))
        share("pool_stage", ("msum_zero", 1), ("pads_zero", 2), ("xssq_zero", 1))

        def ev(name):
            name = shared.get(name, (name, 0))[0]
            if name not in sems:
                sems[name] = sem(name)
            return sems[name]

        BEGIN_AT_ONE = ("ada_used", "cs_free0", "cs_free1", "res_free0", "res_free1", "read_free", "msum_ok", "num_ps", "xs_ok",
                        "ri_ps", "lru_out", "lru_y", "vpad_ok", "cs_out", "proj_out0", "proj_out1", "h_out0", "h_out1",
                        "ffn_conv", "ffn_silu", "act_sb", "xT_sb0", "xT_sb1", "xnT_sb0", "xnT_sb1", "xnT_pe0", "xnT_pe1",
                        "xT_out0", "xT_out1", "cs_sb", "ada_sb", "p_ok", "num_free", "yT_ok", "act_out", "bx")

        def at(name, n):
            return ev(name), n + (1 if name in BEGIN_AT_ONE else shared.get(name, (name, 0))[1])

        XH = sb("XH", [P, KD, SEQ], F32R)
        XL = sb("XL", [P, KD, SEQ], F32R)
        XCH = sb("XCH", [P, KD, CTX], F32R)
        XCL = sb("XCL", [P, KD, CTX], F32R)
        raw = [sb(f"raw{s}", [P, KD, P]) for s in range(2)]
        wh = [sb(f"wh{s}", [P, KD, P], F32R) for s in range(2)]
        wl = [sb(f"wl{s}", [P, KD, P], F32R) for s in range(2)]
        B1 = sb("B1", [P, KD, SEQ])
        B2 = sb("B2", [P, KD, SEQ])
        VP = SEQ + 32
        LP = SEQ + 4
        SCR = sb("SCR", [P, VP + LP + 5 * SEQ])
        PV = sb("PV", [P, NST * P])
        NJ = TAPS + SHORT + 6
        PJ = sb("PJ", [P, KD, NJ])
        ident = sb("ident", [P, P])
        avg = sb("avg", [P, P])
        mask = [sb(f"mask{d}", [P, P]) for d in range(2)]
        CA = sb("CA", [P, KD, 4])
        MOD = sb("MOD", [P, 3 * KD])
        ADA = sb("ADA", [P, 6 * KD, 2])
        SC = sb("SC", [P, 9, KD])
        eps = sb("eps", [P, 1])
        small = sb("small", [P, 6, 16])
        mprev = sb("mprev", [36, NCH])
        PJc = sb("PJc", [P, NJ])
        PJd = sb("PJd", [P, NJ])
        PJa = sb("PJa", [P, NJ])
        lam4 = sb("lam4", [P, 4, KD])
        cols = [sb(f"cols{d}", [P, 24]) for d in range(2)]
        PS = [ctxs.enter_context(nc.psum_tensor(f"PS{b}", [P, SEQ], F32)) for b in range(4)]

        vpad = SCR[:, 0:VP]
        lxpad = SCR[:, VP:VP + LP]
        T = [SCR[:, 0:SEQ], SCR[:, VP:VP + SEQ]] + [SCR[:, VP + LP + SEQ * n:VP + LP + SEQ * (n + 1)] for n in range(5)]
        LS = T[0][:, 0:5 * 2 * HEADS * ALL // P].rearrange("p (q w) -> p q w", q=5)
        b2 = B2[:].rearrange("p k t -> p (k t)")
        b1 = B1[:].rearrange("p k t -> p (k t)")

        ls_t, sg_t, vc_t, th_t, cs_t = (b2[:, n * D:(n + 1) * D] for n in range(3, 8))
        ada_t = b2[:, 0:3 * D].rearrange("p (k n) -> p k n", k=KD)
        xsH = XCH[:].rearrange("p k t -> p (k t)")[:, 0:SEQ]
        xsL = XCL[:].rearrange("p k t -> p (k t)")[:, 0:SEQ]
        xs_t, r_t, i_t, a_t, msum_t = T[2:7]

        def pcol(name, k=0):
            return PV[:, ds(k + col[name], 1)]

        def pvec(name, n):
            return PV[:, col[name]:col[name] + n]

        RF, RI, RB, RM, RZ, RO = (b2[0:36, ALL * n:ALL * (n + 1)] for n in range(6))
        UN = [b1[0:36, 2 * D + ALL * n:2 * D + ALL * (n + 1)] for n in range(4)] + [RB]
        RQ = [RI, RF, RO, RZ, RM]

        M = []
        for flat in (b1, b2):
            off, m = 0, {}
            for name, n, k in (("q", HQ, HEADS), ("k", HQ, HEADS), ("v", D, D // P), ("M", HQ, HEADS), ("U", HQ, HEADS),
                               ("kw", HQ, HEADS), ("va", HEADS * VW, HEADS), ("q2", HQ, HEADS), ("p", HQ, HEADS),
                               ("h", D, HEADS), ("C", HEADS * VW, HEADS)):
                m[name] = flat[:, off:off + n].rearrange("p (k n) -> p k n", k=k)
                off += n
            m["rows"] = flat[0:3 * HEADS, off:off + P]
            M.append(m)

        landed = [sem("landed0"), sem("landed1")]
        hi_done, lo_done, unit_used = sem("hi_done"), sem("lo_done"), sem("unit_used")
        taken = [sem("psum_taken0"), sem("psum_taken1")]
        gates_in = ev("gate_weights_landed")

        class Product:
            unit, tile = 0, 0

            def __init__(self, n, units=None, tiles=None):
                self.U, self.T, self.n = Product.unit, Product.tile, n
                Product.unit += units or n
                Product.tile += tiles or n
                self.end = Product.unit + 2

        L1 = Product(KD, 6 * KD, 4 * KD)
        G1a, G1b = Product(KD // 2), Product(KD // 2)
        G2, G3 = Product(KD), Product(KD)
        GcG, Gc = Product(1), Product(3 * HQ // P)
        GxG, Gx = Product(1), Product(GATE_ROW // P)
        G5 = Product(KD)
        G6 = Product(2 * KF)
        down = [(k, min(KD, KF - k)) for k in range(0, KF, KD)]
        G7 = [Product(KD) for _ in down]
        LAST_UNIT = Product.unit

        def cols_of(w, k0, kc, c):
            return w[k0 * P:(k0 + kc) * P, :].rearrange("(k p) n -> p k n", p=P)[:, :, ds(c, P)]

        class Chain:

            def __init__(self, eng, name):
                self.eng, self.sem, self.base, self.i, self.n, self.k = eng, ev(name), 0, 0, 0, 0

            def loop(self, i, n):
                self.base, self.i, self.n, self.k = self.base + self.k, i, n, 0

            def done(self, times):
                assert self.k == self.n, (self.k, self.n)
                self.base, self.i, self.n, self.k = self.base + self.n * times, 0, 0, 0

            def sig(self, ins):
                self.k += 1
                ins.then_inc(self.sem, 1)

            def wait(self, back=0):
                self.eng.wait_ge(self.sem, self.i * self.n + (self.base + self.k - back))

            def link(self, ins):
                self.sig(ins)
                self.wait()

        def bc(a, n):
            return a.rearrange("p (h o) -> p h o", o=1).to_broadcast([a.shape[0], a.shape[1], n])

        block = ctxs.enter_context(nc.Block())

        @block.sync
        def _(sp):
            def unit(U, slot, src, kc=KD, counted=False):
                sp.wait_ge(lo_done, U + 1)
                if counted:
                    sp.sem_inc(ev("sp_passed"), 1)
                sp.dma_start(raw[slot][:, 0:kc, :], src).then_inc(landed[slot], 16)

            def token_load(i, s, src):
                if i is not None:
                    sp.wait_ge(*at(f"xT_pe{s}", i))
                    sp.wait_ge(*at(f"xn_ok{s}", i))
                sp.dma_start(T[1 + s], src).then_inc(ev(f"tok_in{s}"), 16)

            for name in BEGIN_AT_ONE:
                sp.sem_inc(ev(name), 1)
            sp.wait_ge(*at("stage_zero", 1))
            for t, r, n, src in stage_rows:
                sp.dma_start(SCR[r:r + n, t * P:(t + 1) * P], src).then_inc(ev("stage_in"), 16)
            token_load(None, 0, x[0:P, :])
            token_load(None, 1, x[P:2 * P, :])
            with sp.Fori(0, NT // 2 - 1) as i:
                for s in range(2):
                    token_load(i + 1, s, x[ds(2 * P * i + (2 + s) * P, P), :])
            for s in range(NC):
                token_load(NT // 2, s, ctx[s * P:(s + 1) * P, :])
            for q in range(6):
                if q >= 2:
                    sp.wait_ge(*at("mod_used", q - 1))
                sp.dma_start(B2[:, 4 * (q % 2):4 * (q % 2) + 4, :].rearrange("p a (b n) -> p (a b) n", n=4 * P),
                             mod_w.rearrange("(k p) n -> p k n", p=P)[:, :, 4 * P * q:4 * P * (q + 1)]).then_inc(ev(f"mod_in{q % 2}"), 16)
            for s in range(NC):
                sp.wait_ge(*at(f"ctxT_sb{s}", 1))
                sp.dma_start(ctxT_d.rearrange("(k p) t -> p k t", p=P)[:, :, s * P:(s + 1) * P],
                             T[5 + s].rearrange("p (k t) -> p k t", k=KD)).then_inc(ev("ctxT_out"), 16)

            def l1_unit(j, pos):
                U = 6 * j + pos
                slot = pos % 2
                if pos == 2:
                    sp.wait_ge(lo_done, U + 1)
                    sp.dma_start(raw[0][:, 0:1, :], A["wr"][0][ds(j, 1)].rearrange("h d e -> d h e")).then_inc(landed[0], 16)
                    sp.dma_start(raw[0][:, 1:2, :], A["wi"][0][ds(j, 1)].rearrange("h d e -> d h e")).then_inc(gates_in, 16)
                else:
                    group = {0: 3, 1: 4, 3: 1, 4: 0, 5: 2}[pos]
                    unit(U, slot, cols_of(w_in, 0, KD, group * D + P * j), counted=group == 0)

            def ada_load(j, half):
                sp.wait_ge(*at("ada_used", 2 * j + half))
                sp.dma_start(b2[:, 0:3 * D].rearrange("p (k n) -> p k n", k=KD),
                             ada_w.rearrange("(k p) n -> p k n", p=P)[:, :, ds(6 * P * j + 3 * P * half, 3 * P)]).then_inc(ev("ada_in"), 16)

            def l1_store(j):
                sp.wait_ge(*at("lru_y", j + 1))
                sp.dma_start(lru_d[ds(P * j, P), :], ls_t).then_inc(ev("lru_out"), 16)
                sp.wait_ge(*at("cs_sb", j + 1))
                sp.dma_start(cs_d[ds(P * j, P), :], cs_t).then_inc(ev("cs_out"), 16)

            def l1_loads(j, stores):
                l1_unit(j, 0)
                l1_unit(j, 1)
                if stores:
                    l1_store(j - 1)
                l1_unit(j, 2)
                ada_load(j, 0)
                for pos in range(3, 6):
                    l1_unit(j, pos)
                ada_load(j, 1)

            sp.wait_ge(*at("mod_used", 6))
            l1_loads(0, False)
            with sp.Fori(1, KD) as j:
                l1_loads(j, True)
            for u in range(2):
                unit(G1a.U + u, u, cols_of(w_out, KD, KD, u * P))
            l1_store(KD - 1)

            for k in range(KD):
                sp.wait_ge(*at("lru_out", 16 * (k + 1)))
                if k >= 2:
                    sp.wait_ge(*at("xl_G1", k - 1))
                sp.dma_start(T[2 + k % 2], lru_d[k * P:(k + 1) * P, :]).then_inc(ev(f"lru_in{k % 2}"), 16)
            with sp.Fori(0, KD // 2 - 1) as i:
                for s in range(2):
                    unit(G1a.U + 2 + 2 * i + s, s, cols_of(w_out, KD, KD, 2 * P * i + (2 + s) * P))

            def cs_load(t, s, i):
                sp.wait_ge(*at(f"cs_free{s}", i))
                sp.dma_start(T[s], cs_d[ds(P * t, P), :]).then_inc(ev(f"cs_in{s}"), 16)

            sp.wait_ge(*at("cs_out", 16 * KD))
            sp.wait_ge(*at("conv_ok", KD))
            with sp.Fori(0, KD // 2) as i:
                for s in range(2):
                    unit(G2.U + 2 * i + s, s, cols_of(pw2_w, 0, KD, 2 * P * i + s * P))
                    cs_load(2 * i + s, s, i)

            for s in range(2):
                sp.wait_ge(*at(f"cs_free{s}", KD // 2))
                sp.wait_ge(*at(f"xT_out{s}", 16 * NT // 2))
            with sp.Fori(0, KD // 2) as i:
                for s in range(2):
                    unit(G3.U + 2 * i + s, s, cols_of(w_out, 0, KD, 2 * P * i + s * P))
                    sp.wait_ge(*at(f"res_free{s}", i))
                    sp.dma_start(T[s], xT_d[ds(2 * P * i + s * P, P), :]).then_inc(ev(f"res_in{s}"), 16)
            sp.wait_ge(*at("ctxT_out", 16 * NC))
            sp.wait_ge(unit_used, G3.end)
            sp.dma_start(B1[:, 2:4, :].rearrange("p a (b t) -> p (a b) t", t=CTX),
                         ctxT_d.rearrange("(k p) t -> p k t", p=P)).then_inc(ev("ctx_in"), 16)

            def proj_store(n, s, row, c0, c1):
                sp.wait_ge(*at("proj_sb", n + 1))
                sp.dma_start(proj_d[ds(row, P), c0:c1], B1[:, s, 0:c1 - c0]).then_inc(ev(f"proj_out{s}"), 16)

            unit(GcG.U, 0, cols_of(m_in_w, 0, KD, MP - P))
            unit(Gc.U, 1, cols_of(m_in_w, 0, KD, HQ))
            sp.wait_ge(*at("proj_sb", 1))
            sp.dma_start(proj_d[GATE_ROW:MP, 0:CTX], B1[P - 4 * HEADS:P, 0, 0:CTX]).then_inc(ev("proj_out0"), 16)
            with sp.Fori(0, Gc.n // 2 - 1) as i:
                for s in range(2):
                    unit(Gc.U + 1 + 2 * i + s, s, cols_of(m_in_w, 0, KD, HQ + 2 * P * i + (1 + s) * P))
                    proj_store(2 * i + s + 1, 1 - s, 2 * P * i + HQ + s * P, 0, CTX)
            unit(Gc.U + Gc.n - 1, 0, cols_of(m_in_w, 0, KD, HQ + (Gc.n - 1) * P))
            proj_store(Gc.n - 1, 1, HQ + (Gc.n - 2) * P, 0, CTX)
            unit(GxG.U, 1, cols_of(m_in_w, 0, KD, MP - P))
            proj_store(Gc.n, 0, HQ + (Gc.n - 1) * P, 0, CTX)
            for k in range(KD):
                sp.wait_ge(*at("x2_sb", k + 1))
                sp.dma_start(x2_d[k * P:(k + 1) * P, :], T[2 + k % 2]).then_inc(ev(f"x2_out{k % 2}"), 16)
            unit(Gx.U, 0, cols_of(m_in_w, 0, KD, 0))
            sp.wait_ge(*at("proj_sb", Gc.n + 2))
            sp.dma_start(proj_d[GATE_ROW:MP, CTX:ALL], B1[P - 4 * HEADS:P, 1, :]).then_inc(ev("proj_out1"), 16)

            W = ALL // 16
            sp.wait_ge(*at("proj_out0", 16))
            sp.wait_ge(*at("proj_out1", 16 * (1 + Gc.n // 2)))
            sp.wait_ge(*at("proj_out0", 16 * (1 + Gc.n // 2)))
            sp.wait_ge(*at("x1_used", 1))
            for d in range(2):
                r = GATE_ROW + (2 * d + 1) * HEADS
                sp.dma_start(LS[64 * d:64 * d + 64, 0, :], proj_d[r:r + HEADS, :].rearrange("h (a w) -> (h a) w", w=W)).then_inc(ev("f_in"), 16)
            sp.dma_start(RI[0:HEADS, :], proj_d[GATE_ROW:GATE_ROW + HEADS, :]).then_inc(ev("rows_in"), 16)
            sp.dma_start(UN[0][32:32 + HEADS, :], proj_d[GATE_ROW + 2 * HEADS:GATE_ROW + 3 * HEADS, :]).then_inc(ev("rows_in"), 16)
            sp.wait_ge(*at("lf_sb", 1))
            sp.dma_start(lf_d.rearrange("h (a w) -> (h a) w", w=W), LS[:, 0, :]).then_inc(ev("lf_out"), 16)
            sp.wait_ge(*at("lf_out", 16))
            sp.dma_start(RF[0:HEADS, :], lf_d[0:HEADS, :]).then_inc(ev("rows_in"), 16)
            sp.dma_start(UN[1][32:32 + HEADS, :], lf_d[HEADS:2 * HEADS, :]).then_inc(ev("rows_in"), 16)

            with sp.Fori(0, Gx.n // 2 - 1) as i:
                for s in range(2):
                    unit(Gx.U + 1 + 2 * i + s, 1 - s, cols_of(m_in_w, 0, KD, 2 * P * i + (1 + s) * P))
                    proj_store(2 * i + s + Gc.n + 2, s, 2 * P * i + s * P, CTX, ALL)
            unit(Gx.U + Gx.n - 1, 1, cols_of(m_in_w, 0, KD, (Gx.n - 1) * P))
            unit(G5.U, 0, cols_of(m_out_w, 0, KD, 0))
            proj_store(Gx.n - 2 + Gc.n + 2, 0, (Gx.n - 2) * P, CTX, ALL)
            proj_store(Gx.n - 1 + Gc.n + 2, 1, (Gx.n - 1) * P, CTX, ALL)
            sp.wait_ge(*at("rows_sb", 1))
            for q, (f, b) in enumerate(zip(RQ, UN)):
                sp.dma_start(rows_d[q * 2 * HEADS:q * 2 * HEADS + HEADS, :], f[0:HEADS, :]).then_inc(ev("rows_out"), 16)
                sp.dma_start(rows_d[q * 2 * HEADS + HEADS:(q + 1) * 2 * HEADS, :], b[32:32 + HEADS, :]).then_inc(ev("rows_out"), 16)
            sp.wait_ge(*at("rows_out", 16 * 10))
            for s in range(2):
                sp.wait_ge(*at(f"proj_out{s}", 16 * (1 + (Gc.n + Gx.n) // 2)))

            def chunk_load(n, d, c, first=False, outputs=True):
                m = M[d]
                if not first:
                    sp.wait_ge(*at(f"chunk_free{d}", n))
                def load(dst, src, name="chunk_in"):
                    sp.dma_start(dst, src).then_inc(ev(f"{name}{d}"), 16)
                for dst, r0, k in ((m["k"], HQ, HEADS), (m["v"], 2 * HQ, D // P)):
                    load(dst, proj_d[r0:r0 + k * P, :].rearrange("(h p) t -> p h t", p=P)[:, :, ds(c, P)])
                for q in range(3):
                    r = q * 2 * HEADS + d * HEADS
                    load(m["rows"][q * HEADS:(q + 1) * HEADS, :], rows_d[r:r + HEADS, ds(c, P)])
                for q, dst in ((3, m["U"]), (4, m["M"])):
                    r = q * 2 * HEADS + d * HEADS
                    load(dst, rows_d[r:r + HEADS, ds(c, P)].rearrange("(o h) t -> o h t", o=1).to_broadcast([P, HEADS, P]))
                if outputs:
                    load(m["q"], proj_d[0:HQ, :].rearrange("(h p) t -> p h t", p=P)[:, :, ds(c, P)], "q_in")

            for j in range(NC):
                chunk_load(j, 0, j * P, j == 0, False)
                chunk_load(j, 1, (NC - 1 - j) * P, j == 0, False)
            with sp.Fori(0, NT) as j:
                chunk_load(j + NC, 0, j * P + CTX)
                chunk_load(j + NC, 1, j * (-P) + (ALL - P))
                for d in range(2):
                    sp.wait_ge(*at(f"h_sb{d}", j + 1))
                    t = j * P if d == 0 else j * (-P) + (SEQ - P)
                    sp.dma_start(h_d[d][ds(t, P), :], M[d]["h"].rearrange("p h e -> p (h e)")).then_inc(ev(f"h_out{d}"), 16)

            for d in range(2):
                sp.wait_ge(*at(f"h_out{d}", 16 * NT))
            with sp.Fori(0, NT) as c:
                sp.wait_ge(*at("read_free", c))
                sp.dma_start(T[0], h_d[0][ds(P * c, P), :]).then_inc(ev("read_in"), 16)
                sp.dma_start(T[1], h_d[1][ds(P * c, P), :]).then_inc(ev("read_in"), 16)
                sp.dma_start(T[2].rearrange("p (k t) -> p k t", k=KD),
                             proj_d[GATE_ROW - D:GATE_ROW, :].rearrange("(k p) t -> p k t", p=P)[:, :, ds(P * c + CTX, P)]).then_inc(ev("read_in"), 16)
            with sp.Fori(0, (KD - 2) // 2) as i:
                for s in range(2):
                    unit(G5.U + 1 + 2 * i + s, 1 - s, cols_of(m_out_w, 0, KD, 2 * P * i + (1 + s) * P))
            unit(G5.U + KD - 1, 1, cols_of(m_out_w, 0, KD, (KD - 1) * P))
            unit(G6.U, 0, cols_of(up_w, 0, KD, FFN))
            for s in range(2):
                sp.wait_ge(*at(f"x2_out{s}", 16 * KD // 2))
            sp.wait_ge(*at("read_free", NT))
            for k in range(KD):
                if k >= 2:
                    sp.wait_ge(*at("x3_sb", k - 1))
                sp.dma_start(T[k % 2], x2_d[k * P:(k + 1) * P, :]).then_inc(ev(f"x2_in{k % 2}"), 16)
            def act_store(j):
                sp.wait_ge(*at("act_sb", j + 1))
                sp.dma_start(act_d[ds(P * j, P), :], T[2]).then_inc(ev("act_out"), 16)

            with sp.Fori(0, KF - 1) as j:
                unit(G6.U + 1 + 2 * j, 1, cols_of(up_w, 0, KD, P * j))
                unit(G6.U + 2 + 2 * j, 0, cols_of(up_w, 0, KD, P * j + (FFN + P)))
                act_store(j)
            unit(G6.U + 2 * KF - 1, 1, cols_of(up_w, 0, KD, (KF - 1) * P))
            unit(G7[0].U, 0, cols_of(down_w, 0, KD, 0))
            act_store(KF - 1)
            n = 0
            sp.wait_ge(*at("act_out", 16 * KF))
            for g, (k0, kc) in enumerate(down):
                for k in range(kc):
                    if n >= 2:
                        sp.wait_ge(*at("xl_G7", n - 1))
                    sp.dma_start(T[4 + n % 2], act_d[(k0 + k) * P:(k0 + k + 1) * P, :]).then_inc(ev(f"act_in{n % 2}"), 16)
                    n += 1
                with sp.Fori(0, (KD - 2) // 2) as i:
                    for s in range(2):
                        unit(G7[g].U + 1 + 2 * i + s, 1 - s, cols_of(down_w, k0, kc, 2 * P * i + (1 + s) * P), kc)
                unit(G7[g].U + KD - 1, 1, cols_of(down_w, k0, kc, (KD - 1) * P), kc)
                if g + 1 < len(down):
                    unit(G7[g + 1].U, 0, cols_of(down_w, down[g + 1][0], down[g + 1][1], 0), down[g + 1][1])
            with sp.Fori(0, NT // 2) as i:
                for s in range(2):
                    sp.wait_ge(*at("fin_sb", 2 * i + s + 1))
                    sp.dma_start(out[0][ds(2 * P * i + s * P, P), :], T[2 + s]).then_inc(ev(f"fin_out{s}"), 16)
            for s in range(2):
                sp.wait_ge(*at(f"fin_out{s}", 16 * NT // 2))

        @block.gpsimd
        def _(pool):
            step = Chain(pool, "pool_step")
            tt = nc.gpsimd.tensor_tensor

            def low(U, slot, kc=KD):
                pool.wait_ge(hi_done, U + 1)
                tt(wl[slot][:, 0:kc, :], raw[slot][:, 0:kc, :], wh[slot][:, 0:kc, :].bitcast(F32), ALU.subtract).then_inc(lo_done, 1)

            pool.sem_inc(lo_done, 2)
            nc.gpsimd.memset(ident[:], 0.0).then_inc(step.sem, 1)
            nc.gpsimd.memset(avg[:], 1.0 / D).then_inc(step.sem, 1)
            nc.gpsimd.memset(mask[0][:], 0.0).then_inc(step.sem, 1)
            nc.gpsimd.memset(mask[1][:], 0.0).then_inc(step.sem, 1)
            nc.gpsimd.memset(eps[:], EPS).then_inc(step.sem, 1)
            step.k = 5
            step.wait()
            nc.gpsimd.affine_select(out=ident[:], in_=ident[:], compare_op=ALU.not_equal, fill=1.0, base=0,
                                    pattern=[[-1, P]], channel_multiplier=1).then_inc(ev("consts"), 1)
            nc.gpsimd.affine_select(out=mask[0][:], in_=mask[0][:], compare_op=ALU.is_ge, fill=BIG, base=0,
                                    pattern=[[1, P]], channel_multiplier=-1).then_inc(ev("consts"), 1)
            nc.gpsimd.affine_select(out=mask[1][:], in_=mask[1][:], compare_op=ALU.is_ge, fill=BIG, base=0,
                                    pattern=[[-1, P]], channel_multiplier=1).then_inc(ev("consts"), 1)

            low(0, 0)
            pool.wait_ge(*at("xl_L1", KD))
            nc.gpsimd.memset(msum_t, 0.0).then_inc(ev("msum_zero"), 1)
            nc.gpsimd.memset(vpad[:, 0:TAPS - 1], 0.0).then_inc(ev("pads_zero"), 1)
            nc.gpsimd.memset(lxpad[:, 0:SHORT - 1], 0.0).then_inc(ev("pads_zero"), 1)

            def conv_sum(j):
                pool.wait_ge(*at("conv_ok", j + 1))
                pool.wait_ge(*at("msum_ok", j))
                pool.wait_ge(*at("msum_zero", 1))
                tt(msum_t, msum_t, B1[:, ds(j, 1), :].rearrange("p a t -> p (a t)"), ALU.add).then_inc(ev("msum_ok"), 1)

            def l1_pool(j, summed):
                U = 6 * j
                low(U + 1, 1)
                pool.wait_ge(*at("xsh", j + 1))
                tt(xsL, xs_t, xsH.bitcast(F32), ALU.subtract).then_inc(ev("xsl"), 1)
                low(U + 2, 0, 2)
                low(U + 3, 1)
                pool.wait_ge(*at("i_ok", j + 1))
                tt(i_t, i_t, xs_t, ALU.mult).then_inc(ev("ixs"), 1)
                low(U + 4, 0)
                pool.wait_ge(*at("th_ok", j + 1))
                tt(th_t, th_t, r_t, ALU.mult).then_inc(ev("m2"), 1)
                low(U + 5, 1)
                low(U + 6, 0)
                pool.wait_ge(*at("mult_ok", j + 1))
                tt(i_t, th_t, i_t, ALU.mult).then_inc(ev("bx"), 1)
                if summed:
                    conv_sum(j - 1)
                pool.wait_ge(*at("vc_ok", j + 1))
                pool.wait_ge(*at("pads_zero", 2))
                tt(vpad[:, TAPS - 1:TAPS - 1 + SEQ], vc_t, sg_t, ALU.mult).then_inc(ev("vpad_ok"), 1)

            l1_pool(0, False)
            with pool.Fori(1, KD) as j:
                l1_pool(j, True)

            for k in range(KD):
                pool.wait_ge(*at("xh_G1", k + 1))
                tt(XL[:, k, :], T[2 + k % 2], XH[:, k, :].bitcast(F32), ALU.subtract).then_inc(ev("xl_G1"), 1)

            def low_tiles(g, n=None):
                n = n or g.n
                if n >= 2:
                    with pool.Fori(0, n // 2) as i:
                        for s in range(2):
                            low(g.U + 1 + 2 * i + s, (g.U + 1 + s) % 2)
                if n % 2:
                    low(g.U + n, (g.U + n) % 2)

            for i in range(2):
                low(G1a.U + 1 + i, (G1a.U + 1 + i) % 2)
            conv_sum(KD - 1)
            for i in range(2, 4):
                low(G1a.U + 1 + i, (G1a.U + 1 + i) % 2)
            low_tiles(G1b)
            low_tiles(G2)
            pool.wait_ge(*at("xl_G2", KD))
            nc.gpsimd.memset(T[4], 0.0).then_inc(ev("ssq_ok"), 1)
            nc.gpsimd.memset(T[6], 0.0).then_inc(ev("ssq_ok"), 1)
            with pool.Fori(0, KD // 2) as i:
                for s in range(2):
                    low(G3.U + 1 + 2 * i + s, (G3.U + 1 + s) % 2)
                    pool.wait_ge(*at("sq_ok", 2 * i + s + 1))
                    pool.wait_ge(*at("ssq_ok", 2 * (2 * i + s) + 2))
                    tt(T[4], T[4], T[3], ALU.add).then_inc(ev("ssq_ok"), 1)
                    tt(T[6], T[6], T[5], ALU.add).then_inc(ev("ssq_ok"), 1)
            low_tiles(GcG)
            low_tiles(Gc)
            low_tiles(GxG)
            low_tiles(Gx)

            def q2(j, d):
                pool.wait_ge(*at(f"q_in{d}", 16 * (j + 1)))
                pool.wait_ge(*at("w_ok", 2 * NC + 2 * j + d + 1))
                pool.wait_ge(*at("num_ps", HEADS * (2 * j + d)))
                tt(M[d]["q2"], M[d]["q"], M[d]["U"], ALU.mult).then_inc(ev("q2_ok"), 1)

            with pool.Fori(0, NT) as j:
                for d in range(2):
                    q2(j, d)
            with pool.Fori(0, NT) as c:
                pool.wait_ge(*at("so_ok", c + 1))
                o = T[2].rearrange("p (k t) -> p k t", k=KD)
                tt(o, o, bc(pvec("m_norm_g_2", KD), P), ALU.mult).then_inc(ev("gate_ok"), 1)
            pool.wait_ge(*at("read_free", NT))
            pool.wait_ge(*at("xl_r", NT))
            nc.gpsimd.memset(T[4], 0.0).then_inc(ev("yssq_ok"), 1)
            nc.gpsimd.memset(T[5], 0.0).then_inc(ev("xssq_zero"), 1)
            with pool.Fori(0, KD // 2) as i:
                for s in range(2):
                    low(G5.U + 1 + 2 * i + s, (G5.U + 1 + s) % 2)
                    pool.wait_ge(*at("ysq_ok", 2 * i + s + 1))
                    pool.wait_ge(*at("yssq_ok", 2 * i + s + 1))
                    tt(T[4], T[4], T[3], ALU.add).then_inc(ev("yssq_ok"), 1)
            low_tiles(G6)
            for g in range(len(down)):
                last = g == len(down) - 1
                if not last:
                    low_tiles(G7[g])
                else:
                    nc.gpsimd.memset(T[0], 0.0).then_inc(ev("zssq_ok"), 1)
                    for t in range(KD):
                        if t < KD - 1:
                            low(G7[g].U + 1 + t, (G7[g].U + 1 + t) % 2, down[g][1])
                        pool.wait_ge(*at("zsq_ok", t + 1))
                        pool.wait_ge(*at("zssq_ok", t + 1))
                        tt(T[0], T[0], T[3], ALU.add).then_inc(ev("zssq_ok"), 1)

        @block.scalar
        def _(act):
            step = Chain(act, "act_step")
            f = nc.scalar.activation

            def high(U, slot, kc=KD):
                act.wait_ge(landed[slot], U // 2 * 16 + 16)
                act.wait_ge(unit_used, U + 1)
                f(wh[slot][:, 0:kc, :], raw[slot][:, 0:kc, :], ACT.Copy).then_inc(hi_done, 1)

            def high_at(base, i, kc=KD):
                act.wait_ge(landed[base % 2], 16 * i + 16 * (base // 2 + 1))
                act.wait_ge(unit_used, 2 * i + (base + 1))
                f(wh[base % 2][:, 0:kc, :], raw[base % 2][:, 0:kc, :], ACT.Copy).then_inc(hi_done, 1)

            def tiles(g, evac):
                if g.n >= 2:
                    with act.Fori(0, g.n // 2) as i:
                        for s in range(2):
                            high_at(g.U + 1 + s, i)
                            if evac:
                                act.wait_ge(unit_used, 2 * i + (g.U + s + 3))
                                evac(2 * i + s, PS[(g.T + s) % 2], taken[(g.T + s) % 2])
                if g.n % 2:
                    t = g.n - 1
                    high_at(g.U + t + 1, 0)
                    if evac:
                        act.wait_ge(unit_used, g.U + t + 3)
                        evac(t, PS[(g.T + t) % 2], taken[(g.T + t) % 2])

            act.wait_ge(*at("consts", 3))

            def token(i, s, transposed=True):
                act.wait_ge(*at(f"tok_in{s}", 16 * i + 16))
                act.wait_ge(*at(f"xnT_pe{s}", i))
                step.link(f(T[3 + s], T[1 + s], ACT.Square, accum_out=small[:, 0, s:s + 1]))
                f(small[:, 1, s:s + 1], small[:, 0, s:s + 1], ACT.Sqrt, scale=1.0 / D, bias=eps[:]).then_inc(ev(f"rms{s}"), 1)
                if transposed:
                    act.wait_ge(*at(f"xT_pe{s}", i + 1))
                    act.wait_ge(*at(f"xT_out{s}", 16 * i))
                    f(T[5 + s], PS[s][:], ACT.Copy).then_inc(ev(f"xT_sb{s}"), 1)
                    act.wait_ge(*at(f"xT_sb{s}", i + 1))
                    act.dma_start(xT_d.rearrange("(k p) t -> p k t", p=P)[:, :, ds(2 * P * i + s * P, P)],
                                  T[5 + s].rearrange("p (k t) -> p k t", k=KD)).then_inc(ev(f"xT_out{s}"), 16)

            with act.Fori(0, NT // 2) as i:
                step.loop(i, 2)
                for s in range(2):
                    token(i, s)
            step.done(NT // 2)
            for s in range(NC):
                token(NT // 2, s, False)

            act.wait_ge(*at("pv", 1))
            for n, name in enumerate(("c", "c", "c_2", "c_ctx")):
                f(CA[:, :, n], pvec(name, KD), ACT.Silu).then_inc(ev("ca"), 1)
            step.link(f(lam4[:, 0, :], pvec("lam", KD), ACT.Abs))
            f(lam4[:, 1, :], lam4[:, 0, :], ACT.Exp, scale=-1.0).then_inc(ev("lam_e"), 1)
            high(0, 0)
            act.wait_ge(*at("mod_ok", 1))
            for k in range(KD):
                f(XH[:, k, :], B1[:, k, :], ACT.Identity, scale=SC[:, 0, k:k + 1], bias=MOD[:, k:k + 1]).then_inc(ev("xh_L1"), 1)

            act.wait_ge(*at("pj", 1))

            def l1_act(j):
                U = 6 * j
                def land(pos):
                    act.wait_ge(landed[pos % 2], 48 * j + 16 * (pos // 2 + 1))
                def hi(pos, kc=KD):
                    land(pos)
                    act.wait_ge(unit_used, U + pos + 1)
                    f(wh[pos % 2][:, 0:kc, :], raw[pos % 2][:, 0:kc, :], ACT.Copy).then_inc(hi_done, 1)

                step.link(f(PJa[:], PJ[:, ds(j, 1), :].rearrange("p a n -> p (a n)"), ACT.Copy))
                hi(1)
                act.wait_ge(unit_used, U + 3)
                act.wait_ge(*at("xs_ok", j))
                f(lxpad[:, SHORT - 1:SHORT - 1 + SEQ], PS[0][:], ACT.Copy).then_inc(ev("lx_sb"), 1)
                act.wait_ge(*at("lx_sb", j + 1))
                act.sem_inc(taken[0], 1)
                act.wait_ge(*at("xs_ok", j + 1))
                act.wait_ge(*at("ri_ps", j))
                f(xsH, xs_t, ACT.Copy).then_inc(ev("xsh"), 1)
                act.wait_ge(gates_in, 16 * j + 16)
                hi(2, 2)
                act.wait_ge(unit_used, U + 4)
                act.wait_ge(*at("lru_out", 16 * j))
                f(ls_t, PS[1][:], ACT.Silu).then_inc(ev("ls_sb"), 1)
                act.wait_ge(*at("ls_sb", j + 1))
                act.sem_inc(taken[1], 1)
                hi(3)
                act.wait_ge(*at("ri_ps", j + 1))
                act.wait_ge(*at("lru_y", j))
                f(r_t, PS[2][:], ACT.Sigmoid, bias=PJa[:, TAPS + SHORT + 2:TAPS + SHORT + 3]).then_inc(ev("r_ok"), 1)
                f(i_t, PS[3][:], ACT.Sigmoid, bias=PJa[:, TAPS + SHORT + 3:TAPS + SHORT + 4]).then_inc(ev("i_ok"), 1)
                hi(4)
                act.wait_ge(unit_used, U + 6)
                act.wait_ge(*at("vpad_ok", j))
                f(sg_t, PS[0][:], ACT.Sigmoid).then_inc(taken[0], 1)
                act.wait_ge(*at("r_ok", j + 1))
                f(th_t, r_t, ACT.Tanh, scale=PJa[:, TAPS + SHORT + 5:TAPS + SHORT + 6]).then_inc(ev("th_raw"), 1)
                f(a_t, r_t, ACT.Exp, scale=PJa[:, TAPS + SHORT + 4:TAPS + SHORT + 5]).then_inc(ev("a_ok"), 1)
                act.wait_ge(*at("a_ok", j + 1))
                act.wait_ge(*at("th_raw", j + 1))
                step.link(f(r_t, a_t, ACT.Square))
                f(r_t, r_t, ACT.Copy, bias=1.0).then_inc(ev("th_ok"), 1)
                hi(5)
                act.wait_ge(unit_used, U + 7)
                f(vc_t, PS[1][:], ACT.Copy).then_inc(ev("vc_ok"), 1)
                act.wait_ge(*at("vc_ok", j + 1))
                act.sem_inc(taken[1], 1)
                act.wait_ge(landed[0], 48 * j + 64)
                act.wait_ge(unit_used, U + 7)
                f(wh[0][:], raw[0][:], ACT.Copy).then_inc(hi_done, 1)
                act.wait_ge(*at("m2", j + 1))
                f(th_t, th_t, ACT.Sqrt).then_inc(ev("mult_ok"), 1)
                act.wait_ge(*at("cs_ps", j + 1))
                act.wait_ge(*at("cs_out", 16 * j))
                f(cs_t, PS[2][:], ACT.Silu).then_inc(ev("cs_sb"), 1)

            with act.Fori(0, KD) as j:
                step.loop(j, 2)
                l1_act(j)
            step.done(KD)

            for k in range(KD):
                act.wait_ge(*at(f"lru_in{k % 2}", 16 * (k // 2 + 1)))
                if k == 0:
                    act.wait_ge(unit_used, L1.end)
                f(XH[:, k, :], T[2 + k % 2], ACT.Copy).then_inc(ev("xh_G1"), 1)
            act.wait_ge(*at("vpad_ok", KD))
            act.wait_ge(*at("cs_out", 16 * KD))
            act.wait_ge(*at("ada_used", 2 * KD))
            for g, k0 in ((G1a, 0), (G1b, KD // 2)):
                tiles(g, lambda t, ps, tk: f(B2[:, ds(t + k0, 1), :].rearrange("p a t -> p (a t)"), ps[:], ACT.Copy).then_inc(tk, 1))

            act.wait_ge(*at("var_ps", 1))
            f(T[3], PS[3][:], ACT.Sqrt, bias=eps[:]).then_inc(ev("ln_sd"), 1)
            for k in range(KD):
                act.wait_ge(*at("ln_t", k + 1))
                if k >= 2:
                    act.wait_ge(*at("xl_G2", k - 1))
                elif k == 1:
                    act.wait_ge(*at("ln_t", 2))
                step.link(f(T[2 + k % 2], B1[:, k, :], ACT.Silu, scale=pcol("cln_g", k), bias=pcol("cln_b", k)))
                if k == 0:
                    act.wait_ge(unit_used, G1b.end)
                f(XH[:, k, :], T[2 + k % 2], ACT.Copy).then_inc(ev("xh_G2"), 1)
            tiles(G2, None)
            for k in range(KD):
                act.wait_ge(*at("yconv_ok", KD))
                act.wait_ge(unit_used, G2.end)
                f(XH[:, k, :], B1[:, k, :], ACT.Copy).then_inc(ev("xh_G3"), 1)

            with act.Fori(0, KD // 2) as i:
                for s in range(2):
                    high_at(G3.U + 1 + s, i)
                    t = 2 * i + s
                    act.wait_ge(*at("x1_ok", t + 1))
                    act.wait_ge(*at("ssq_ok", 2 * t + 2))
                    x1 = B2[:, ds(t, 1), :].rearrange("p a t -> p (a t)")
                    f(T[3], x1, ACT.Square).then_inc(ev("sq1"), 1)
                    f(T[5], x1, ACT.Square, scale=pcol("final_g", t)).then_inc(ev("sq_ok"), 1)

            act.wait_ge(*at("ctx_in", 16))
            act.wait_ge(*at("sc_ok", 1))
            cn = B1[:, 2:4, :].rearrange("p a (b t) -> p (a b) t", t=CTX)
            for k in range(KD):
                f(XCH[:, k, :], cn[:, k, :], ACT.Identity, scale=SC[:, 4, k:k + 1], bias=ADA[:, k, 1:2]).then_inc(ev("xh_c"), 1)
            act.wait_ge(*at("stat1_ps2", 1))
            f(T[3], PS[2][:], ACT.Sqrt, bias=eps[:]).then_inc(ev("n1_sd1"), 1)
            act.wait_ge(*at("n1_ms", 1))
            f(T[3], T[1], ACT.Sqrt, bias=eps[:]).then_inc(ev("n1_sd2"), 1)

            def proj_tiles(g, n0, width, bias):
                def one(t, par, u_wait, ps, tk, hi_args):
                    s = (n0 + par) % 2
                    high_at(*hi_args)
                    act.wait_ge(unit_used, u_wait)
                    act.wait_ge(*at(f"proj_out{s}", 8 * t + 8 * (n0 - s)))
                    f(B1[:, s, 0:width], ps[:, 0:width], ACT.Identity, bias=bias(t)).then_inc(ev("proj_sb"), 1)
                    act.wait_ge(*at("proj_sb", t + (n0 + 1)))
                    act.sem_inc(tk, 1)
                if g.n >= 2:
                    with act.Fori(0, g.n // 2) as i:
                        for s in range(2):
                            one(2 * i + s, s, 2 * i + (g.U + s + 3), PS[(g.T + s) % 2], taken[(g.T + s) % 2], (g.U + 1 + s, i))
                else:
                    one(0, 0, g.U + 3, PS[g.T % 2], taken[g.T % 2], (g.U + 1, 0))

            proj_tiles(GcG, 0, CTX, lambda t: pcol("gate_b"))
            proj_tiles(Gc, 1, CTX, lambda t: pcol("m_in_b", t + HEADS))
            proj_tiles(GxG, 1 + Gc.n, SEQ, lambda t: pcol("gate_b"))
            act.wait_ge(*at("f_in", 32))
            step.link(f(LS[:, 1, :], LS[:, 0, :], ACT.Abs))
            f(LS[:, 1, :], LS[:, 1, :], ACT.Exp, scale=-1.0).then_inc(ev("f_e"), 1)
            proj_tiles(Gx, 2 + Gc.n, SEQ, lambda t: pcol("m_in_b", t))

            def chunk(q, n, d, j=None):
                m = M[d]
                act.wait_ge(*at(f"chunk_in{d}", 112 * n + 112))
                f(m["U"], m["U"], ACT.Exp).then_inc(ev("w_ok"), 1)
                act.wait_ge(*at("t_ps", q + 1))
                act.wait_ge(*at("rec_zero", 1))
                f(m["va"][:, :, 0:DV], PS[1][:].rearrange("p (h e) -> p h e", h=HEADS), ACT.Copy).then_inc(ev("va_ok"), 1)
                act.wait_ge(*at("cols_sb", q + 1))
                f(cols[d][:, 12:20], cols[d][:, 4:12], ACT.Exp).then_inc(ev("eg_ok"), 1)
                if j is not None:
                    x = 2 * j + d
                    act.wait_ge(*at("d_ok", x + 1))
                    f(m["M"], m["M"], ACT.Exp, scale=-1.0).then_inc(ev("e_ok"), 1)
                    for h in range(HEADS):
                        act.wait_ge(*at("rec_ok", HEADS * x + h + 1))
                        if h == 0:
                            act.wait_ge(*at(f"h_out{d}", 16 * j))
                        bank = (PS[2][:, 512:512 + DV], PS[3][:, 0:DV])[h % 2]
                        f(m["h"][:, h, :], bank, ACT.Copy, scale=cols[d][:, 20 + h:21 + h]).then_inc(ev("num_free"), 1)
                    act.wait_ge(*at("num_free", HEADS * x + HEADS))
                    act.sem_inc(ev(f"h_sb{d}"), 1)

            for n in range(NC):
                for d in range(2):
                    chunk(2 * n + d, n, d)
            with act.Fori(0, NT) as j:
                for d in range(2):
                    chunk(2 * j + (2 * NC + d), j + NC, d, j)

            with act.Fori(0, NT) as c:
                step.loop(c, 1)
                act.wait_ge(*at("read_in", 48 * c + 48))
                f(T[2], T[2], ACT.Sigmoid).then_inc(ev("so_ok"), 1)
                act.wait_ge(*at("hs_ok", c + 1))
                for h in range(HEADS):
                    ins = f(T[3][:, h * DV:(h + 1) * DV], T[0][:, h * DV:(h + 1) * DV], ACT.Square, accum_out=small[:, 3, h:h + 1])
                step.link(ins)
                f(small[:, 4, 0:HEADS], small[:, 3, 0:HEADS], ACT.Sqrt, scale=1.0 / DV, bias=eps[:]).then_inc(ev("hrms"), 1)
                act.wait_ge(*at("yT_ok", c + 1))
                f(XH[:, :, ds(P * c, P)], T[5].rearrange("p (k t) -> p k t", k=KD), ACT.Copy).then_inc(ev("xh_r"), 1)
            step.done(NT)

            with act.Fori(0, KD // 2) as i:
                for s in range(2):
                    high_at(G5.U + 1 + s, i)
                    t = 2 * i + s
                    b = (G5.T + s) % 2
                    act.wait_ge(unit_used, 2 * i + (G5.U + s + 3))
                    f(B1[:, ds(t, 1), :].rearrange("p a t -> p (a t)"), PS[b][:], ACT.Copy).then_inc(ev("y_sb"), 1)
                    act.wait_ge(*at("yssq_ok", t + 1))
                    f(T[3], PS[b][:], ACT.Square).then_inc(ev("ysq_ok"), 1)
                    act.wait_ge(*at("y_sb", t + 1))
                    act.wait_ge(*at("ysq_ok", t + 1))
                    act.sem_inc(taken[b], 1)
            act.wait_ge(*at("stat2_ps", 1))
            f(T[6], PS[2][:], ACT.Sqrt, bias=eps[:]).then_inc(ev("n2_sd"), 1)
            for k in range(KD):
                act.wait_ge(*at("x3_sb", k + 1))
                if k == 0:
                    act.wait_ge(*at("stat2_ps", 1))
                if k >= 2:
                    act.wait_ge(*at("xssq_ok", k - 1))
                f(T[2 + k % 2], B2[:, k, :], ACT.Square).then_inc(ev("xsq_ok"), 1)
            act.wait_ge(*at("stat3_ps", 1))
            act.wait_ge(*at("n2_done", 1))
            f(T[6], PS[3][:], ACT.Sqrt, bias=eps[:]).then_inc(ev("n3_sd"), 1)
            for k in range(KD):
                act.wait_ge(*at("h2_t", k + 1))
                if k == 0:
                    act.wait_ge(unit_used, G5.end)
                f(XH[:, k, :], T[2 + k % 2], ACT.Identity, bias=ADA[:, 3 * KD + k, 0:1]).then_inc(ev("xh_G6"), 1)
            with act.Fori(0, KF) as j:
                high_at(G6.U + 1, j)
                b = G6.T % 2
                act.wait_ge(unit_used, 2 * j + (G6.U + 3))
                act.wait_ge(*at("ffn_conv", j))
                act.wait_ge(*at("ffn_silu", j))
                f(T[0], PS[b][:], ACT.Copy).then_inc(ev("g_sb"), 1)
                f(T[1], PS[b][:], ACT.Identity, scale=pcol("ffn_conv_w", j + KF), bias=pcol("ffn_conv_b_2", j)).then_inc(ev("g_sb"), 1)
                act.wait_ge(*at("g_sb", 2 * j + 2))
                act.sem_inc(taken[b], 1)
                high_at(G6.U + 2, j)
                act.wait_ge(*at("ffn_conv", j + 1))
                act.wait_ge(*at("act_sb", j))
                f(T[3], T[1], ACT.Silu).then_inc(ev("ffn_silu"), 1)
            n = 0
            for g, (k0, kc) in enumerate(down):
                for k in range(kc):
                    act.wait_ge(*at(f"act_in{n % 2}", 16 * (n // 2 + 1)))
                    if k == 0:
                        act.wait_ge(unit_used, (G6 if g == 0 else G7[g - 1]).end)
                    f(XH[:, k, :], T[4 + n % 2], ACT.Copy).then_inc(ev("xh_G7"), 1)
                    n += 1
                if g < len(down) - 1:
                    tiles(G7[g], None)
                else:
                    for t in range(KD):
                        if t < KD - 1:
                            high_at(G7[g].U + 1 + t, 0, kc)
                        act.wait_ge(*at("z_ok", (g + 1) * KD - KD + t + 1))
                        act.wait_ge(*at("zssq_ok", t + 1))
                        f(T[3], B1[:, t, :], ACT.Square).then_inc(ev("zsq_ok"), 1)
            act.wait_ge(*at("stat4_ps", 1))
            f(T[6], PS[2][:], ACT.Sqrt, bias=eps[:]).then_inc(ev("n4_sd"), 1)
            for t in range(NT):
                act.wait_ge(*at("out_ps", t + 1))
                if t >= 2:
                    act.wait_ge(*at(f"fin_out{t % 2}", 16 * (t // 2)))
                f(T[2 + t % 2], PS[t % 2][:], ACT.Copy).then_inc(ev("fin_sb"), 1)

        @block.tensor
        def _(pe):
            mm = nc.tensor.matmul

            def product(ps, w, kc, X, n, first=0):
                XHt, XLt = X
                step_n = min(n, 512)
                total, seen = 3 * kc, 0
                for k in range(kc):
                    for W, Y in ((wh[w], XHt), (wl[w], XHt), (wh[w], XLt)):
                        for c in range(0, n, step_n):
                            last = mm(ps[:, c:c + step_n], W[:, k, :], Y[:, k, c:c + step_n], start=(seen == 0), stop=(seen == total - 1))
                        seen += 1
                return last

            def tile(U, slot, ps, tk, nth, kc=KD, X=(XH, XL), n=SEQ):
                pe.wait_ge(lo_done, U + 3)
                pe.wait_ge(tk, nth + 1)
                product(ps, slot, kc, X, n).then_inc(unit_used, 1)

            def tiles(g, **kw):
                if g.n >= 2:
                    with pe.Fori(0, g.n // 2) as i:
                        for s in range(2):
                            b = (g.T + s) % 2
                            tile(2 * i + (g.U + s), (g.U + s) % 2, PS[b], taken[b], i + (g.T + s) // 2, **kw)
                else:
                    tile(g.U, g.U % 2, PS[g.T % 2], taken[g.T % 2], g.T // 2, **kw)

            def stat(ps, src, event):
                for c in range(2):
                    last = mm(ps[:, 512 * c:512 * c + 512], avg[:], src[:, 512 * c:512 * c + 512], start=True, stop=True)
                last.then_inc(ev(event), 1)

            pe.sem_inc(unit_used, 2)
            pe.sem_inc(taken[0], 1)
            pe.sem_inc(taken[1], 1)
            pe.wait_ge(*at("consts", 3))
            pe.wait_ge(*at("stage_in", 16 * len(stage_rows)))
            for t in range(NST):
                last = nc.tensor.transpose(PS[2][:, t * P:(t + 1) * P], SCR[:, t * P:(t + 1) * P], ident[:])
            last.then_inc(ev("stage_ps"), 1)

            def token(i, s, both=True):
                if both:
                    pe.wait_ge(*at(f"tok_in{s}", 16 * i + 16))
                    pe.wait_ge(*at(f"xT_sb{s}", i))
                    for k in range(KD):
                        last = nc.tensor.transpose(PS[s][:, k * P:(k + 1) * P], T[1 + s][:, k * P:(k + 1) * P], ident[:])
                    last.then_inc(ev(f"xT_pe{s}"), 1)
                pe.wait_ge(*at(f"xn_ok{s}", i + 1))
                pe.wait_ge(*at(f"xnT_sb{s}", i))
                for k in range(KD):
                    last = nc.tensor.transpose(PS[2 + s][:, k * P:(k + 1) * P], T[3 + s][:, k * P:(k + 1) * P], ident[:])
                last.then_inc(ev(f"xnT_pe{s}"), 1)

            pe.wait_ge(*at("pv", 1))
            with pe.Fori(0, NT // 2) as i:
                for s in range(2):
                    token(i, s)
            for s in range(NC):
                token(NT // 2, s, False)
            pe.wait_ge(*at("ca", 4))
            pe.wait_ge(*at("ctxT_sb1", 1))
            for q in range(6):
                pe.wait_ge(*at(f"mod_in{q % 2}", 16 * (q // 2 + 1)))
                w = B2[:, 4 * (q % 2):4 * (q % 2) + 4, :].rearrange("p a (b n) -> p (a b) n", n=4 * P)
                for c in range(4):
                    for k in range(KD):
                        last = mm(PS[3][:, 8 * q + 2 * c:8 * q + 2 * c + 2], w[:, k, c * P:(c + 1) * P], CA[:, k, 0:2],
                                  start=(k == 0), stop=(k == KD - 1))
                last.then_inc(ev("mod_used"), 1)

            def ada(j, half):
                pe.wait_ge(*at("ada_in", 32 * j + 16 * (half + 1)))
                for c in range(3):
                    for k in range(KD):
                        last = mm(PS[3][:, 512 * half + 2 * c:512 * half + 2 * c + 2], ada_t[:, k, c * P:(c + 1) * P], CA[:, k, 2:4],
                                  start=(k == 0), stop=(k == KD - 1))
                last.then_inc(ev("ada_used"), 1)

            pe.wait_ge(*at("xl_L1", KD))
            with pe.Fori(0, KD) as j:
                U = 6 * j
                tile(U, 0, PS[0], taken[0], 2 * j)
                tile(U + 1, 1, PS[1], taken[1], 2 * j)
                pe.wait_ge(lo_done, U + 2 + 3)
                pe.wait_ge(*at("xsl", j + 1))
                pe.wait_ge(*at("cs_sb", j))
                pe.wait_ge(*at("ada_sb", j))
                for c, ps in enumerate((PS[2], PS[3])):
                    for n, (W, Y) in enumerate(((wh[0], xsH), (wl[0], xsH), (wh[0], xsL))):
                        for h in range(0, SEQ, 512):
                            last = mm(ps[:, h:h + 512], W[:, c, :], Y[:, h:h + 512], start=(n == 0), stop=(n == 2))
                last.then_inc(unit_used, 1)
                pe.wait_ge(unit_used, U + 5)
                pe.sem_inc(ev("ri_ps"), 1)
                tile(U + 3, 1, PS[0], taken[0], 2 * j + 1)
                pe.wait_ge(*at("i_ok", j + 1))
                ada(j, 0)
                tile(U + 4, 0, PS[1], taken[1], 2 * j + 1)
                pe.wait_ge(lo_done, U + 5 + 3)
                pe.wait_ge(*at("r_ok", j + 1))
                product(PS[2], 1, KD, (XH, XL), SEQ).then_inc(unit_used, 1)
                pe.wait_ge(unit_used, U + 8)
                pe.sem_inc(ev("cs_ps"), 1)
                ada(j, 1)

            pe.wait_ge(*at("xl_G1", KD))
            tiles(G1a)
            pe.wait_ge(*at("msum_ok", KD))
            pe.wait_ge(*at("cs_sb", KD))
            stat(PS[2], msum_t, "mean_ps")
            tiles(G1b)
            pe.wait_ge(*at("var_ok", 1))
            pe.wait_ge(*at("ada_sb", KD))
            stat(PS[3], T[5], "var_ps")
            pe.wait_ge(*at("xl_G2", KD))
            tiles(G2)
            pe.wait_ge(*at("xl_G3", KD))
            tiles(G3)
            pe.wait_ge(*at("ssq_ok", 2 * KD + 2))
            stat(PS[2], T[4], "stat1_ps")
            stat(PS[3], T[6], "stat1_ps2")
            pe.wait_ge(*at("xl_c", KD))
            for g in (GcG, Gc):
                tiles(g, X=(XCH, XCL), n=CTX)
            pe.wait_ge(*at("xl_Gx", KD))
            tiles(GxG)
            tiles(Gx)

            NUM = [PS[2][:, 512:512 + VW], PS[3][:, 0:VW]]
            DC = [PS[3][:, 512:512 + VW], PS[0][:, 512:512 + VW]]

            def chunk(q, n, d, j=None):
                m = M[d]
                pe.wait_ge(*at(f"chunk_in{d}", 112 * n + 112))
                pe.wait_ge(*at("kw_ok", q))
                pe.wait_ge(*at("va_ok", q))
                pe.wait_ge(*at("c_ok", HEADS * q))
                for h in range(HEADS):
                    nc.tensor.transpose(PS[0][:, h * P:(h + 1) * P], m["k"][:, h, :], ident[:])
                for h in range(D // P):
                    nc.tensor.transpose(PS[1][:, h * P:(h + 1) * P], m["v"][:, h, :], ident[:])
                nc.tensor.transpose(PS[0][:, 512:512 + 3 * HEADS], m["rows"], ident[0:3 * HEADS, 0:3 * HEADS]).then_inc(ev("t_ps"), 1)
                if j is not None:
                    x = 2 * j + d
                    pe.wait_ge(*at(f"q_in{d}", 16 * j + 16))
                    pe.wait_ge(*at("p_ok", x))
                    for h in range(HEADS):
                        last = mm(PS[2][:, h * P:(h + 1) * P], m["k"][:, h, :], m["q"][:, h, :], start=True, stop=True)
                    last.then_inc(ev("s_ps"), 1)
                    pe.wait_ge(*at("p_ok", x + 1))
                    pe.wait_ge(*at("q2_ok", x + 1))
                pe.wait_ge(*at("va_ok", q + 1))
                pe.wait_ge(*at("kw_ok", q + 1))
                for h in range(HEADS):
                    if j is not None:
                        if h >= 2:
                            pe.wait_ge(*at("num_free", HEADS * x + h - 1))
                        else:
                            pe.wait_ge(*at("num_free", HEADS * x))
                        mm(NUM[h % 2], m["p"][:, h, :], m["va"][:, h, :], start=True, stop=False)
                        mm(NUM[h % 2], m["q2"][:, h, :], m["C"][:, h, :], start=False, stop=True).then_inc(ev("num_ps"), 1)
                    if h >= 2:
                        pe.wait_ge(*at("c_ok", HEADS * q + h - 1))
                    mm(DC[h % 2], m["kw"][:, h, :], m["va"][:, h, :], start=True, stop=True).then_inc(ev("dc_ps"), 1)

            pe.wait_ge(taken[0], (G5.T + 1) // 2 + 1)
            pe.wait_ge(taken[1], G5.T // 2 + 1)
            pe.wait_ge(*at("rec_zero", 1))
            for n in range(NC):
                for d in range(2):
                    chunk(2 * n + d, n, d)
            with pe.Fori(0, NT) as j:
                for d in range(2):
                    chunk(2 * j + (2 * NC + d), j + NC, d, j)
            pe.wait_ge(*at("c_ok", HEADS * 2 * NCH))
            with pe.Fori(0, NT) as c:
                pe.wait_ge(*at("hn_ok", c + 1))
                pe.wait_ge(*at("yT_ok", c))
                for k in range(KD):
                    last = nc.tensor.transpose(PS[0][:, k * P:(k + 1) * P], T[4][:, k * P:(k + 1) * P], ident[:])
                last.then_inc(ev("hT_ps"), 1)
            pe.wait_ge(*at("xl_r", NT))
            tiles(G5)
            pe.wait_ge(*at("yssq_ok", KD + 1))
            stat(PS[2], T[4], "stat2_ps")
            pe.wait_ge(*at("xssq_ok", KD))
            stat(PS[3], T[5], "stat3_ps")
            pe.wait_ge(*at("xl_G6", KD))
            tiles(G6)
            for g, (k0, kc) in enumerate(down):
                pe.wait_ge(*at("xl_G7", k0 + kc))
                tiles(G7[g], kc=kc)
            pe.wait_ge(*at("zssq_ok", KD + 1))
            stat(PS[2], T[0], "stat4_ps")
            pe.wait_ge(*at("fin_ok", KD))
            for t in range(NT):
                if t >= 2:
                    pe.wait_ge(*at("fin_sb", t - 1))
                for k in range(KD):
                    last = nc.tensor.transpose(PS[t % 2][:, k * P:(k + 1) * P], B1[:, k, t * P:(t + 1) * P], ident[:])
                last.then_inc(ev("out_ps"), 1)

        @block.vector
        def _(dve):
            step = Chain(dve, "dve_step")
            V = nc.vector

            def log1p(e, s, z, p):
                step.link(V.tensor_scalar(s, e, 2.0, None, ALU.add))
                step.link(V.reciprocal(s, s))
                step.link(V.tensor_tensor(s, e, s, ALU.mult))
                step.link(V.tensor_tensor(z, s, s, ALU.mult))
                n = LOG1P_TERMS
                step.link(V.tensor_scalar(p, z, 1.0 / (2 * n + 1), 1.0 / (2 * n - 1), ALU.mult, ALU.add))
                for t in range(n - 2, -1, -1):
                    step.link(V.tensor_tensor(p, p, z, ALU.mult))
                    step.link(V.tensor_scalar(p, p, 1.0 / (2 * t + 1), None, ALU.add))
                step.link(V.scalar_tensor_tensor(out=p, in0=s, scalar=2.0, in1=p, op0=ALU.mult, op1=ALU.mult))

            V.memset(SCR[:, 0:NST * P], 0.0).then_inc(ev("stage_zero"), 1)
            dve.wait_ge(*at("stage_ps", 1))
            V.tensor_copy(PV[:], PS[2][:, 0:NST * P]).then_inc(ev("pv"), 1)

            def token(i, s):
                dve.wait_ge(*at(f"rms{s}", i + 1))
                step.link(V.reciprocal(small[:, 2, s:s + 1], small[:, 1, s:s + 1]))
                V.tensor_scalar(T[3 + s], T[1 + s], small[:, 2, s:s + 1], None, ALU.mult).then_inc(ev(f"xn_ok{s}"), 1)
                dve.wait_ge(*at(f"xnT_pe{s}", i + 1))

            with dve.Fori(0, NT // 2) as i:
                step.loop(i, 2)
                for s in range(2):
                    token(i, s)
                    V.tensor_copy(B1[:, :, ds(2 * P * i + s * P, P)],
                                  PS[2 + s][:].rearrange("p (k t) -> p k t", k=KD)).then_inc(ev(f"xnT_sb{s}"), 1)
            step.done(NT // 2)
            for s in range(NC):
                token(NT // 2, s)
                dve.wait_ge(*at(f"xT_out{s}", 16 * NT // 2))
                V.tensor_copy(T[5 + s], PS[2 + s][:]).then_inc(ev(f"ctxT_sb{s}"), 1)

            dve.wait_ge(*at("pv", 1))
            dve.wait_ge(*at("lam_e", 1))
            log1p(lam4[:, 1, :], lam4[:, 0, :], lam4[:, 2, :], lam4[:, 3, :])
            step.link(V.tensor_scalar(lam4[:, 0, :], pvec("lam", KD), -1.0, 0.0, ALU.mult, ALU.max))
            step.link(V.tensor_tensor(lam4[:, 0, :], lam4[:, 0, :], lam4[:, 3, :], ALU.add))
            step.sig(V.tensor_scalar(PJ[:, :, TAPS + SHORT + 4], lam4[:, 0, :], -LRU_C, None, ALU.mult))
            step.sig(V.tensor_scalar(PJ[:, :, TAPS + SHORT + 5], lam4[:, 0, :], LRU_C, None, ALU.mult))
            for t0 in range(0, TAPS, P // KD):
                n = min(P // KD, TAPS - t0)
                step.sig(V.tensor_copy(PJ[:, :, t0:t0 + n], pvec(f"dw_w{t0}", n * KD).rearrange("p (t k) -> p k t", k=KD)))
            step.sig(V.tensor_copy(PJ[:, :, TAPS], pvec("dw_b", KD)))
            step.sig(V.tensor_copy(PJ[:, :, TAPS + 1:TAPS + 1 + SHORT], pvec("sc_w", SHORT * KD).rearrange("p (t k) -> p k t", k=KD)))
            for n, name in enumerate(("sc_b", "br", "bi")):
                step.sig(V.tensor_copy(PJ[:, :, TAPS + SHORT + 1 + n], pvec(name, KD)))
            step.wait()
            dve.sem_inc(ev("pj"), 1)
            dve.wait_ge(*at("mod_used", 6))
            step.link(V.tensor_tensor(MOD[:], PS[3][:, 0:6 * KD].rearrange("p (c t) -> p c t", t=2)[:, :, 0], pvec("mod_b", 3 * KD), ALU.add))
            step.sig(V.scalar_tensor_tensor(out=SC[:, 0, :], in0=MOD[:, KD:2 * KD], scalar=1.0, in1=pvec("norm_g", KD), op0=ALU.add, op1=ALU.mult))
            step.sig(V.tensor_scalar(SC[:, 1, :], MOD[:, 2 * KD:3 * KD], 1.0, None, ALU.add))
            step.wait()
            dve.sem_inc(ev("mod_ok"), 1)
            for s in range(2):
                dve.wait_ge(*at(f"xnT_pe{s}", NT // 2 + 1))
            for k in range(KD):
                tmp = T[3 + k % 2]
                step.link(V.tensor_scalar(tmp, B1[:, k, :], SC[:, 0, k:k + 1], MOD[:, k:k + 1], ALU.mult, ALU.add))
                dve.wait_ge(*at("xh_L1", k + 1))
                ins = V.tensor_tensor(XL[:, k, :], tmp, XH[:, k, :].bitcast(F32), ALU.subtract)
                ins.then_inc(ev("xl_L1"), 1)
                dve.wait_ge(*at("xl_L1", k + 1))

            def short_conv(j):
                step.link(V.tensor_copy(PJd[:, TAPS:NJ], PJ[:, ds(j, 1), TAPS:NJ].rearrange("p a n -> p (a n)")))
                dve.wait_ge(*at("lx_sb", j + 1))
                dve.wait_ge(*at("pads_zero", 2))
                dve.wait_ge(*at("bx", j))
                step.link(V.tensor_scalar(xs_t, lxpad[:, 0:SEQ], PJd[:, TAPS + 1:TAPS + 2], PJd[:, TAPS + SHORT + 1:TAPS + SHORT + 2],
                                          ALU.mult, ALU.add))
                for t in range(1, SHORT):
                    ins = V.scalar_tensor_tensor(out=xs_t, in0=lxpad[:, t:t + SEQ], scalar=PJd[:, TAPS + 1 + t:TAPS + 2 + t],
                                                 in1=xs_t, op0=ALU.mult, op1=ALU.add)
                    if t < SHORT - 1:
                        step.link(ins)
                ins.then_inc(ev("xs_ok"), 1)

            def conv(j):
                step.link(V.tensor_copy(PJc[:], PJ[:, ds(j, 1), :].rearrange("p a n -> p (a n)")))
                dve.wait_ge(*at("vpad_ok", j + 1))
                o = B1[:, ds(j, 1), :].rearrange("p a t -> p (a t)")
                step.link(V.tensor_scalar(o, vpad[:, 0:SEQ], PJc[:, 0:1], PJc[:, TAPS:TAPS + 1], ALU.mult, ALU.add))
                for t in range(1, TAPS):
                    ins = V.scalar_tensor_tensor(out=o, in0=vpad[:, t:t + SEQ], scalar=PJc[:, t:t + 1], in1=o, op0=ALU.mult, op1=ALU.add)
                    if t < TAPS - 1:
                        step.link(ins)
                ins.then_inc(ev("conv_ok"), 1)

            def lru(j):
                dve.wait_ge(*at("bx", j + 1))
                dve.wait_ge(*at("a_ok", j + 1))
                step.link(V.tensor_tensor_scan(out=r_t, data0=a_t, data1=i_t, initial=0.0, op0=ALU.mult, op1=ALU.add))
                dve.wait_ge(*at("ls_sb", j + 1))
                V.tensor_tensor(ls_t, r_t, ls_t, ALU.mult).then_inc(ev("lru_y"), 1)
                dve.wait_ge(*at("ada_used", 2 * j + 2))
                for half in range(2):
                    ins = V.tensor_copy(ADA[:, ds(6 * j + 3 * half, 3), :], PS[3][:, 512 * half:512 * half + 6].rearrange("p (c t) -> p c t", t=2))
                ins.then_inc(ev("ada_sb"), 1)

            short_conv(0)
            lru(0)
            with dve.Fori(1, KD) as j:
                n = 1 + (SHORT - 1) + 1 + (TAPS - 1) + 1
                step.loop(j, n)
                step.base -= n
                short_conv(j)
                conv(j - 1)
                lru(j)
            step.done(KD)

            dve.wait_ge(*at("ada_sb", KD))
            step.sig(V.tensor_tensor(ADA[:, :, 0], ADA[:, :, 0], pvec("ada_b_2", 6 * KD), ALU.add))
            step.sig(V.tensor_tensor(ADA[:, 0:2 * KD, 1], ADA[:, 0:2 * KD, 1], pvec("ada_b_2", 2 * KD), ALU.add))
            step.wait()
            stt = V.scalar_tensor_tensor
            step.link(stt(out=SC[:, 4, :], in0=ADA[:, KD:2 * KD, 1], scalar=1.0, in1=pvec("pre_mix_g_2", KD), op0=ALU.add, op1=ALU.mult))
            step.link(stt(out=SC[:, 5, :], in0=ADA[:, KD:2 * KD, 0], scalar=1.0, in1=pvec("pre_mix_g_2", KD), op0=ALU.add, op1=ALU.mult))
            step.link(V.tensor_tensor(SC[:, 5, :], SC[:, 5, :], pvec("final_g", KD), ALU.mult))
            step.link(V.tensor_tensor(SC[:, 6, :], ADA[:, 2 * KD:3 * KD, 0], pvec("post_mix_g_2", KD), ALU.mult))
            step.link(stt(out=SC[:, 7, :], in0=ADA[:, 4 * KD:5 * KD, 0], scalar=1.0, in1=pvec("pre_ffn_g_2", KD), op0=ALU.add, op1=ALU.mult))
            step.link(V.tensor_tensor(SC[:, 8, :], ADA[:, 5 * KD:6 * KD, 0], pvec("post_ffn_g_2", KD), ALU.mult))
            dve.sem_inc(ev("sc_ok"), 1)

            conv(KD - 1)
            dve.wait_ge(*at("mean_ps", 1))
            dve.wait_ge(*at("msum_ok", KD))
            for k in range(KD):
                step.link(V.tensor_tensor(B1[:, k, :], B1[:, k, :], PS[2][:], ALU.subtract))
                if k == 0:
                    step.link(V.tensor_tensor(T[5], B1[:, 0, :], B1[:, 0, :], ALU.mult))
                else:
                    step.link(V.tensor_tensor(T[4], B1[:, k, :], B1[:, k, :], ALU.mult))
                    step.link(V.tensor_tensor(T[5], T[5], T[4], ALU.add))
            dve.sem_inc(ev("var_ok"), 1)
            dve.wait_ge(*at("ln_sd", 1))
            step.link(V.reciprocal(T[6], T[3]))

            def ln_low(k):
                dve.wait_ge(*at("xh_G2", k + 1))
                V.tensor_tensor(XL[:, k, :], T[2 + k % 2], XH[:, k, :].bitcast(F32), ALU.subtract).then_inc(ev("xl_G2"), 1)

            for k in range(KD):
                V.tensor_tensor(B1[:, k, :], B1[:, k, :], T[6], ALU.mult).then_inc(ev("ln_t"), 1)
                if k >= 1:
                    ln_low(k - 1)
            ln_low(KD - 1)

            def tiles(g, evac, n=None):
                with dve.Fori(0, g.n // 2) as i:
                    if n:
                        step.loop(i, 2 * n)
                    for s in range(2):
                        b = (g.T + s) % 2
                        dve.wait_ge(unit_used, 2 * i + (g.U + s + 3))
                        evac(2 * i + s, s, i, PS[b], taken[b])
                if n:
                    step.done(g.n // 2)

            def g2(t, s, i, ps, tk):
                dve.wait_ge(*at(f"cs_in{s}", 16 * i + 16))
                stt(out=B1[:, ds(t, 1), :].rearrange("p a t -> p (a t)"), in0=ps[:], scalar=pcol("pw2_b", t), in1=T[s],
                    op0=ALU.add, op1=ALU.mult).then_inc(ev("yconv_ok"), 1)
                dve.wait_ge(*at("yconv_ok", t + 1))
                dve.sem_inc(tk, 1)
                dve.sem_inc(ev(f"cs_free{s}"), 1)

            dve.wait_ge(*at("xl_G2", KD))
            tiles(G2, g2)
            for k in range(KD):
                dve.wait_ge(*at("xh_G3", k + 1))
                V.tensor_tensor(XL[:, k, :], B1[:, k, :], XH[:, k, :].bitcast(F32), ALU.subtract).then_inc(ev("xl_G3"), 1)

            def g3(t, s, i, ps, tk):
                row = B2[:, ds(t, 1), :].rearrange("p a t -> p (a t)")
                step.link(V.tensor_tensor(T[2], ps[:], row, ALU.add))
                dve.sem_inc(tk, 1)
                dve.wait_ge(*at(f"res_in{s}", 16 * i + 16))
                stt(out=row, in0=T[2], scalar=SC[:, 1, :][:, ds(t, 1)], in1=T[s], op0=ALU.mult, op1=ALU.add).then_inc(ev("x1_ok"), 1)
                dve.wait_ge(*at("x1_ok", t + 1))
                dve.sem_inc(ev(f"res_free{s}"), 1)

            tiles(G3, g3, 1)

            dve.wait_ge(*at("ctx_in", 16))
            cn = B1[:, 2:4, :].rearrange("p a (b t) -> p (a b) t", t=CTX)
            for k in range(KD):
                tmp = T[2][:, 0:CTX]
                step.link(V.tensor_scalar(tmp, cn[:, k, :], SC[:, 4, k:k + 1], ADA[:, k, 1:2], ALU.mult, ALU.add))
                dve.wait_ge(*at("xh_c", k + 1))
                V.tensor_tensor(XCL[:, k, :], tmp, XCH[:, k, :].bitcast(F32), ALU.subtract).then_inc(ev("xl_c"), 1)
                dve.wait_ge(*at("xl_c", k + 1))
            dve.wait_ge(*at("n1_sd1", 1))
            step.link(V.reciprocal(T[0], T[3]))
            step.link(V.tensor_tensor(T[1], PS[3][:], T[0], ALU.mult))
            step.link(V.tensor_tensor(T[1], T[1], T[0], ALU.mult))
            dve.sem_inc(ev("n1_ms"), 1)
            dve.wait_ge(*at("n1_sd2", 1))
            step.link(V.reciprocal(T[2], T[3]))
            step.link(V.tensor_tensor(T[1], T[2], T[0], ALU.mult))
            dve.wait_ge(unit_used, G3.end)
            for k in range(KD):
                if k >= 2:
                    dve.wait_ge(*at(f"x2_out{k % 2}", 16 * (k // 2)))
                stt(out=T[2 + k % 2], in0=B2[:, k, :], scalar=pcol("final_g", k), in1=T[0], op0=ALU.mult, op1=ALU.mult).then_inc(ev("x2_sb"), 1)
                t, shift = T[4 + k % 2], ADA[:, k, 0:1]
                step.link(stt(out=t, in0=B2[:, k, :], scalar=SC[:, 5, k:k + 1], in1=T[1], op0=ALU.mult, op1=ALU.mult))
                step.link(V.tensor_scalar(XH[:, k, :], t, shift, None, ALU.add))
                stt(out=XL[:, k, :], in0=t, scalar=shift, in1=XH[:, k, :].bitcast(F32), op0=ALU.add, op1=ALU.subtract).then_inc(ev("xl_Gx"), 1)
                dve.wait_ge(*at("xl_Gx", k + 1))
            dve.sem_inc(ev("x1_used"), 1)

            dve.wait_ge(*at("f_in", 32))
            dve.wait_ge(*at("f_e", 1))
            log1p(LS[:, 1, :], LS[:, 2, :], LS[:, 3, :], LS[:, 4, :])
            stt(out=LS[:, 0, :], in0=LS[:, 0, :], scalar=0.0, in1=LS[:, 4, :], op0=ALU.min, op1=ALU.subtract).then_inc(ev("lf_sb"), 1)

            def reverse(dst, src):
                for a, b in ((0, CTX), (CTX, ALL)):
                    step.link(V.tensor_copy(dst[32:32 + HEADS, a:b], src[32:32 + HEADS, a:b][:, ::-1]))

            step.link(V.memset(RZ, 1.0))
            step.link(V.memset(RZ.rearrange("p (c t) -> p c t", t=P)[:, :, 0:1], 0.0))
            dve.wait_ge(*at("rows_in", 64))
            reverse(RI, UN[0])
            reverse(RF, UN[1])
            step.link(V.tensor_tensor_scan(out=RB, data0=RZ, data1=RF, initial=0.0, op0=ALU.mult, op1=ALU.add))
            step.link(V.tensor_tensor(RI, RI, RB, ALU.subtract))
            step.link(V.memset(RZ, 0.0))

            def by_chunk(r):
                return r.rearrange("p (c t) -> p c t", t=P)

            step.link(V.tensor_copy(by_chunk(RZ)[:, 1:NCH, 0], by_chunk(RB)[:, 0:NCH - 1, P - 1]))
            step.link(V.tensor_tensor_scan(out=RM, data0=RZ, data1=RI, initial=0.0, op0=ALU.add, op1=ALU.max))
            step.link(V.memset(mprev[:], 0.0))
            step.link(V.tensor_tensor(mprev[:, 1:NCH], by_chunk(RB)[:, 0:NCH - 1, P - 1], by_chunk(RM)[:, 0:NCH - 1, P - 1], ALU.add))
            step.link(V.scalar_tensor_tensor(out=RF, in0=RB, scalar=-1.0, in1=RM, op0=ALU.mult, op1=ALU.subtract))
            step.link(V.tensor_tensor(by_chunk(RO), by_chunk(RI), by_chunk(RM)[:, :, P - 1:P].to_broadcast([36, NCH, P]), ALU.subtract))
            step.link(V.tensor_tensor(by_chunk(RZ), bc(mprev[:], P), by_chunk(RM), ALU.subtract))
            for q in range(5):
                reverse(UN[q], RQ[q])
            dve.sem_inc(ev("rows_sb"), 1)

            dve.wait_ge(*at("rows_out", 16 * 10))
            for s in range(2):
                dve.wait_ge(*at(f"proj_out{s}", 16 * (1 + (Gc.n + Gx.n) // 2)))
            for d in range(2):
                step.link(V.memset(M[d]["C"], 0.0))
                step.link(V.memset(M[d]["va"][:, :, DV:VW], 1.0))
            dve.sem_inc(ev("rec_zero"), 1)
            NUM = [PS[2][:, 512:512 + VW], PS[3][:, 0:VW]]
            DC = [PS[3][:, 512:512 + VW], PS[0][:, 512:512 + VW]]

            def chunk(q, n, d, j=None):
                m = M[d]
                a, en, eg, rec = cols[d][:, 0:4], cols[d][:, 12:16], cols[d][:, 16:20], cols[d][:, 20:24]
                dve.wait_ge(*at("t_ps", q + 1))
                V.tensor_copy(cols[d][:, 0:12], PS[0][:, 512:512 + 3 * HEADS]).then_inc(ev("cols_sb"), 1)
                if j is not None:
                    x = 2 * j + d
                    dve.wait_ge(*at(f"chunk_in{d}", 112 * n + 112))
                    dve.wait_ge(*at("cols_sb", q + 1))
                    step.link(V.tensor_tensor(m["M"], m["M"], bc(a, P), ALU.subtract))
                    stt(out=m["M"], in0=m["M"], scalar=0.0, in1=mask[d][:].rearrange("p (o t) -> p o t", o=1).to_broadcast([P, HEADS, P]), op0=ALU.max, op1=ALU.add).then_inc(ev("d_ok"), 1)
                dve.wait_ge(*at("eg_ok", q + 1))
                V.tensor_tensor(m["kw"], PS[0][:, 0:HQ].rearrange("p (h n) -> p h n", h=HEADS), bc(eg, P), ALU.mult).then_inc(ev("kw_ok"), 1)
                if j is not None:
                    step.link(V.tensor_scalar(en, en, float(DK) ** 0.5, None, ALU.mult))
                    dve.wait_ge(*at("s_ps", x + 1))
                    dve.wait_ge(*at("e_ok", x + 1))
                    V.tensor_tensor(m["p"], PS[2][:, 0:HQ].rearrange("p (h n) -> p h n", h=HEADS), m["M"], ALU.mult).then_inc(ev("p_ok"), 1)
                last = P - 1 if d == 0 else 0
                dve.wait_ge(*at("w_ok", q + 1))
                for h in range(HEADS):
                    if j is not None:
                        dve.wait_ge(*at("num_ps", HEADS * x + h + 1))
                        den, r = NUM[h % 2][:, DV:VW], rec[:, h:h + 1]
                        step.link(V.tensor_scalar(r, den, -1.0, en[:, h:h + 1], ALU.mult, ALU.max))
                        step.link(V.tensor_tensor(r, den, r, ALU.max))
                        V.reciprocal(rec[:, h:h + 1], rec[:, h:h + 1]).then_inc(ev("rec_ok"), 1)
                    dve.wait_ge(*at("dc_ps", HEADS * q + h + 1))
                    dve.wait_ge(*at("c_ok", HEADS * q + h))
                    stt(out=m["C"][:, h, :], in0=m["C"][:, h, :], scalar=m["U"][:, h, last:last + 1], in1=DC[h % 2],
                        op0=ALU.mult, op1=ALU.add).then_inc(ev("c_ok"), 1)
                dve.wait_ge(*at("c_ok", HEADS * q + HEADS))
                dve.sem_inc(ev(f"chunk_free{d}"), 1)

            for n in range(NC):
                for d in range(2):
                    chunk(2 * n + d, n, d)
            with dve.Fori(0, NT) as j:
                step.loop(j, 2 * (2 + 2 * HEADS))
                for d in range(2):
                    chunk(2 * j + (2 * NC + d), j + NC, d, j)
            step.done(NT)

            with dve.Fori(0, NT) as c:
                step.loop(c, 2)
                dve.wait_ge(*at("read_in", 48 * c + 48))
                V.tensor_tensor(T[0], T[0], T[1], ALU.add).then_inc(ev("hs_ok"), 1)
                dve.wait_ge(*at("hrms", c + 1))
                step.link(V.reciprocal(small[:, 5, 0:HEADS], small[:, 4, 0:HEADS]))
                dve.wait_ge(*at("hs_ok", c + 1))
                V.tensor_tensor(T[4].rearrange("p (h e) -> p h e", h=HEADS), T[0].rearrange("p (h e) -> p h e", h=HEADS),
                                bc(small[:, 5, 0:HEADS], DV), ALU.mult).then_inc(ev("hn_ok"), 1)
                dve.wait_ge(*at("hT_ps", c + 1))
                dve.wait_ge(*at("gate_ok", c + 1))
                V.tensor_tensor(T[5], PS[0][:], T[2], ALU.mult).then_inc(ev("yT_ok"), 1)
                dve.wait_ge(*at("xh_r", c + 1))
                step.link(V.tensor_tensor(XL[:, :, ds(P * c, P)], T[5].rearrange("p (k t) -> p k t", k=KD),
                                          XH[:, :, ds(P * c, P)].bitcast(F32), ALU.subtract))
                dve.sem_inc(ev("xl_r"), 1)
                dve.sem_inc(ev("read_free"), 1)
            step.done(NT)

            dve.wait_ge(*at("n2_sd", 1))
            step.link(V.reciprocal(T[6], T[6]))
            dve.wait_ge(*at("xssq_zero", 1))
            for k in range(KD):
                dve.wait_ge(*at("y_sb", KD))
                step.link(V.tensor_tensor(B1[:, k, :], B1[:, k, :], T[6], ALU.mult))
                dve.wait_ge(*at(f"x2_in{k % 2}", 16 * (k // 2 + 1)))
                stt(out=B2[:, k, :], in0=B1[:, k, :], scalar=SC[:, 6, k:k + 1], in1=T[k % 2], op0=ALU.mult, op1=ALU.add).then_inc(ev("x3_sb"), 1)
                dve.wait_ge(*at("xsq_ok", k + 1))
                V.tensor_tensor(T[5], T[5], T[2 + k % 2], ALU.add).then_inc(ev("xssq_ok"), 1)
                dve.wait_ge(*at("xssq_ok", k + 1))
            dve.sem_inc(ev("n2_done"), 1)
            dve.wait_ge(*at("n3_sd", 1))
            step.link(V.reciprocal(T[6], T[6]))

            def h2_low(k):
                dve.wait_ge(*at("xh_G6", k + 1))
                stt(out=XL[:, k, :], in0=T[2 + k % 2], scalar=ADA[:, 3 * KD + k, 0:1], in1=XH[:, k, :].bitcast(F32),
                    op0=ALU.add, op1=ALU.subtract).then_inc(ev("xl_G6"), 1)

            for k in range(KD):
                if k >= 2:
                    dve.wait_ge(*at("xl_G6", k - 1))
                stt(out=T[2 + k % 2], in0=B2[:, k, :], scalar=SC[:, 7, k:k + 1], in1=T[6], op0=ALU.mult, op1=ALU.mult).then_inc(ev("h2_t"), 1)
                dve.wait_ge(*at("h2_t", k + 1))
                if k >= 1:
                    h2_low(k - 1)
            h2_low(KD - 1)
            dve.wait_ge(*at("xl_G6", KD))

            def grid(t):
                return t.rearrange("p (r w) -> p r w", w=GRID)

            with dve.Fori(0, KF) as j:
                step.loop(j, 1)
                dve.wait_ge(*at("g_sb", 2 * j + 2))
                step.link(stt(out=grid(T[1])[:, :, 1:GRID], in0=grid(T[0])[:, :, 0:GRID - 1], scalar=pcol("ffn_conv_w", j),
                              in1=grid(T[1])[:, :, 1:GRID], op0=ALU.mult, op1=ALU.add))
                stt(out=grid(T[1])[:, :, 0:GRID - 1], in0=grid(T[0])[:, :, 1:GRID], scalar=pcol("ffn_conv_w", j + 2 * KF),
                    in1=grid(T[1])[:, :, 0:GRID - 1], op0=ALU.mult, op1=ALU.add).then_inc(ev("ffn_conv"), 1)
                b = (G6.T + 1) % 2
                dve.wait_ge(unit_used, 2 * j + (G6.U + 4))
                dve.wait_ge(*at("ffn_silu", j + 1))
                dve.wait_ge(*at("act_out", 16 * j))
                V.tensor_tensor(T[2], PS[b][:], T[3], ALU.mult).then_inc(ev("act_sb"), 1)
                dve.wait_ge(*at("act_sb", j + 1))
                dve.sem_inc(taken[b], 1)
            step.done(KF)

            n = 0
            for g, (k0, kc) in enumerate(down):
                for k in range(kc):
                    dve.wait_ge(*at("xh_G7", n + 1))
                    V.tensor_tensor(XL[:, k, :], T[4 + n % 2], XH[:, k, :].bitcast(F32), ALU.subtract).then_inc(ev("xl_G7"), 1)
                    n += 1

                def down_evac(t, s, i, ps, tk, g=g):
                    row = B1[:, ds(t, 1), :].rearrange("p a t -> p (a t)")
                    ins = V.tensor_copy(row, ps[:]) if g == 0 else V.tensor_tensor(row, ps[:], row, ALU.add)
                    ins.then_inc(ev("z_ok"), 1)
                    dve.wait_ge(*at("z_ok", t + (g * KD + 1)))
                    dve.sem_inc(tk, 1)

                tiles(G7[g], down_evac)
            dve.wait_ge(*at("n4_sd", 1))
            step.link(V.reciprocal(T[6], T[6]))
            for k in range(KD):
                step.link(V.tensor_tensor(B1[:, k, :], B1[:, k, :], T[6], ALU.mult))
                stt(out=B1[:, k, :], in0=B1[:, k, :], scalar=SC[:, 8, k:k + 1], in1=B2[:, k, :], op0=ALU.mult, op1=ALU.add).then_inc(ev("fin_ok"), 1)


_INS = ["x", "c", "norm_g", "mod_w", "mod_b", "w_in", "dw_w", "dw_b", "cln_g", "cln_b", "pw2_w", "pw2_b", "sc_w", "sc_b",
        "wr", "br", "wi", "bi", "lam", "w_out", "final_g", "c_2", "ctx_2", "c_ctx_2", "ada_w_2", "ada_b_2", "pre_mix_g_2",
        "post_mix_g_2", "pre_ffn_g_2", "post_ffn_g_2", "ffn_up_w_2", "ffn_conv_w_2", "ffn_conv_b_2", "ffn_down_w_2",
        "m_in_w_2", "m_in_b_2", "m_norm_g_2", "m_out_w_2"]


def kernel(**inputs):
    import numpy as _np
    import concourse.bacc as _bacc
    from concourse import mybir as _mybir
    from concourse.bass_utils import run_bass_kernel_spmd as _run

    nc = _bacc.Bacc("TRN2", target_bir_lowering=False, num_devices=1)
    arrays, args = {}, {}
    for name in _INS:
        a = _np.ascontiguousarray(inputs[name])
        arrays[f"in_{name}"] = a
        args[name] = nc.dram_tensor(f"in_{name}", a.shape, _mybir.dt.from_np(a.dtype), kind="ExternalInput").ap()
    shape = inputs["x"].shape
    out = nc.dram_tensor("out_dram", shape, _mybir.dt.float32, kind="ExternalOutput").ap()
    block_pair_kernel(nc, args, out)
    r = _run(nc, [arrays], core_ids=[0])
    return r.results[0]["out_dram"]
```

```python
from contextlib import ExitStack

import concourse.bass as bass
from concourse import mybir

F32 = mybir.dt.float32
F32R = mybir.dt.float32r
ALU = mybir.AluOpType
ACT = mybir.ActivationFunctionType
ds = bass.ds

P = 128
EPS = 1e-6
BIG = 1e30
GRID = 64


def block_pair_kernel(nc, A, out):
    x, ctx = A["x"][0], A["ctx_2"][0]
    SEQ, D = x.shape
    CTX = ctx.shape[0]
    KD = D // P
    NT = SEQ // P
    NC = CTX // P
    TAPS = A["dw_w"].shape[1]
    SHORT = A["sc_w"].shape[1]
    FFN = A["ffn_down_w_2"].shape[1]
    KF = FFN // P
    HEADS, DK, DV = 4, P, D // 4
    ALL = CTX + SEQ
    NCH = ALL // P
    HQ = HEADS * DK
    MP = A["m_in_w_2"].shape[2]
    GATE_ROW = MP - 4 * HEADS
    LRU_C = 8.0
    LOG1P_TERMS = 9
    VW = DV + 1

    mod_w, w_in, pw2_w, w_out = A["mod_w"][0], A["w_in"][0], A["pw2_w"][0], A["w_out"][0]
    ada_w, m_in_w, m_out_w = A["ada_w_2"][0], A["m_in_w_2"][0], A["m_out_w_2"][0]
    up_w, down_w = A["ffn_up_w_2"][0], A["ffn_down_w_2"][0]

    def dram(name, shape):
        return nc.dram_tensor(name, shape, F32).ap()

    xT_d = dram("xT_d", [D, SEQ])
    ctxT_d = dram("ctxT_d", [D, CTX])
    lru_d = dram("lru_d", [D, SEQ])
    cs_d = dram("cs_d", [D, SEQ])
    x2_d = dram("x2_d", [D, SEQ])
    proj_d = dram("proj_d", [MP, ALL])
    lf_d = dram("lf_d", [2 * HEADS, ALL])
    rows_d = dram("rows_d", [5 * 2 * HEADS, ALL])
    h_d = dram("h_d", [2, SEQ, D])
    act_d = dram("act_d", [FFN, SEQ])

    stage_rows, col, fill = [], {}, [0]

    def place(name, src, n):
        if fill[0] % P + n > P:
            fill[0] += P - fill[0] % P
        col[name] = fill[0]
        stage_rows.append((fill[0] // P, fill[0] % P, n, src))
        fill[0] += n

    def vec(a):
        return a.rearrange("(k p) -> k p", p=P)

    for name in ("norm_g", "mod_b", "dw_b", "cln_g", "cln_b", "pw2_b", "sc_b", "br", "bi", "lam"):
        place(name, vec(A[name][0]), A[name].shape[1] // P)
    place("c", vec(A["c"][0]), KD)
    place("sc_w", A["sc_w"][0].rearrange("t (k p) -> (t k) p", p=P), SHORT * KD)
    for name in ("pre_mix_g_2", "post_mix_g_2", "pre_ffn_g_2", "post_ffn_g_2", "m_norm_g_2", "ffn_conv_b_2", "ada_b_2"):
        place(name, vec(A[name][0]), A[name].shape[1] // P)
    place("c_2", vec(A["c_2"][0]), KD)
    place("final_g", vec(A["final_g"]), KD)
    dw = A["dw_w"][0].rearrange("t (k p) -> (t k) p", p=P)
    for t0 in range(0, TAPS, P // KD):
        n = min(P // KD, TAPS - t0) * KD
        place(f"dw_w{t0}", dw[t0 * KD:t0 * KD + n, :], n)
    place("ffn_conv_w", A["ffn_conv_w_2"][0].rearrange("t (k p) -> (t k) p", p=P), 3 * KF)
    place("m_in_b", vec(A["m_in_b_2"][0][0:GATE_ROW]), GATE_ROW // P)
    place("gate_b", vec(A["m_in_b_2"][0][MP - P:MP]), 1)
    place("c_ctx", vec(A["c_ctx_2"]), KD)
    NST = (fill[0] + P - 1) // P

    with ExitStack() as ctxs:
        def sb(name, shape, dt=F32):
            return ctxs.enter_context(nc.sbuf_tensor(name, shape, dt))

        def sem(name):
            return ctxs.enter_context(nc.semaphore(name))

        sems = {}

        shared = {}

        def share(total, *events):
            at_count = 0
            for name, n in events:
                shared[name] = (total, at_count)
                at_count += n

        share("x_high", ("xh_L1", KD), ("xh_G1", KD), ("xh_G2", KD), ("xh_G3", KD), ("xh_c", KD), ("xh_Gx", KD), ("xh_r", NT), ("xh_G6", KD), ("xh_G7", KF))
        share("x_low", ("xl_L1", KD), ("xl_G1", KD), ("xl_G2", KD), ("xl_G3", KD), ("xl_c", KD), ("xl_Gx", KD), ("xl_r", NT), ("xl_G6", KD), ("xl_G7", KF))
        share("dve_stage", *((n, 1) for n in ("stage_zero", "pv", "pj", "mod_ok", "sc_ok", "var_ok", "n1_ms", "lf_sb", "rows_sb", "rec_zero", "n2_done")))
        share("pe_stage", *((n, 1) for n in ("stage_ps", "mean_ps", "var_ps", "stat1_ps", "stat1_ps2", "stat2_ps", "stat3_ps", "stat4_ps")))
        share("act_stage", *((n, 1) for n in ("lam_e", "ln_sd", "n1_sd1", "n1_sd2", "f_e", "n2_sd", "n3_sd", "n4_sd")))
        for a, b, n in (("xsh", "w_ok", KD), ("xsl", "va_ok", KD), ("i_ok", "kw_ok", KD), ("r_ok", "t_ps", KD), ("th_ok", "e_ok", KD),
                        ("m2", "q2_ok", KD), ("mult_ok", "d_ok", KD), ("lx_sb", "s_ps", KD), ("ls_sb", "den_ps", KD), ("a_ok", "num_ps", KD),
                        ("rms0", "gate_ok", NT // 2 + 1), ("rms1", "hs_ok", NT // 2 + 1)):
            share(f"{a}_then_{b}", (a, n), (b, 0))
        share("pool_stage", ("msum_zero", 1), ("pads_zero", 2), ("xssq_zero", 1))

        def ev(name):
            name = shared.get(name, (name, 0))[0]
            if name not in sems:
                sems[name] = sem(name)
            return sems[name]

        BEGIN_AT_ONE = ("ada_used", "cs_free0", "cs_free1", "res_free0", "res_free1", "msum_ok", "xs_ok",
                        "ri_ps", "lru_out", "lru_y", "vpad_ok", "cs_out", "proj_out0", "proj_out1", "h_out0", "h_out1",
                        "ffn_conv", "ffn_silu", "act_sb", "xT_sb0", "xT_sb1", "xnT_sb0", "xnT_sb1", "xnT_pe0", "xnT_pe1",
                        "xT_out0", "xT_out1", "cs_sb", "ada_sb", "p_ok", "num_free", "yT_free0", "yT_free1", "act_out", "bx", "h_sb0", "h_sb1")

        def at(name, n):
            return ev(name), n + (1 if name in BEGIN_AT_ONE else shared.get(name, (name, 0))[1])

        XH = sb("XH", [P, KD, SEQ], F32R)
        XL = sb("XL", [P, KD, SEQ], F32R)
        XCH = sb("XCH", [P, KD, CTX], F32R)
        XCL = sb("XCL", [P, KD, CTX], F32R)
        raw = [sb(f"raw{s}", [P, KD, P]) for s in range(2)]
        wh = [sb(f"wh{s}", [P, KD, P], F32R) for s in range(2)]
        wl = [sb(f"wl{s}", [P, KD, P], F32R) for s in range(2)]
        B1 = sb("B1", [P, KD, SEQ])
        B2 = sb("B2", [P, KD, SEQ])
        VP = SEQ + 32
        LP = SEQ + 4
        SCR = sb("SCR", [P, VP + LP + 5 * SEQ])
        PV = sb("PV", [P, NST * P])
        NJ = TAPS + SHORT + 6
        PJ = sb("PJ", [P, KD, NJ])
        ident = sb("ident", [P, P])
        avg = sb("avg", [P, P])
        mask = [sb(f"mask{d}", [P, P]) for d in range(2)]
        CA = sb("CA", [P, KD, 4])
        MOD = sb("MOD", [P, 3 * KD])
        ADA = sb("ADA", [P, 6 * KD, 2])
        SC = sb("SC", [P, 9, KD])
        eps = sb("eps", [P, 1])
        small = sb("small", [P, 6, 16])
        mprev = sb("mprev", [36, NCH])
        PJc = sb("PJc", [P, NJ])
        PJd = sb("PJd", [P, NJ])
        PJa = sb("PJa", [P, NJ])
        lam4 = sb("lam4", [P, 4, KD])
        rec_t = [sb(f"rec{d}", [P, HEADS]) for d in range(2)]
        PS = [ctxs.enter_context(nc.psum_tensor(f"PS{b}", [P, SEQ], F32)) for b in range(4)]

        vpad = SCR[:, 0:VP]
        lxpad = SCR[:, VP:VP + LP]
        T = [SCR[:, 0:SEQ], SCR[:, VP:VP + SEQ]] + [SCR[:, VP + LP + SEQ * n:VP + LP + SEQ * (n + 1)] for n in range(5)]
        LS = T[0][:, 0:5 * 2 * HEADS * ALL // P].rearrange("p (q w) -> p q w", q=5)
        b2 = B2[:].rearrange("p k t -> p (k t)")
        b1 = B1[:].rearrange("p k t -> p (k t)")

        ls_t, sg_t, vc_t, th_t, cs_t = (b2[:, n * D:(n + 1) * D] for n in range(3, 8))
        ada_t = b2[:, 0:3 * D].rearrange("p (k n) -> p k n", k=KD)
        xsH = XCH[:].rearrange("p k t -> p (k t)")[:, 0:SEQ]
        xsL = XCL[:].rearrange("p k t -> p (k t)")[:, 0:SEQ]
        cn = B1[:, 4:6, :].rearrange("p a (b t) -> p (a b) t", t=CTX)
        xs_t, r_t, i_t, a_t, msum_t = T[2:7]
        HN = T[4:6]

        def pcol(name, k=0):
            return PV[:, ds(k + col[name], 1)]

        def pvec(name, n):
            return PV[:, col[name]:col[name] + n]

        RF, RI, RB, RM, RZ, RO = (b2[0:36, ALL * n:ALL * (n + 1)] for n in range(6))
        UN = [b1[0:36, ALL * n:ALL * (n + 1)] for n in range(2, 6)] + [RB]
        stage = [b1[:, ALL * n:ALL * (n + 1)] for n in range(2)]
        RQ = [RI, RF, RO, RZ, RM]

        M = []
        for d, flat in enumerate((b1, b2)):
            m = {}

            def take(buf, off, *parts):
                for name, n, k in parts:
                    m[name] = buf[:, off:off + n].rearrange("p (k n) -> p k n", k=k)
                    off += n
                return off

            loaded = [("q", HQ, HEADS), ("k", HQ, HEADS), ("v", D, D // P), ("U", HQ, HEADS), ("M", HQ, HEADS)]
            n_loaded = sum(n for _, n, _ in loaded)
            m["slots"] = []
            for slot, (buf, off) in enumerate(((flat, 0), (SCR, d * n_loaded))):
                end = take(buf, off, *loaded)
                m["slots"].append({name: m[name] for name, _, _ in loaded} | {
                    "qkv": buf[:, off:off + 2 * HQ + D].rearrange("p (k n) -> p k n", n=P),
                    "kv": buf[:, off + HQ:off + 2 * HQ + D].rearrange("p (k n) -> p k n", n=P),
                    "UM": buf[:, off + 2 * HQ + D:end].rearrange("p (k n) -> p k n", n=P)})
            end = take(flat, n_loaded, ("kw", HQ, HEADS), ("va", HEADS * VW, HEADS), ("q2", HQ, HEADS), ("p", HQ, HEADS),
                       ("h", D, HEADS), ("C", HEADS * VW, HEADS))
            M.append(m)
        NCOL = 3 * 2 * HEADS
        COLS = b1[:, end:end + NCH * NCOL].rearrange("p (c n) -> p c n", n=NCOL)
        ECOL = b2[:, end:end + NCH * 4 * HEADS].rearrange("p (c n) -> p c n", n=4 * HEADS)
        ROWS = b2[0:NCOL, n_loaded + HQ:n_loaded + HQ + ALL]

        def chunk_of(n, d):
            if isinstance(n, int):
                return n if d == 0 else (NC - 1 - n if n < NC else NC + NCH - 1 - n)
            return n if d == 0 else n * -1 + (NC + NCH - 1)

        landed = [sem("landed0"), sem("landed1")]
        hi_done, lo_done, unit_used = sem("hi_done"), sem("lo_done"), sem("unit_used")
        taken = [sem("psum_taken0"), sem("psum_taken1")]
        gates_in = ev("gate_weights_landed")

        class Product:
            unit, tile = 0, 0

            def __init__(self, n, units=None, tiles=None):
                self.U, self.T, self.n = Product.unit, Product.tile, n
                Product.unit += units or n
                Product.tile += tiles or n
                self.end = Product.unit + 2

        L1 = Product(KD, 6 * KD, 4 * KD)
        G1a, G1b = Product(KD // 2), Product(KD // 2)
        G2, G3 = Product(KD), Product(KD)
        GxG, Gx = Product(1), Product(GATE_ROW // P)
        Q_TILES, KV_TILES = HQ // P, (HQ + D) // P
        PAIR = GxG.T % 2
        STORES = [(1 + Gx.n - n + 1) // 2 for n in range(2)]
        G5 = Product(KD)
        G6 = Product(2 * KF)
        down = [(k, min(KD, KF - k)) for k in range(0, KF, KD)]
        G7 = [Product(KD) for _ in down]
        LAST_UNIT = Product.unit

        def cols_of(w, k0, kc, c):
            return w[k0 * P:(k0 + kc) * P, :].rearrange("(k p) n -> p k n", p=P)[:, :, ds(c, P)]

        class Chain:

            def __init__(self, eng, name):
                self.eng, self.sem, self.base, self.i, self.n, self.k = eng, ev(name), 0, 0, 0, 0

            def loop(self, i, n):
                self.base, self.i, self.n, self.k = self.base + self.k, i, n, 0

            def done(self, times):
                assert self.k == self.n, (self.k, self.n)
                self.base, self.i, self.n, self.k = self.base + self.n * times, 0, 0, 0

            def sig(self, ins):
                self.k += 1
                ins.then_inc(self.sem, 1)

            def wait(self, back=0):
                self.eng.wait_ge(self.sem, self.i * self.n + (self.base + self.k - back))

            def link(self, ins):
                self.sig(ins)
                self.wait()

        def bc(a, n):
            return a.rearrange("p (h o) -> p h o", o=1).to_broadcast([a.shape[0], a.shape[1], n])

        def recurrence(eng, prepare, heads, step=None, steps=0):
            def pair(k, at4, seq, seq_next, more=True):
                nxt = at4 + 1
                if more:
                    prepare(k + nxt // 4, nxt % 4 // 2, nxt % 2, seq_next)
                heads(k, at4 // 2, at4 % 2, seq)

            assert NC == 2 and NT % 2 == 0
            prepare(0, 0, 0, False)
            for u in range(4):
                pair(0, u, False, u == 3)
            with eng.Fori(0, NT // 2 - 1) as i:
                if step:
                    step.loop(i, steps)
                for u in range(4):
                    pair(i + 1, u, True, True)
            if step:
                step.done(NT // 2 - 1)
            for u in range(4):
                pair(NCH // 2 - 1, u, True, True, u < 3)

        def indices(k, slot, d):
            n, x = 2 * k + slot, 4 * k + (2 * slot + d)
            return n, x, n + -NC, x + -2 * NC

        block = ctxs.enter_context(nc.Block())

        @block.sync
        def _(sp):
            def unit(U, slot, src, kc=KD, counted=False):
                sp.wait_ge(lo_done, U + 1)
                if counted:
                    sp.sem_inc(ev("sp_passed"), 1)
                sp.dma_start(raw[slot][:, 0:kc, :], src).then_inc(landed[slot], 16)

            def token_load(i, s, src):
                if i is not None:
                    sp.wait_ge(*at(f"xT_pe{s}", i))
                    sp.wait_ge(*at(f"xn_ok{s}", i))
                sp.dma_start(T[1 + s], src).then_inc(ev(f"tok_in{s}"), 16)

            for name in BEGIN_AT_ONE:
                sp.sem_inc(ev(name), 1)
            sp.wait_ge(*at("stage_zero", 1))
            for t, r, n, src in stage_rows:
                sp.dma_start(SCR[r:r + n, t * P:(t + 1) * P], src).then_inc(ev("stage_in"), 16)
            token_load(None, 0, x[0:P, :])
            token_load(None, 1, x[P:2 * P, :])
            with sp.Fori(0, NT // 2 - 1) as i:
                for s in range(2):
                    token_load(i + 1, s, x[ds(2 * P * i + (2 + s) * P, P), :])
            for s in range(NC):
                token_load(NT // 2, s, ctx[s * P:(s + 1) * P, :])
            for q in range(6):
                if q >= 2:
                    sp.wait_ge(*at("mod_used", q - 1))
                sp.dma_start(B2[:, 4 * (q % 2):4 * (q % 2) + 4, :].rearrange("p a (b n) -> p (a b) n", n=4 * P),
                             mod_w.rearrange("(k p) n -> p k n", p=P)[:, :, 4 * P * q:4 * P * (q + 1)]).then_inc(ev(f"mod_in{q % 2}"), 16)
            for s in range(NC):
                sp.wait_ge(*at(f"ctxT_sb{s}", 1))
                sp.dma_start(ctxT_d.rearrange("(k p) t -> p k t", p=P)[:, :, s * P:(s + 1) * P],
                             T[5 + s].rearrange("p (k t) -> p k t", k=KD)).then_inc(ev("ctxT_out"), 16)

            def l1_unit(j, pos):
                U = 6 * j + pos
                slot = pos % 2
                if pos == 2:
                    sp.wait_ge(lo_done, U + 1)
                    sp.dma_start(raw[0][:, 0:1, :], A["wr"][0][ds(j, 1)].rearrange("h d e -> d h e")).then_inc(landed[0], 16)
                    sp.dma_start(raw[0][:, 1:2, :], A["wi"][0][ds(j, 1)].rearrange("h d e -> d h e")).then_inc(gates_in, 16)
                else:
                    group = {0: 3, 1: 4, 3: 1, 4: 0, 5: 2}[pos]
                    unit(U, slot, cols_of(w_in, 0, KD, group * D + P * j), counted=group == 0)

            def ada_load(j, half):
                sp.wait_ge(*at("ada_used", 2 * j + half))
                sp.dma_start(b2[:, 0:3 * D].rearrange("p (k n) -> p k n", k=KD),
                             ada_w.rearrange("(k p) n -> p k n", p=P)[:, :, ds(6 * P * j + 3 * P * half, 3 * P)]).then_inc(ev("ada_in"), 16)

            def l1_store(j):
                sp.wait_ge(*at("lru_y", j + 1))
                sp.dma_start(lru_d[ds(P * j, P), :], ls_t).then_inc(ev("lru_out"), 16)
                sp.wait_ge(*at("cs_sb", j + 1))
                sp.dma_start(cs_d[ds(P * j, P), :], cs_t).then_inc(ev("cs_out"), 16)

            def l1_loads(j, stores):
                l1_unit(j, 0)
                l1_unit(j, 1)
                if stores:
                    l1_store(j - 1)
                l1_unit(j, 2)
                ada_load(j, 0)
                for pos in range(3, 6):
                    l1_unit(j, pos)
                ada_load(j, 1)

            sp.wait_ge(*at("mod_used", 6))
            l1_loads(0, False)
            with sp.Fori(1, KD) as j:
                l1_loads(j, True)
            for u in range(2):
                unit(G1a.U + u, u, cols_of(w_out, KD, KD, u * P))
            l1_store(KD - 1)

            for k in range(KD):
                sp.wait_ge(*at("lru_out", 16 * (k + 1)))
                if k >= 2:
                    sp.wait_ge(*at("xl_G1", k - 1))
                sp.dma_start(T[2 + k % 2], lru_d[k * P:(k + 1) * P, :]).then_inc(ev(f"lru_in{k % 2}"), 16)
            with sp.Fori(0, KD // 2 - 1) as i:
                for s in range(2):
                    unit(G1a.U + 2 + 2 * i + s, s, cols_of(w_out, KD, KD, 2 * P * i + (2 + s) * P))

            def cs_load(t, s, i):
                sp.wait_ge(*at(f"cs_free{s}", i))
                sp.dma_start(T[s], cs_d[ds(P * t, P), :]).then_inc(ev(f"cs_in{s}"), 16)

            sp.wait_ge(*at("cs_out", 16 * KD))
            sp.wait_ge(*at("conv_ok", KD))
            with sp.Fori(0, KD // 2) as i:
                for s in range(2):
                    unit(G2.U + 2 * i + s, s, cols_of(pw2_w, 0, KD, 2 * P * i + s * P))
                    cs_load(2 * i + s, s, i)

            for s in range(2):
                unit(G3.U + s, s, cols_of(w_out, 0, KD, s * P))
            sp.wait_ge(*at("ctxT_out", 16 * NC))
            sp.wait_ge(*at("xl_G3", KD))
            sp.dma_start(cn, ctxT_d.rearrange("(k p) t -> p k t", p=P)).then_inc(ev("ctx_in"), 16)
            for s in range(2):
                sp.wait_ge(*at(f"cs_free{s}", KD // 2))
                sp.wait_ge(*at(f"xT_out{s}", 16 * NT // 2))
                sp.dma_start(T[s], xT_d[s * P:(s + 1) * P, :]).then_inc(ev(f"res_in{s}"), 16)
            with sp.Fori(0, KD // 2 - 1) as i:
                for s in range(2):
                    unit(G3.U + 2 + 2 * i + s, s, cols_of(w_out, 0, KD, 2 * P * i + (2 + s) * P))
                    sp.wait_ge(*at(f"res_free{s}", i + 1))
                    sp.dma_start(T[s], xT_d[ds(2 * P * i + (2 + s) * P, P), :]).then_inc(ev(f"res_in{s}"), 16)

            def proj_unit(t, s):
                unit(GxG.U + t, (GxG.U + s) % 2, cols_of(m_in_w, 0, KD, MP - P if isinstance(t, int) and t == 0 else t * P + -P))

            def proj_store(t, s, ctx=False):
                sp.wait_ge(*at("proj_sb", t + 1))
                c0 = 0 if ctx else CTX
                dst, src = (proj_d[GATE_ROW:MP, c0:ALL], stage[s][P - 4 * HEADS:P, c0:ALL]) if isinstance(t, int) and t == 0 else \
                    (proj_d[ds(t * P + -P, P), c0:ALL], stage[s][:, c0:ALL])
                sp.dma_start(dst, src).then_inc(ev(f"proj_out{s}"), 16)

            for t in range(3):
                proj_unit(t, t % 2)
            sp.wait_ge(*at("x2_sb", KD))
            sp.dma_start(x2_d.rearrange("(k p) t -> p k t", p=P), B2[:]).then_inc(ev("x2_out"), 16)
            proj_store(0, 0, True)

            W = ALL // 16
            sp.wait_ge(*at("proj_out0", 16))
            for d in range(2):
                r = GATE_ROW + (2 * d + 1) * HEADS
                sp.dma_start(LS[64 * d:64 * d + 64, 0, :], proj_d[r:r + HEADS, :].rearrange("h (a w) -> (h a) w", w=W)).then_inc(ev("f_in"), 16)
            proj_unit(3, 1)
            sp.wait_ge(*at("x2_out", 16))
            sp.dma_start(RI[0:HEADS, :], proj_d[GATE_ROW:GATE_ROW + HEADS, :]).then_inc(ev("rows_in"), 16)
            sp.dma_start(UN[0][32:32 + HEADS, :], proj_d[GATE_ROW + 2 * HEADS:GATE_ROW + 3 * HEADS, :]).then_inc(ev("rows_in"), 16)
            proj_store(1, 1)
            sp.wait_ge(*at("lf_sb", 1))
            sp.dma_start(lf_d.rearrange("h (a w) -> (h a) w", w=W), LS[:, 0, :]).then_inc(ev("lf_out"), 16)
            proj_unit(4, 0)
            proj_store(2, 0)
            sp.wait_ge(*at("lf_out", 16))
            sp.dma_start(RF[0:HEADS, :], lf_d[0:HEADS, :]).then_inc(ev("rows_in"), 16)
            sp.dma_start(UN[1][32:32 + HEADS, :], lf_d[HEADS:2 * HEADS, :]).then_inc(ev("rows_in"), 16)
            for t in range(5, Q_TILES + 3):
                proj_unit(t, t % 2)
                proj_store(t - 2, t % 2)

            first = Q_TILES + 1
            with sp.Fori(0, KV_TILES // 2) as i:
                for u in range(2):
                    s = (first + u) % 2
                    proj_unit(2 * i + (first + u + 2), s)
                    proj_store(2 * i + (first + u), s, True)
            first += KV_TILES
            with sp.Fori(0, KD // 2 - 1) as i:
                for u in range(2):
                    s = (first + u) % 2
                    proj_unit(2 * i + (first + u + 2), s)
                    proj_store(2 * i + (first + u), s)
            for t in range(Gx.n - 1, Gx.n + 1):
                unit(GxG.U + t + 2, (GxG.U + t) % 2, cols_of(m_out_w, 0, KD, (t - Gx.n + 1) * P))
                proj_store(t, t % 2)
            sp.wait_ge(*at("rows_sb", 1))
            for q, (f, b) in enumerate(zip(RQ, UN)):
                for d, r in enumerate((f[0:HEADS, :], b[32:32 + HEADS, :])):
                    row = (2 * q + d) * HEADS if q < 3 else NCOL + (2 * d + q - 3) * HEADS
                    sp.dma_start(rows_d[row:row + HEADS, :], r).then_inc(ev("rows_out"), 16)
            sp.wait_ge(*at("rows_out", 16 * 10))
            for s in range(2):
                sp.wait_ge(*at(f"proj_out{s}", 16 * STORES[s]))

            sp.dma_start(ROWS, rows_d[0:NCOL, :]).then_inc(ev("gate_rows_in"), 16)

            def chunk_load(n, d, slot, outputs=True):
                m = M[d]["slots"][slot]
                if not isinstance(n, int) or n >= 2:
                    sp.wait_ge(*at(f"chunk_free{d}", n + -1))
                c = chunk_of(n, d) * P
                r0 = 0 if outputs else HQ
                sp.dma_start(m["qkv" if outputs else "kv"],
                             proj_d[r0:2 * HQ + D, :].rearrange("(h p) t -> p h t", p=P)[:, :, ds(c, P)]).then_inc(ev(f"chunk_in{d}{slot}"), 16)
                r = NCOL + 2 * HEADS * d
                sp.dma_start(m["UM"], rows_d[r:r + 2 * HEADS, ds(c, P)].rearrange("(o h) t -> o h t", o=1)
                             .to_broadcast([P, 2 * HEADS, P])).then_inc(ev(f"chunk_in{d}{slot}"), 16)

            def h_store(j, d):
                sp.wait_ge(*at(f"h_sb{d}", j + 1))
                sp.dma_start(h_d[d][ds((chunk_of(j + NC, d) + -NC) * P, P), :], M[d]["h"].rearrange("p h e -> p (h e)")).then_inc(ev(f"h_out{d}"), 16)

            for n in range(4):
                for d in range(2):
                    chunk_load(n, d, n % 2, n >= NC)
            with sp.Fori(0, NT // 2 - 1) as i:
                for u in range(2):
                    for d in range(2):
                        h_store(2 * i + u, d)
                        chunk_load(2 * i + (u + NC + 2), d, u)
            for j in range(NT - 2, NT):
                for d in range(2):
                    h_store(j, d)

            def read_load(c, s):
                for d, B in enumerate((B1, B2)):
                    sp.dma_start(B[:, ds(c, 1), :], h_d[d].rearrange("(c p) e -> p c e", p=P)[:, ds(c, 1), :]).then_inc(ev(f"h_in{s}"), 16)

            for d in range(2):
                sp.wait_ge(*at(f"h_out{d}", 16 * NT))
                sp.wait_ge(*at(f"chunk_free{d}", NCH))
            for s in range(2):
                read_load(s, s)
            with sp.Fori(0, NT // 2 - 1) as i:
                for s in range(2):
                    sp.wait_ge(*at("hs_ok", 2 * i + s + 1))
                    read_load(2 * i + s + 2, s)
            with sp.Fori(0, (KD - 2) // 2) as i:
                for s in range(2):
                    unit(G5.U + 2 + 2 * i + s, (G5.U + s) % 2, cols_of(m_out_w, 0, KD, 2 * P * i + (2 + s) * P))
            for s in range(2):
                unit(G6.U + s, (G6.U + s) % 2, cols_of(up_w, 0, KD, FFN * (1 - s)))
            sp.wait_ge(*at("yT_ok", NT))
            for k in range(KD):
                if k >= 2:
                    sp.wait_ge(*at("x3_sb", k - 1))
                sp.dma_start(T[k % 2], x2_d[k * P:(k + 1) * P, :]).then_inc(ev(f"x2_in{k % 2}"), 16)
            def act_store(j):
                sp.wait_ge(*at("act_sb", j + 1))
                sp.dma_start(act_d[ds(P * j, P), :], T[2]).then_inc(ev("act_out"), 16)

            with sp.Fori(0, KF - 1) as j:
                unit(G6.U + 2 + 2 * j, G6.U % 2, cols_of(up_w, 0, KD, P * j + (FFN + P)))
                unit(G6.U + 3 + 2 * j, (G6.U + 1) % 2, cols_of(up_w, 0, KD, P * j + P))
                act_store(j)
            for s in range(2):
                unit(G7[0].U + s, (G7[0].U + s) % 2, cols_of(down_w, 0, KD, s * P))
            act_store(KF - 1)
            n = 0
            sp.wait_ge(*at("act_out", 16 * KF))
            for g, (k0, kc) in enumerate(down):
                for k in range(kc):
                    if n >= 2:
                        sp.wait_ge(*at("xl_G7", n - 1))
                    sp.dma_start(T[4 + n % 2], act_d[(k0 + k) * P:(k0 + k + 1) * P, :]).then_inc(ev(f"act_in{n % 2}"), 16)
                    n += 1
                with sp.Fori(0, (KD - 2) // 2) as i:
                    for s in range(2):
                        unit(G7[g].U + 2 + 2 * i + s, (G7[g].U + s) % 2, cols_of(down_w, k0, kc, 2 * P * i + (2 + s) * P), kc)
                if g + 1 < len(down):
                    for s in range(2):
                        unit(G7[g + 1].U + s, (G7[g + 1].U + s) % 2, cols_of(down_w, *down[g + 1], s * P), down[g + 1][1])
            with sp.Fori(0, NT // 2) as i:
                for s in range(2):
                    sp.wait_ge(*at("fin_sb", 2 * i + s + 1))
                    sp.dma_start(out[0][ds(2 * P * i + s * P, P), :], T[2 + s]).then_inc(ev(f"fin_out{s}"), 16)
            for s in range(2):
                sp.wait_ge(*at(f"fin_out{s}", 16 * NT // 2))

        @block.gpsimd
        def _(pool):
            step = Chain(pool, "pool_step")
            tt = nc.gpsimd.tensor_tensor

            def low(U, slot, kc=KD):
                pool.wait_ge(hi_done, U + 1)
                tt(wl[slot][:, 0:kc, :], raw[slot][:, 0:kc, :], wh[slot][:, 0:kc, :].bitcast(F32), ALU.subtract).then_inc(lo_done, 1)

            pool.sem_inc(lo_done, 2)
            nc.gpsimd.memset(ident[:], 0.0).then_inc(step.sem, 1)
            nc.gpsimd.memset(avg[:], 1.0 / D).then_inc(step.sem, 1)
            nc.gpsimd.memset(mask[0][:], 0.0).then_inc(step.sem, 1)
            nc.gpsimd.memset(mask[1][:], 0.0).then_inc(step.sem, 1)
            nc.gpsimd.memset(eps[:], EPS).then_inc(step.sem, 1)
            step.k = 5
            step.wait()
            nc.gpsimd.affine_select(out=ident[:], in_=ident[:], compare_op=ALU.not_equal, fill=1.0, base=0,
                                    pattern=[[-1, P]], channel_multiplier=1).then_inc(ev("consts"), 1)
            nc.gpsimd.affine_select(out=mask[0][:], in_=mask[0][:], compare_op=ALU.is_ge, fill=BIG, base=0,
                                    pattern=[[1, P]], channel_multiplier=-1).then_inc(ev("consts"), 1)
            nc.gpsimd.affine_select(out=mask[1][:], in_=mask[1][:], compare_op=ALU.is_ge, fill=BIG, base=0,
                                    pattern=[[-1, P]], channel_multiplier=1).then_inc(ev("consts"), 1)

            low(0, 0)
            pool.wait_ge(*at("xl_L1", KD))
            nc.gpsimd.memset(msum_t, 0.0).then_inc(ev("msum_zero"), 1)
            nc.gpsimd.memset(vpad[:, 0:TAPS - 1], 0.0).then_inc(ev("pads_zero"), 1)
            nc.gpsimd.memset(lxpad[:, 0:SHORT - 1], 0.0).then_inc(ev("pads_zero"), 1)

            def conv_sum(j):
                pool.wait_ge(*at("conv_ok", j + 1))
                pool.wait_ge(*at("msum_ok", j))
                pool.wait_ge(*at("msum_zero", 1))
                tt(msum_t, msum_t, B1[:, ds(j, 1), :].rearrange("p a t -> p (a t)"), ALU.add).then_inc(ev("msum_ok"), 1)

            def l1_pool(j, summed):
                U = 6 * j
                low(U + 1, 1)
                pool.wait_ge(*at("xsh", j + 1))
                tt(xsL, xs_t, xsH.bitcast(F32), ALU.subtract).then_inc(ev("xsl"), 1)
                low(U + 2, 0, 2)
                low(U + 3, 1)
                pool.wait_ge(*at("i_ok", j + 1))
                tt(i_t, i_t, xs_t, ALU.mult).then_inc(ev("ixs"), 1)
                low(U + 4, 0)
                pool.wait_ge(*at("th_ok", j + 1))
                tt(th_t, th_t, r_t, ALU.mult).then_inc(ev("m2"), 1)
                low(U + 5, 1)
                low(U + 6, 0)
                pool.wait_ge(*at("mult_ok", j + 1))
                tt(i_t, th_t, i_t, ALU.mult).then_inc(ev("bx"), 1)
                if summed:
                    conv_sum(j - 1)
                pool.wait_ge(*at("vc_ok", j + 1))
                pool.wait_ge(*at("pads_zero", 2))
                tt(vpad[:, TAPS - 1:TAPS - 1 + SEQ], vc_t, sg_t, ALU.mult).then_inc(ev("vpad_ok"), 1)

            l1_pool(0, False)
            with pool.Fori(1, KD) as j:
                l1_pool(j, True)

            for k in range(KD):
                pool.wait_ge(*at("xh_G1", k + 1))
                tt(XL[:, k, :], T[2 + k % 2], XH[:, k, :].bitcast(F32), ALU.subtract).then_inc(ev("xl_G1"), 1)

            def low_tiles(g, n=None):
                n = n or g.n
                if n >= 2:
                    with pool.Fori(0, n // 2) as i:
                        for s in range(2):
                            low(g.U + 1 + 2 * i + s, (g.U + 1 + s) % 2)
                if n % 2:
                    low(g.U + n, (g.U + n) % 2)

            for i in range(2):
                low(G1a.U + 1 + i, (G1a.U + 1 + i) % 2)
            conv_sum(KD - 1)
            for i in range(2, 4):
                low(G1a.U + 1 + i, (G1a.U + 1 + i) % 2)
            low_tiles(G1b)
            low_tiles(G2)
            pool.wait_ge(*at("xl_G2", KD))
            nc.gpsimd.memset(T[4], 0.0).then_inc(ev("ssq_ok"), 1)
            nc.gpsimd.memset(T[6], 0.0).then_inc(ev("ssq_ok"), 1)
            with pool.Fori(0, KD // 2) as i:
                for s in range(2):
                    low(G3.U + 1 + 2 * i + s, (G3.U + 1 + s) % 2)
                    pool.wait_ge(*at("sq_ok", 2 * i + s + 1))
                    pool.wait_ge(*at("ssq_ok", 2 * (2 * i + s) + 2))
                    tt(T[4], T[4], T[3], ALU.add).then_inc(ev("ssq_ok"), 1)
                    tt(T[6], T[6], T[5], ALU.add).then_inc(ev("ssq_ok"), 1)
            low_tiles(GxG)
            low_tiles(Gx)

            def q2(j, d, slot):
                m = M[d]["slots"][slot]
                pool.wait_ge(*at("w_ok", 2 * j + (2 * NC + d + 1)))
                pool.wait_ge(*at("dc_ps", HEADS * 2 * j + HEADS * (2 * NC + d - 1)))
                tt(M[d]["q2"], m["q"], m["U"], ALU.mult).then_inc(ev("q2_ok"), 1)

            with pool.Fori(0, NT // 2) as i:
                for u in range(2):
                    for d in range(2):
                        q2(2 * i + u, d, u)
            with pool.Fori(0, NT // 2) as i:
                for s in range(2):
                    pool.wait_ge(*at(f"o_in{s}", 16 * i + 16))
                    o = T[s].rearrange("p (k t) -> p k t", k=KD)
                    tt(o, o, bc(pvec("m_norm_g_2", KD), P), ALU.mult).then_inc(ev("gate_ok"), 1)
            pool.wait_ge(*at("yT_ok", NT))
            pool.wait_ge(*at("xl_r", NT))
            nc.gpsimd.memset(T[4], 0.0).then_inc(ev("yssq_ok"), 1)
            nc.gpsimd.memset(T[5], 0.0).then_inc(ev("xssq_zero"), 1)
            with pool.Fori(0, KD // 2) as i:
                for s in range(2):
                    low(G5.U + 1 + 2 * i + s, (G5.U + 1 + s) % 2)
                    pool.wait_ge(*at("ysq_ok", 2 * i + s + 1))
                    pool.wait_ge(*at("yssq_ok", 2 * i + s + 1))
                    tt(T[4], T[4], T[3], ALU.add).then_inc(ev("yssq_ok"), 1)
            low_tiles(G6)
            for g in range(len(down)):
                last = g == len(down) - 1
                if not last:
                    low_tiles(G7[g])
                else:
                    nc.gpsimd.memset(T[0], 0.0).then_inc(ev("zssq_ok"), 1)
                    for t in range(KD):
                        if t < KD - 1:
                            low(G7[g].U + 1 + t, (G7[g].U + 1 + t) % 2, down[g][1])
                        pool.wait_ge(*at("zsq_ok", t + 1))
                        pool.wait_ge(*at("zssq_ok", t + 1))
                        tt(T[0], T[0], T[3], ALU.add).then_inc(ev("zssq_ok"), 1)

        @block.scalar
        def _(act):
            step = Chain(act, "act_step")
            f = nc.scalar.activation

            def high(U, slot, kc=KD):
                act.wait_ge(landed[slot], U // 2 * 16 + 16)
                act.wait_ge(unit_used, U + 1)
                f(wh[slot][:, 0:kc, :], raw[slot][:, 0:kc, :], ACT.Copy).then_inc(hi_done, 1)

            def high_at(base, i, kc=KD):
                act.wait_ge(landed[base % 2], 16 * i + 16 * (base // 2 + 1))
                act.wait_ge(unit_used, 2 * i + (base + 1))
                f(wh[base % 2][:, 0:kc, :], raw[base % 2][:, 0:kc, :], ACT.Copy).then_inc(hi_done, 1)

            def second(g, kc=KD):
                high_at(g.U + 1, 0, kc)

            def tiles(g, evac, opened=True, kc=KD, kc_next=KD):
                def pair(i, first, kcs):
                    for s in range(2):
                        if not (first and s == 0):
                            high_at(g.U + 1 + s, i, kcs[s])
                        if evac:
                            act.wait_ge(unit_used, 2 * i + (g.U + s + 3))
                            evac(2 * i + s, PS[(g.T + s) % 2], taken[(g.T + s) % 2])

                pair(0, opened, (kc, kc))
                if g.n // 2 > 2:
                    with act.Fori(1, g.n // 2 - 1) as i:
                        pair(i, False, (kc, kc))
                pair(g.n // 2 - 1, False, (kc, kc_next))

            act.wait_ge(*at("consts", 3))

            def token(i, s, transposed=True):
                act.wait_ge(*at(f"tok_in{s}", 16 * i + 16))
                act.wait_ge(*at(f"xnT_pe{s}", i))
                step.link(f(T[3 + s], T[1 + s], ACT.Square, accum_out=small[:, 0, s:s + 1]))
                f(small[:, 1, s:s + 1], small[:, 0, s:s + 1], ACT.Sqrt, scale=1.0 / D, bias=eps[:]).then_inc(ev(f"rms{s}"), 1)
                if transposed:
                    act.wait_ge(*at(f"xT_pe{s}", i + 1))
                    act.wait_ge(*at(f"xT_out{s}", 16 * i))
                    f(T[5 + s], PS[s][:], ACT.Copy).then_inc(ev(f"xT_sb{s}"), 1)
                    act.wait_ge(*at(f"xT_sb{s}", i + 1))
                    act.dma_start(xT_d.rearrange("(k p) t -> p k t", p=P)[:, :, ds(2 * P * i + s * P, P)],
                                  T[5 + s].rearrange("p (k t) -> p k t", k=KD)).then_inc(ev(f"xT_out{s}"), 16)

            with act.Fori(0, NT // 2) as i:
                step.loop(i, 2)
                for s in range(2):
                    token(i, s)
            step.done(NT // 2)
            for s in range(NC):
                token(NT // 2, s, False)

            act.wait_ge(*at("pv", 1))
            for n, name in enumerate(("c", "c", "c_2", "c_ctx")):
                f(CA[:, :, n], pvec(name, KD), ACT.Silu).then_inc(ev("ca"), 1)
            step.link(f(lam4[:, 0, :], pvec("lam", KD), ACT.Abs))
            f(lam4[:, 1, :], lam4[:, 0, :], ACT.Exp, scale=-1.0).then_inc(ev("lam_e"), 1)
            high(0, 0)
            act.wait_ge(*at("mod_ok", 1))
            for k in range(KD):
                f(XH[:, k, :], B1[:, k, :], ACT.Identity, scale=SC[:, 0, k:k + 1], bias=MOD[:, k:k + 1]).then_inc(ev("xh_L1"), 1)

            act.wait_ge(*at("pj", 1))

            def l1_act(j):
                U = 6 * j
                def land(pos):
                    act.wait_ge(landed[pos % 2], 48 * j + 16 * (pos // 2 + 1))
                def hi(pos, kc=KD):
                    land(pos)
                    act.wait_ge(unit_used, U + pos + 1)
                    f(wh[pos % 2][:, 0:kc, :], raw[pos % 2][:, 0:kc, :], ACT.Copy).then_inc(hi_done, 1)

                step.link(f(PJa[:], PJ[:, ds(j, 1), :].rearrange("p a n -> p (a n)"), ACT.Copy))
                hi(1)
                act.wait_ge(unit_used, U + 3)
                act.wait_ge(*at("xs_ok", j))
                f(lxpad[:, SHORT - 1:SHORT - 1 + SEQ], PS[0][:], ACT.Copy).then_inc(ev("lx_sb"), 1)
                act.wait_ge(*at("lx_sb", j + 1))
                act.sem_inc(taken[0], 1)
                act.wait_ge(*at("xs_ok", j + 1))
                act.wait_ge(*at("ri_ps", j))
                f(xsH, xs_t, ACT.Copy).then_inc(ev("xsh"), 1)
                act.wait_ge(gates_in, 16 * j + 16)
                hi(2, 2)
                act.wait_ge(unit_used, U + 4)
                act.wait_ge(*at("lru_out", 16 * j))
                f(ls_t, PS[1][:], ACT.Silu).then_inc(ev("ls_sb"), 1)
                act.wait_ge(*at("ls_sb", j + 1))
                act.sem_inc(taken[1], 1)
                hi(3)
                act.wait_ge(*at("ri_ps", j + 1))
                act.wait_ge(*at("lru_y", j))
                f(r_t, PS[2][:], ACT.Sigmoid, bias=PJa[:, TAPS + SHORT + 2:TAPS + SHORT + 3]).then_inc(ev("r_ok"), 1)
                f(i_t, PS[3][:], ACT.Sigmoid, bias=PJa[:, TAPS + SHORT + 3:TAPS + SHORT + 4]).then_inc(ev("i_ok"), 1)
                hi(4)
                act.wait_ge(unit_used, U + 6)
                act.wait_ge(*at("vpad_ok", j))
                f(sg_t, PS[0][:], ACT.Sigmoid).then_inc(taken[0], 1)
                act.wait_ge(*at("r_ok", j + 1))
                f(th_t, r_t, ACT.Tanh, scale=PJa[:, TAPS + SHORT + 5:TAPS + SHORT + 6]).then_inc(ev("th_raw"), 1)
                f(a_t, r_t, ACT.Exp, scale=PJa[:, TAPS + SHORT + 4:TAPS + SHORT + 5]).then_inc(ev("a_ok"), 1)
                act.wait_ge(*at("a_ok", j + 1))
                act.wait_ge(*at("th_raw", j + 1))
                step.link(f(r_t, a_t, ACT.Square))
                f(r_t, r_t, ACT.Copy, bias=1.0).then_inc(ev("th_ok"), 1)
                hi(5)
                act.wait_ge(unit_used, U + 7)
                f(vc_t, PS[1][:], ACT.Copy).then_inc(ev("vc_ok"), 1)
                act.wait_ge(*at("vc_ok", j + 1))
                act.sem_inc(taken[1], 1)
                act.wait_ge(landed[0], 48 * j + 64)
                act.wait_ge(unit_used, U + 7)
                f(wh[0][:], raw[0][:], ACT.Copy).then_inc(hi_done, 1)
                act.wait_ge(*at("m2", j + 1))
                f(th_t, th_t, ACT.Sqrt).then_inc(ev("mult_ok"), 1)
                act.wait_ge(*at("cs_ps", j + 1))
                act.wait_ge(*at("cs_out", 16 * j))
                f(cs_t, PS[2][:], ACT.Silu).then_inc(ev("cs_sb"), 1)

            with act.Fori(0, KD) as j:
                step.loop(j, 2)
                l1_act(j)
            step.done(KD)

            second(G1a)
            for k in range(KD):
                act.wait_ge(*at(f"lru_in{k % 2}", 16 * (k // 2 + 1)))
                if k == 0:
                    act.wait_ge(unit_used, L1.end)
                f(XH[:, k, :], T[2 + k % 2], ACT.Copy).then_inc(ev("xh_G1"), 1)
            act.wait_ge(*at("vpad_ok", KD))
            act.wait_ge(*at("cs_out", 16 * KD))
            act.wait_ge(*at("ada_used", 2 * KD))
            for g, k0 in ((G1a, 0), (G1b, KD // 2)):
                tiles(g, lambda t, ps, tk: f(B2[:, ds(t + k0, 1), :].rearrange("p a t -> p (a t)"), ps[:], ACT.Copy).then_inc(tk, 1), g is G1a)

            second(G2)
            act.wait_ge(*at("var_ps", 1))
            f(T[3], PS[3][:], ACT.Sqrt, bias=eps[:]).then_inc(ev("ln_sd"), 1)
            for k in range(KD):
                act.wait_ge(*at("ln_t", k + 1))
                if k >= 2:
                    act.wait_ge(*at("xl_G2", k - 1))
                elif k == 1:
                    act.wait_ge(*at("ln_t", 2))
                step.link(f(T[2 + k % 2], B1[:, k, :], ACT.Silu, scale=pcol("cln_g", k), bias=pcol("cln_b", k)))
                if k == 0:
                    act.wait_ge(unit_used, G1b.end)
                f(XH[:, k, :], T[2 + k % 2], ACT.Copy).then_inc(ev("xh_G2"), 1)
            tiles(G2, None)
            second(G3)
            for k in range(KD):
                act.wait_ge(*at("yconv_ok", KD))
                act.wait_ge(unit_used, G2.end)
                f(XH[:, k, :], B1[:, k, :], ACT.Copy).then_inc(ev("xh_G3"), 1)
            act.wait_ge(*at("ctx_in", 16))
            act.wait_ge(*at("sc_ok", 1))
            for k in range(KD):
                f(XCH[:, k, :], cn[:, k, :], ACT.Identity, scale=SC[:, 4, k:k + 1], bias=ADA[:, k, 1:2]).then_inc(ev("xh_c"), 1)

            def x1_squares(i, opened=False):
                for s in range(2):
                    if not (opened and s == 0):
                        high_at(G3.U + 1 + s, i)
                    t = 2 * i + s
                    act.wait_ge(*at("x1_ok", t + 1))
                    act.wait_ge(*at("ssq_ok", 2 * t + 2))
                    x1 = B2[:, ds(t, 1), :].rearrange("p a t -> p (a t)")
                    f(T[3], x1, ACT.Square).then_inc(ev("sq1"), 1)
                    f(T[5], x1, ACT.Square, scale=pcol("final_g", t)).then_inc(ev("sq_ok"), 1)

            x1_squares(0, True)
            with act.Fori(1, KD // 2) as i:
                x1_squares(i)

            high_at(Gx.U, 0)
            act.wait_ge(*at("stat1_ps", 1))
            f(T[3], PS[2][:], ACT.Sqrt, bias=eps[:]).then_inc(ev("n1_sd1"), 1)
            act.wait_ge(*at("n1_ms", 1))
            f(T[3], T[1], ACT.Sqrt, bias=eps[:]).then_inc(ev("n1_sd2"), 1)
            for k in range(KD):
                act.wait_ge(*at("x2n", k + 1))
                f(XH[:, k, :], T[4 + k % 2], ACT.Identity, bias=ADA[:, k, 0:1]).then_inc(ev("xh_Gx"), 1)

            def proj(t, s, bias, ctx=False, fn=ACT.Identity):
                b = (PAIR + s) % 2
                act.wait_ge(unit_used, t + (GxG.U + 3))
                act.wait_ge(*at(f"proj_out{s}", 8 * t + -8 * s))
                if ctx:
                    step.sig(f(stage[s][:, 0:CTX], PS[2 + s][:, 0:CTX], fn, bias=bias))
                step.sig(f(stage[s][:, CTX:ALL], PS[b][:], fn, bias=bias))
                step.wait()
                act.sem_inc(ev("proj_sb"), 1)
                act.sem_inc(taken[b], 1)

            def proj_pairs(first, n, ctx=False, fn=ACT.Identity):
                with act.Fori(0, n // 2) as i:
                    step.loop(i, 4 if ctx else 2)
                    for u in range(2):
                        high_at(GxG.U + first + u + 1, i)
                        proj(2 * i + (first + u), (first + u) % 2, pcol("m_in_b", 2 * i + (first + u - 1)), ctx, fn)
                step.done(n // 2)

            proj(0, 0, pcol("gate_b"), True)
            for t in range(1, Q_TILES + 1):
                high_at(GxG.U + t + 1, 0)
                proj(t, t % 2, pcol("m_in_b", t - 1))
                if t == 1:
                    act.wait_ge(*at("f_in", 32))
                    step.link(f(LS[:, 1, :], LS[:, 0, :], ACT.Abs))
                    f(LS[:, 1, :], LS[:, 1, :], ACT.Exp, scale=-1.0).then_inc(ev("f_e"), 1)
            proj_pairs(Q_TILES + 1, KV_TILES, True)
            proj_pairs(Q_TILES + KV_TILES + 1, KD, False, ACT.Sigmoid)

            act.wait_ge(*at("cols_sb", 1))
            f(ECOL, COLS[:, :, 2 * HEADS:NCOL], ACT.Exp).then_inc(ev("ecol"), 1)

            def weights(k, slot, d, seq):
                m = M[d]["slots"][slot]
                n, x, j, y = indices(k, slot, d)
                act.wait_ge(*at(f"chunk_in{d}{slot}", 32 * k + 32))
                f(m["U"], m["U"], ACT.Exp).then_inc(ev("w_ok"), 1)
                if seq:
                    act.wait_ge(*at("d_ok", y + 1))
                    f(m["M"], m["M"], ACT.Exp, scale=-1.0).then_inc(ev("e_ok"), 1)
                act.wait_ge(*at("t_ps", x + 1))
                act.wait_ge(*at("rec_zero", 1))
                f(M[d]["va"][:, :, 0:DV], PS[1][:].rearrange("p (h e) -> p h e", h=HEADS), ACT.Copy).then_inc(ev("va_ok"), 1)

            def heads(k, slot, d, seq):
                if not seq:
                    return
                n, x, j, y = indices(k, slot, d)
                act.wait_ge(*at("rec_ok", y + 1))
                act.wait_ge(*at(f"h_out{d}", 16 * j))
                for h in range(HEADS):
                    act.wait_ge(*at("num_ps", HEADS * y + (h // 2 * 2 + 2)))
                    f(M[d]["h"][:, h, :], PS[3][:, DV * h:DV * (h + 1)], ACT.Copy, scale=rec_t[d][:, h:h + 1]).then_inc(ev("num_free"), 1)
                act.wait_ge(*at("num_free", HEADS * y + HEADS))
                act.sem_inc(ev(f"h_sb{d}"), 1)

            recurrence(act, weights, heads)

            def read_ssq(c):
                act.wait_ge(*at("hs_ok", c + 1))
                for h in range(HEADS):
                    e = slice(h * DV, (h + 1) * DV)
                    ins = f(B2[:, ds(c, 1), e].rearrange("p a e -> p (a e)"), B1[:, ds(c, 1), e].rearrange("p a e -> p (a e)"), ACT.Square,
                            accum_out=small[:, 3, h:h + 1])
                step.link(ins)
                f(small[:, 4, 0:HEADS], small[:, 3, 0:HEADS], ACT.Sqrt, scale=1.0 / DV, bias=eps[:]).then_inc(ev("hrms"), 1)

            def gate_load(c, s):
                act.dma_start(T[s].rearrange("p (k t) -> p k t", k=KD),
                              proj_d[GATE_ROW - D:GATE_ROW, :].rearrange("(k p) t -> p k t", p=P)[:, :, ds(P * c + CTX, P)]).then_inc(ev(f"o_in{s}"), 16)

            def read_high(c, s, load=True):
                act.wait_ge(*at("yT_ok", c + 1))
                if load:
                    gate_load(c + 2, s)
                f(XH[:, :, ds(P * c, P)], T[2 + s].rearrange("p (k t) -> p k t", k=KD), ACT.Copy).then_inc(ev("xh_r"), 1)

            for d in range(2):
                act.wait_ge(*at(f"chunk_free{d}", NCH))
            gate_load(0, 0)
            gate_load(1, 1)
            second(G5)
            read_ssq(0)
            read_ssq(1)
            with act.Fori(0, NT // 2 - 1) as i:
                step.loop(i, 2)
                for s in range(2):
                    read_high(2 * i + s, s)
                    read_ssq(2 * i + s + 2)
            step.done(NT // 2 - 1)
            read_high(NT - 2, 0, False)
            read_high(NT - 1, 1, False)

            def y_tiles(i, opened=False):
                for s in range(2):
                    if not (opened and s == 0):
                        high_at(G5.U + 1 + s, i)
                    t = 2 * i + s
                    b = (G5.T + s) % 2
                    act.wait_ge(unit_used, 2 * i + (G5.U + s + 3))
                    f(B1[:, ds(t, 1), :].rearrange("p a t -> p (a t)"), PS[b][:], ACT.Copy).then_inc(ev("y_sb"), 1)
                    act.wait_ge(*at("yssq_ok", t + 1))
                    f(T[3], PS[b][:], ACT.Square).then_inc(ev("ysq_ok"), 1)
                    act.wait_ge(*at("y_sb", t + 1))
                    act.wait_ge(*at("ysq_ok", t + 1))
                    act.sem_inc(taken[b], 1)

            y_tiles(0, True)
            with act.Fori(1, KD // 2) as i:
                y_tiles(i)
            second(G6)
            act.wait_ge(*at("stat2_ps", 1))
            f(T[6], PS[2][:], ACT.Sqrt, bias=eps[:]).then_inc(ev("n2_sd"), 1)
            for k in range(KD):
                act.wait_ge(*at("x3_sb", k + 1))
                if k == 0:
                    act.wait_ge(*at("stat2_ps", 1))
                if k >= 2:
                    act.wait_ge(*at("xssq_ok", k - 1))
                f(T[2 + k % 2], B2[:, k, :], ACT.Square).then_inc(ev("xsq_ok"), 1)
            act.wait_ge(*at("stat3_ps", 1))
            act.wait_ge(*at("n2_done", 1))
            f(T[6], PS[3][:], ACT.Sqrt, bias=eps[:]).then_inc(ev("n3_sd"), 1)
            for k in range(KD):
                act.wait_ge(*at("h2_t", k + 1))
                if k == 0:
                    act.wait_ge(unit_used, G5.end)
                f(XH[:, k, :], T[2 + k % 2], ACT.Identity, bias=ADA[:, 3 * KD + k, 0:1]).then_inc(ev("xh_G6"), 1)
            def ffn_tile(j, opened=False, kc_next=KD):
                if not opened:
                    high_at(G6.U + 1, j)
                b = G6.T % 2
                act.wait_ge(unit_used, 2 * j + (G6.U + 3))
                act.wait_ge(*at("ffn_conv", j))
                act.wait_ge(*at("ffn_silu", j))
                f(T[0], PS[b][:], ACT.Copy).then_inc(ev("g_sb"), 1)
                f(T[1], PS[b][:], ACT.Identity, scale=pcol("ffn_conv_w", j + KF), bias=pcol("ffn_conv_b_2", j)).then_inc(ev("g_sb"), 1)
                act.wait_ge(*at("g_sb", 2 * j + 2))
                act.sem_inc(taken[b], 1)
                high_at(G6.U + 2, j)
                act.wait_ge(*at("ffn_conv", j + 1))
                act.wait_ge(*at("act_sb", j))
                f(T[3], T[1], ACT.Silu).then_inc(ev("ffn_silu"), 1)

            ffn_tile(0, True)
            with act.Fori(1, KF) as j:
                ffn_tile(j)
            n = 0
            for g, (k0, kc) in enumerate(down):
                second(G7[g], kc)
                for k in range(kc):
                    act.wait_ge(*at(f"act_in{n % 2}", 16 * (n // 2 + 1)))
                    if k == 0:
                        act.wait_ge(unit_used, (G6 if g == 0 else G7[g - 1]).end)
                    f(XH[:, k, :], T[4 + n % 2], ACT.Copy).then_inc(ev("xh_G7"), 1)
                    n += 1
                if g < len(down) - 1:
                    tiles(G7[g], None, True, kc, down[g + 1][1])
                else:
                    for t in range(KD):
                        if 1 <= t < KD - 1:
                            high_at(G7[g].U + 1 + t, 0, kc)
                        act.wait_ge(*at("z_ok", (g + 1) * KD - KD + t + 1))
                        act.wait_ge(*at("zssq_ok", t + 1))
                        f(T[3], B1[:, t, :], ACT.Square).then_inc(ev("zsq_ok"), 1)
            act.wait_ge(*at("stat4_ps", 1))
            f(T[6], PS[2][:], ACT.Sqrt, bias=eps[:]).then_inc(ev("n4_sd"), 1)
            for t in range(NT):
                act.wait_ge(*at("out_ps", t + 1))
                if t >= 2:
                    act.wait_ge(*at(f"fin_out{t % 2}", 16 * (t // 2)))
                f(T[2 + t % 2], PS[t % 2][:], ACT.Copy).then_inc(ev("fin_sb"), 1)

        @block.tensor
        def _(pe):
            mm = nc.tensor.matmul

            def product(ps, w, kc, X, n, first=0):
                XHt, XLt = X
                step_n = min(n, 512)
                total, seen = 3 * kc, 0
                for k in range(kc):
                    for W, Y in ((wh[w], XHt), (wl[w], XHt), (wh[w], XLt)):
                        for c in range(0, n, step_n):
                            last = mm(ps[:, c:c + step_n], W[:, k, :], Y[:, k, c:c + step_n], start=(seen == 0), stop=(seen == total - 1))
                        seen += 1
                return last

            def tile(U, slot, ps, tk, nth, kc=KD, X=(XH, XL), n=SEQ):
                pe.wait_ge(lo_done, U + 3)
                pe.wait_ge(tk, nth + 1)
                product(ps, slot, kc, X, n).then_inc(unit_used, 1)

            def opening(g, ready, kc=KD, before=0):
                pe.wait_ge(lo_done, g.U + 4)
                for s in range(2):
                    pe.wait_ge(taken[(g.T + s) % 2], (g.T + s) // 2 + 1)
                for k in range(kc):
                    pe.wait_ge(*at(ready, before + k + 1))
                    for s in range(2):
                        w, ps = (g.U + s) % 2, PS[(g.T + s) % 2]
                        for n, (W, Y) in enumerate(((wh[w], XH), (wl[w], XH), (wh[w], XL))):
                            for c in range(0, SEQ, 512):
                                last = mm(ps[:, c:c + 512], W[:, k, :], Y[:, k, c:c + 512], start=(k == 0 and n == 0), stop=(k == kc - 1 and n == 2))
                        if k == kc - 1:
                            last.then_inc(unit_used, 1)

            def tiles(g, opened=True, **kw):
                with pe.Fori(1 if opened else 0, g.n // 2) as i:
                    for s in range(2):
                        b = (g.T + s) % 2
                        tile(2 * i + (g.U + s), (g.U + s) % 2, PS[b], taken[b], i + (g.T + s) // 2, **kw)

            def stat(ps, src, event):
                for c in range(2):
                    last = mm(ps[:, 512 * c:512 * c + 512], avg[:], src[:, 512 * c:512 * c + 512], start=True, stop=True)
                last.then_inc(ev(event), 1)

            pe.sem_inc(unit_used, 2)
            pe.sem_inc(taken[0], 1)
            pe.sem_inc(taken[1], 1)
            pe.wait_ge(*at("consts", 3))
            pe.wait_ge(*at("stage_in", 16 * len(stage_rows)))
            for t in range(NST):
                last = nc.tensor.transpose(PS[2][:, t * P:(t + 1) * P], SCR[:, t * P:(t + 1) * P], ident[:])
            last.then_inc(ev("stage_ps"), 1)

            def token(i, s, both=True):
                if both:
                    pe.wait_ge(*at(f"tok_in{s}", 16 * i + 16))
                    pe.wait_ge(*at(f"xT_sb{s}", i))
                    for k in range(KD):
                        last = nc.tensor.transpose(PS[s][:, k * P:(k + 1) * P], T[1 + s][:, k * P:(k + 1) * P], ident[:])
                    last.then_inc(ev(f"xT_pe{s}"), 1)
                pe.wait_ge(*at(f"xn_ok{s}", i + 1))
                pe.wait_ge(*at(f"xnT_sb{s}", i))
                for k in range(KD):
                    last = nc.tensor.transpose(PS[2 + s][:, k * P:(k + 1) * P], T[3 + s][:, k * P:(k + 1) * P], ident[:])
                last.then_inc(ev(f"xnT_pe{s}"), 1)

            pe.wait_ge(*at("pv", 1))
            with pe.Fori(0, NT // 2) as i:
                for s in range(2):
                    token(i, s)
            for s in range(NC):
                token(NT // 2, s, False)
            pe.wait_ge(*at("ca", 4))
            pe.wait_ge(*at("ctxT_sb1", 1))
            for q in range(6):
                pe.wait_ge(*at(f"mod_in{q % 2}", 16 * (q // 2 + 1)))
                w = B2[:, 4 * (q % 2):4 * (q % 2) + 4, :].rearrange("p a (b n) -> p (a b) n", n=4 * P)
                for c in range(4):
                    for k in range(KD):
                        last = mm(PS[3][:, 8 * q + 2 * c:8 * q + 2 * c + 2], w[:, k, c * P:(c + 1) * P], CA[:, k, 0:2],
                                  start=(k == 0), stop=(k == KD - 1))
                last.then_inc(ev("mod_used"), 1)

            def ada(j, half):
                pe.wait_ge(*at("ada_in", 32 * j + 16 * (half + 1)))
                for c in range(3):
                    for k in range(KD):
                        last = mm(PS[3][:, 512 * half + 2 * c:512 * half + 2 * c + 2], ada_t[:, k, c * P:(c + 1) * P], CA[:, k, 2:4],
                                  start=(k == 0), stop=(k == KD - 1))
                last.then_inc(ev("ada_used"), 1)

            pe.wait_ge(*at("xl_L1", KD))
            with pe.Fori(0, KD) as j:
                U = 6 * j
                tile(U, 0, PS[0], taken[0], 2 * j)
                tile(U + 1, 1, PS[1], taken[1], 2 * j)
                pe.wait_ge(lo_done, U + 2 + 3)
                pe.wait_ge(*at("xsl", j + 1))
                pe.wait_ge(*at("cs_sb", j))
                pe.wait_ge(*at("ada_sb", j))
                for c, ps in enumerate((PS[2], PS[3])):
                    for n, (W, Y) in enumerate(((wh[0], xsH), (wl[0], xsH), (wh[0], xsL))):
                        for h in range(0, SEQ, 512):
                            last = mm(ps[:, h:h + 512], W[:, c, :], Y[:, h:h + 512], start=(n == 0), stop=(n == 2))
                last.then_inc(unit_used, 1)
                pe.wait_ge(unit_used, U + 5)
                pe.sem_inc(ev("ri_ps"), 1)
                tile(U + 3, 1, PS[0], taken[0], 2 * j + 1)
                pe.wait_ge(*at("i_ok", j + 1))
                ada(j, 0)
                tile(U + 4, 0, PS[1], taken[1], 2 * j + 1)
                pe.wait_ge(lo_done, U + 5 + 3)
                pe.wait_ge(*at("r_ok", j + 1))
                product(PS[2], 1, KD, (XH, XL), SEQ).then_inc(unit_used, 1)
                pe.wait_ge(unit_used, U + 8)
                pe.sem_inc(ev("cs_ps"), 1)
                ada(j, 1)

            opening(G1a, "xl_G1")
            tiles(G1a)
            pe.wait_ge(*at("msum_ok", KD))
            pe.wait_ge(*at("cs_sb", KD))
            stat(PS[2], msum_t, "mean_ps")
            tiles(G1b, False)
            pe.wait_ge(*at("var_ok", 1))
            pe.wait_ge(*at("ada_sb", KD))
            stat(PS[3], T[5], "var_ps")
            opening(G2, "xl_G2")
            tiles(G2)
            opening(G3, "xl_G3")
            tiles(G3)
            pe.wait_ge(*at("ssq_ok", 2 * KD + 2))
            stat(PS[2], T[4], "stat1_ps")
            stat(PS[3], T[6], "stat1_ps2")

            def ctx_product(s, w):
                return product(PS[2 + s][:, 0:CTX], w, KD, (XCH, XCL), CTX)

            pe.wait_ge(lo_done, GxG.U + 3)
            pe.wait_ge(*at("xl_c", KD))
            pe.wait_ge(*at("n1_sd1", 1))
            ctx_product(0, GxG.U % 2)
            opening(GxG, "xl_Gx")
            for t in range(2, Q_TILES + 1):
                tile(GxG.U + t, (GxG.U + t) % 2, PS[(GxG.T + t) % 2], taken[(GxG.T + t) % 2], (GxG.T + t) // 2)

            def proj_pairs(first, n, ctx):
                with pe.Fori(0, n // 2) as i:
                    for u in range(2):
                        t = first + u
                        b, w = (GxG.T + t) % 2, (GxG.U + t) % 2
                        if ctx:
                            pe.wait_ge(lo_done, 2 * i + (GxG.U + t + 3))
                            pe.wait_ge(taken[b], i + ((GxG.T + t) // 2 + 1))
                            ctx_product(t % 2, w)
                        tile(2 * i + (GxG.U + t), w, PS[b], taken[b], i + (GxG.T + t) // 2)

            proj_pairs(Q_TILES + 1, KV_TILES, True)
            proj_pairs(Q_TILES + KV_TILES + 1, KD, False)

            DC = [PS[2][:, 512:512 + VW], PS[0][:, 512:512 + VW]]
            DEN = PS[0][:, SEQ - HEADS:SEQ]

            pe.wait_ge(taken[0], (G5.T + 1) // 2 + 1)
            pe.wait_ge(taken[1], G5.T // 2 + 1)
            pe.wait_ge(*at("gate_rows_in", 16))
            for c in range(NCH):
                last = nc.tensor.transpose(PS[1][:, NCOL * c:NCOL * (c + 1)], ROWS[:, P * c:P * (c + 1)], ident[0:NCOL, 0:NCOL])
            last.then_inc(ev("cols_ps"), 1)

            def transposes(k, slot, d, seq):
                m = M[d]["slots"][slot]
                n, x, j, y = indices(k, slot, d)
                pe.wait_ge(*at(f"chunk_in{d}{slot}", 32 * k + 32))
                if isinstance(x, int) and x == 0:
                    pe.wait_ge(*at("cols_sb", 1))
                pe.wait_ge(*at("kw_ok", x))
                for h in range(HEADS):
                    nc.tensor.transpose(PS[0][:, h * P:(h + 1) * P], m["k"][:, h, :], ident[:])
                pe.wait_ge(*at("va_ok", x))
                for h in range(D // P):
                    last = nc.tensor.transpose(PS[1][:, h * P:(h + 1) * P], m["v"][:, h, :], ident[:])
                last.then_inc(ev("t_ps"), 1)
                if seq:
                    if not (isinstance(y, int) and y == 0):
                        pe.wait_ge(*at("p_ok", y))
                    for h in range(HEADS):
                        last = mm(PS[2][:, h * P:(h + 1) * P], m["k"][:, h, :], m["q"][:, h, :], start=True, stop=True)
                    last.then_inc(ev("s_ps"), 1)

            def heads(k, slot, d, seq):
                m = M[d]
                n, x, j, y = indices(k, slot, d)
                pe.wait_ge(*at("va_ok", x + 1))
                pe.wait_ge(*at("kw_ok", x + 1))
                if seq:
                    pe.wait_ge(*at("p_ok", y + 1))
                    pe.wait_ge(*at("q2_ok", y + 1))
                    pe.wait_ge(*at("c_ok", HEADS * x))
                    for h in range(HEADS):
                        mm(DEN[:, h:h + 1], m["p"][:, h, :], m["va"][:, h, DV:VW], start=True, stop=False)
                        last = mm(DEN[:, h:h + 1], m["q2"][:, h, :], m["C"][:, h, DV:VW], start=False, stop=True)
                    last.then_inc(ev("den_ps"), 1)
                    pe.wait_ge(*at("num_free", HEADS * y))
                for h in range(HEADS):
                    if seq:
                        num = PS[3][:, DV * h:DV * (h + 1)]
                        mm(num, m["p"][:, h, :], m["va"][:, h, 0:DV], start=True, stop=False)
                        mm(num, m["q2"][:, h, :], m["C"][:, h, 0:DV], start=False, stop=True).then_inc(ev("num_ps"), 1)
                    if h >= 2:
                        pe.wait_ge(*at("c_ok", HEADS * x + (h - 1)))
                    elif not seq:
                        pe.wait_ge(*at("c_ok", HEADS * x))
                    elif h == 1:
                        pe.wait_ge(*at("rec_ok", y + 1))
                    mm(DC[h % 2], m["kw"][:, h, :], m["va"][:, h, :], start=True, stop=True).then_inc(ev("dc_ps"), 1)

            recurrence(pe, transposes, heads)
            pe.wait_ge(*at("c_ok", HEADS * 2 * NCH))
            pe.wait_ge(*at("kw_ok", 2 * NCH))
            with pe.Fori(0, NT // 2) as i:
                for s in range(2):
                    c = 2 * i + s
                    pe.wait_ge(*at("hn_ok", c + 1))
                    pe.wait_ge(*at(f"yT_free{s}", i))
                    for k in range(KD):
                        last = nc.tensor.transpose(PS[s][:, k * P:(k + 1) * P],
                                                   HN[s][:, k * P:(k + 1) * P], ident[:])
                    last.then_inc(ev("hT_ps"), 1)
            half = SEQ // 2
            pe.wait_ge(lo_done, G5.U + 4)
            for c in range(2):
                pe.wait_ge(*at("xl_r", (c + 1) * NT // 2))
                for s in range(2):
                    if c == 0:
                        pe.wait_ge(*at(f"yT_free{s}", NT // 2))
                    w, ps = (G5.U + s) % 2, PS[(G5.T + s) % 2]
                    for k in range(KD):
                        for n, (W, Y) in enumerate(((wh[w], XH), (wl[w], XH), (wh[w], XL))):
                            last = mm(ps[:, half * c:half * (c + 1)], W[:, k, :], Y[:, k, half * c:half * (c + 1)],
                                      start=(k == 0 and n == 0), stop=(k == KD - 1 and n == 2))
                    if c == 1:
                        last.then_inc(unit_used, 1)
            tiles(G5)
            pe.wait_ge(*at("yssq_ok", KD + 1))
            stat(PS[2], T[4], "stat2_ps")
            pe.wait_ge(*at("xssq_ok", KD))
            stat(PS[3], T[5], "stat3_ps")
            opening(G6, "xl_G6")
            tiles(G6)
            for g, (k0, kc) in enumerate(down):
                opening(G7[g], "xl_G7", kc, k0)
                tiles(G7[g], kc=kc)
            pe.wait_ge(*at("zssq_ok", KD + 1))
            stat(PS[2], T[0], "stat4_ps")
            pe.wait_ge(*at("fin_ok", KD))
            for t in range(NT):
                if t >= 2:
                    pe.wait_ge(*at("fin_sb", t - 1))
                for k in range(KD):
                    last = nc.tensor.transpose(PS[t % 2][:, k * P:(k + 1) * P], B1[:, k, t * P:(t + 1) * P], ident[:])
                last.then_inc(ev("out_ps"), 1)

        @block.vector
        def _(dve):
            step = Chain(dve, "dve_step")
            V = nc.vector

            def log1p(e, s, z, p):
                step.link(V.tensor_scalar(s, e, 2.0, None, ALU.add))
                step.link(V.reciprocal(s, s))
                step.link(V.tensor_tensor(s, e, s, ALU.mult))
                step.link(V.tensor_tensor(z, s, s, ALU.mult))
                n = LOG1P_TERMS
                step.link(V.tensor_scalar(p, z, 1.0 / (2 * n + 1), 1.0 / (2 * n - 1), ALU.mult, ALU.add))
                for t in range(n - 2, -1, -1):
                    step.link(V.tensor_tensor(p, p, z, ALU.mult))
                    step.link(V.tensor_scalar(p, p, 1.0 / (2 * t + 1), None, ALU.add))
                step.link(V.scalar_tensor_tensor(out=p, in0=s, scalar=2.0, in1=p, op0=ALU.mult, op1=ALU.mult))

            V.memset(SCR[:, 0:NST * P], 0.0).then_inc(ev("stage_zero"), 1)
            dve.wait_ge(*at("stage_ps", 1))
            V.tensor_copy(PV[:], PS[2][:, 0:NST * P]).then_inc(ev("pv"), 1)

            def token(i, s):
                dve.wait_ge(*at(f"rms{s}", i + 1))
                step.link(V.reciprocal(small[:, 2, s:s + 1], small[:, 1, s:s + 1]))
                V.tensor_scalar(T[3 + s], T[1 + s], small[:, 2, s:s + 1], None, ALU.mult).then_inc(ev(f"xn_ok{s}"), 1)
                dve.wait_ge(*at(f"xnT_pe{s}", i + 1))

            with dve.Fori(0, NT // 2) as i:
                step.loop(i, 2)
                for s in range(2):
                    token(i, s)
                    V.tensor_copy(B1[:, :, ds(2 * P * i + s * P, P)],
                                  PS[2 + s][:].rearrange("p (k t) -> p k t", k=KD)).then_inc(ev(f"xnT_sb{s}"), 1)
            step.done(NT // 2)
            for s in range(NC):
                token(NT // 2, s)
                dve.wait_ge(*at(f"xT_out{s}", 16 * NT // 2))
                V.tensor_copy(T[5 + s], PS[2 + s][:]).then_inc(ev(f"ctxT_sb{s}"), 1)

            dve.wait_ge(*at("pv", 1))
            dve.wait_ge(*at("lam_e", 1))
            log1p(lam4[:, 1, :], lam4[:, 0, :], lam4[:, 2, :], lam4[:, 3, :])
            step.link(V.tensor_scalar(lam4[:, 0, :], pvec("lam", KD), -1.0, 0.0, ALU.mult, ALU.max))
            step.link(V.tensor_tensor(lam4[:, 0, :], lam4[:, 0, :], lam4[:, 3, :], ALU.add))
            step.sig(V.tensor_scalar(PJ[:, :, TAPS + SHORT + 4], lam4[:, 0, :], -LRU_C, None, ALU.mult))
            step.sig(V.tensor_scalar(PJ[:, :, TAPS + SHORT + 5], lam4[:, 0, :], LRU_C, None, ALU.mult))
            for t0 in range(0, TAPS, P // KD):
                n = min(P // KD, TAPS - t0)
                step.sig(V.tensor_copy(PJ[:, :, t0:t0 + n], pvec(f"dw_w{t0}", n * KD).rearrange("p (t k) -> p k t", k=KD)))
            step.sig(V.tensor_copy(PJ[:, :, TAPS], pvec("dw_b", KD)))
            step.sig(V.tensor_copy(PJ[:, :, TAPS + 1:TAPS + 1 + SHORT], pvec("sc_w", SHORT * KD).rearrange("p (t k) -> p k t", k=KD)))
            for n, name in enumerate(("sc_b", "br", "bi")):
                step.sig(V.tensor_copy(PJ[:, :, TAPS + SHORT + 1 + n], pvec(name, KD)))
            step.wait()
            dve.sem_inc(ev("pj"), 1)
            dve.wait_ge(*at("mod_used", 6))
            step.link(V.tensor_tensor(MOD[:], PS[3][:, 0:6 * KD].rearrange("p (c t) -> p c t", t=2)[:, :, 0], pvec("mod_b", 3 * KD), ALU.add))
            step.sig(V.scalar_tensor_tensor(out=SC[:, 0, :], in0=MOD[:, KD:2 * KD], scalar=1.0, in1=pvec("norm_g", KD), op0=ALU.add, op1=ALU.mult))
            step.sig(V.tensor_scalar(SC[:, 1, :], MOD[:, 2 * KD:3 * KD], 1.0, None, ALU.add))
            step.wait()
            dve.sem_inc(ev("mod_ok"), 1)
            for s in range(2):
                dve.wait_ge(*at(f"xnT_pe{s}", NT // 2 + 1))
            for k in range(KD):
                tmp = T[3 + k % 2]
                step.link(V.tensor_scalar(tmp, B1[:, k, :], SC[:, 0, k:k + 1], MOD[:, k:k + 1], ALU.mult, ALU.add))
                dve.wait_ge(*at("xh_L1", k + 1))
                ins = V.tensor_tensor(XL[:, k, :], tmp, XH[:, k, :].bitcast(F32), ALU.subtract)
                ins.then_inc(ev("xl_L1"), 1)
                dve.wait_ge(*at("xl_L1", k + 1))

            def short_conv(j):
                step.link(V.tensor_copy(PJd[:, TAPS:NJ], PJ[:, ds(j, 1), TAPS:NJ].rearrange("p a n -> p (a n)")))
                dve.wait_ge(*at("lx_sb", j + 1))
                dve.wait_ge(*at("pads_zero", 2))
                dve.wait_ge(*at("bx", j))
                step.link(V.tensor_scalar(xs_t, lxpad[:, 0:SEQ], PJd[:, TAPS + 1:TAPS + 2], PJd[:, TAPS + SHORT + 1:TAPS + SHORT + 2],
                                          ALU.mult, ALU.add))
                for t in range(1, SHORT):
                    ins = V.scalar_tensor_tensor(out=xs_t, in0=lxpad[:, t:t + SEQ], scalar=PJd[:, TAPS + 1 + t:TAPS + 2 + t],
                                                 in1=xs_t, op0=ALU.mult, op1=ALU.add)
                    if t < SHORT - 1:
                        step.link(ins)
                ins.then_inc(ev("xs_ok"), 1)

            def conv(j):
                step.link(V.tensor_copy(PJc[:], PJ[:, ds(j, 1), :].rearrange("p a n -> p (a n)")))
                dve.wait_ge(*at("vpad_ok", j + 1))
                o = B1[:, ds(j, 1), :].rearrange("p a t -> p (a t)")
                step.link(V.tensor_scalar(o, vpad[:, 0:SEQ], PJc[:, 0:1], PJc[:, TAPS:TAPS + 1], ALU.mult, ALU.add))
                for t in range(1, TAPS):
                    ins = V.scalar_tensor_tensor(out=o, in0=vpad[:, t:t + SEQ], scalar=PJc[:, t:t + 1], in1=o, op0=ALU.mult, op1=ALU.add)
                    if t < TAPS - 1:
                        step.link(ins)
                ins.then_inc(ev("conv_ok"), 1)

            def lru(j):
                dve.wait_ge(*at("bx", j + 1))
                dve.wait_ge(*at("a_ok", j + 1))
                step.link(V.tensor_tensor_scan(out=r_t, data0=a_t, data1=i_t, initial=0.0, op0=ALU.mult, op1=ALU.add))
                dve.wait_ge(*at("ls_sb", j + 1))
                V.tensor_tensor(ls_t, r_t, ls_t, ALU.mult).then_inc(ev("lru_y"), 1)
                dve.wait_ge(*at("ada_used", 2 * j + 2))
                for half in range(2):
                    ins = V.tensor_copy(ADA[:, ds(6 * j + 3 * half, 3), :], PS[3][:, 512 * half:512 * half + 6].rearrange("p (c t) -> p c t", t=2))
                ins.then_inc(ev("ada_sb"), 1)

            short_conv(0)
            lru(0)
            with dve.Fori(1, KD) as j:
                n = 1 + (SHORT - 1) + 1 + (TAPS - 1) + 1
                step.loop(j, n)
                step.base -= n
                short_conv(j)
                conv(j - 1)
                lru(j)
            step.done(KD)

            dve.wait_ge(*at("ada_sb", KD))
            step.sig(V.tensor_tensor(ADA[:, :, 0], ADA[:, :, 0], pvec("ada_b_2", 6 * KD), ALU.add))
            step.sig(V.tensor_tensor(ADA[:, 0:2 * KD, 1], ADA[:, 0:2 * KD, 1], pvec("ada_b_2", 2 * KD), ALU.add))
            step.wait()
            stt = V.scalar_tensor_tensor
            step.link(stt(out=SC[:, 4, :], in0=ADA[:, KD:2 * KD, 1], scalar=1.0, in1=pvec("pre_mix_g_2", KD), op0=ALU.add, op1=ALU.mult))
            step.link(stt(out=SC[:, 5, :], in0=ADA[:, KD:2 * KD, 0], scalar=1.0, in1=pvec("pre_mix_g_2", KD), op0=ALU.add, op1=ALU.mult))
            step.link(V.tensor_tensor(SC[:, 5, :], SC[:, 5, :], pvec("final_g", KD), ALU.mult))
            step.link(V.tensor_tensor(SC[:, 6, :], ADA[:, 2 * KD:3 * KD, 0], pvec("post_mix_g_2", KD), ALU.mult))
            step.link(stt(out=SC[:, 7, :], in0=ADA[:, 4 * KD:5 * KD, 0], scalar=1.0, in1=pvec("pre_ffn_g_2", KD), op0=ALU.add, op1=ALU.mult))
            step.link(V.tensor_tensor(SC[:, 8, :], ADA[:, 5 * KD:6 * KD, 0], pvec("post_ffn_g_2", KD), ALU.mult))
            dve.sem_inc(ev("sc_ok"), 1)

            conv(KD - 1)
            dve.wait_ge(*at("mean_ps", 1))
            dve.wait_ge(*at("msum_ok", KD))
            for k in range(KD):
                step.link(V.tensor_tensor(B1[:, k, :], B1[:, k, :], PS[2][:], ALU.subtract))
                if k == 0:
                    step.link(V.tensor_tensor(T[5], B1[:, 0, :], B1[:, 0, :], ALU.mult))
                else:
                    step.link(V.tensor_tensor(T[4], B1[:, k, :], B1[:, k, :], ALU.mult))
                    step.link(V.tensor_tensor(T[5], T[5], T[4], ALU.add))
            dve.sem_inc(ev("var_ok"), 1)
            dve.wait_ge(*at("ln_sd", 1))
            step.link(V.reciprocal(T[6], T[3]))

            def ln_low(k):
                dve.wait_ge(*at("xh_G2", k + 1))
                V.tensor_tensor(XL[:, k, :], T[2 + k % 2], XH[:, k, :].bitcast(F32), ALU.subtract).then_inc(ev("xl_G2"), 1)

            for k in range(KD):
                V.tensor_tensor(B1[:, k, :], B1[:, k, :], T[6], ALU.mult).then_inc(ev("ln_t"), 1)
                if k >= 1:
                    ln_low(k - 1)
            ln_low(KD - 1)

            def tiles(g, evac, n=None):
                with dve.Fori(0, g.n // 2) as i:
                    if n:
                        step.loop(i, 2 * n)
                    for s in range(2):
                        b = (g.T + s) % 2
                        dve.wait_ge(unit_used, 2 * i + (g.U + s + 3))
                        evac(2 * i + s, s, i, PS[b], taken[b])
                if n:
                    step.done(g.n // 2)

            def g2(t, s, i, ps, tk):
                dve.wait_ge(*at(f"cs_in{s}", 16 * i + 16))
                stt(out=B1[:, ds(t, 1), :].rearrange("p a t -> p (a t)"), in0=ps[:], scalar=pcol("pw2_b", t), in1=T[s],
                    op0=ALU.add, op1=ALU.mult).then_inc(ev("yconv_ok"), 1)
                dve.wait_ge(*at("yconv_ok", t + 1))
                dve.sem_inc(tk, 1)
                dve.sem_inc(ev(f"cs_free{s}"), 1)

            dve.wait_ge(*at("xl_G2", KD))
            tiles(G2, g2)
            for k in range(KD):
                dve.wait_ge(*at("xh_G3", k + 1))
                V.tensor_tensor(XL[:, k, :], B1[:, k, :], XH[:, k, :].bitcast(F32), ALU.subtract).then_inc(ev("xl_G3"), 1)

            def g3(t, s, i, ps, tk):
                row = B2[:, ds(t, 1), :].rearrange("p a t -> p (a t)")
                step.link(V.tensor_tensor(T[2], ps[:], row, ALU.add))
                dve.sem_inc(tk, 1)
                dve.wait_ge(*at(f"res_in{s}", 16 * i + 16))
                stt(out=row, in0=T[2], scalar=SC[:, 1, :][:, ds(t, 1)], in1=T[s], op0=ALU.mult, op1=ALU.add).then_inc(ev("x1_ok"), 1)
                dve.wait_ge(*at("x1_ok", t + 1))
                dve.sem_inc(ev(f"res_free{s}"), 1)

            dve.wait_ge(*at("ctx_in", 16))
            for k in range(KD):
                tmp = T[2][:, 0:CTX]
                step.link(V.tensor_scalar(tmp, cn[:, k, :], SC[:, 4, k:k + 1], ADA[:, k, 1:2], ALU.mult, ALU.add))
                dve.wait_ge(*at("xh_c", k + 1))
                V.tensor_tensor(XCL[:, k, :], tmp, XCH[:, k, :].bitcast(F32), ALU.subtract).then_inc(ev("xl_c"), 1)
                dve.wait_ge(*at("xl_c", k + 1))
            tiles(G3, g3, 1)

            dve.wait_ge(*at("n1_sd1", 1))
            step.link(V.reciprocal(T[0], T[3]))
            dve.wait_ge(*at("stat1_ps2", 1))
            step.link(V.tensor_tensor(T[1], PS[3][:], T[0], ALU.mult))
            step.link(V.tensor_tensor(T[1], T[1], T[0], ALU.mult))
            dve.sem_inc(ev("n1_ms"), 1)
            dve.wait_ge(*at("n1_sd2", 1))
            step.link(V.reciprocal(T[2], T[3]))
            step.link(V.tensor_tensor(T[1], T[2], T[0], ALU.mult))

            def x_low(k):
                dve.wait_ge(*at("xh_Gx", k + 1))
                stt(out=XL[:, k, :], in0=T[4 + k % 2], scalar=ADA[:, k, 0:1], in1=XH[:, k, :].bitcast(F32), op0=ALU.add, op1=ALU.subtract).then_inc(ev("xl_Gx"), 1)

            for k in range(KD):
                if k >= 2:
                    dve.wait_ge(*at("xl_Gx", k - 1))
                stt(out=T[4 + k % 2], in0=B2[:, k, :], scalar=SC[:, 5, k:k + 1], in1=T[1], op0=ALU.mult, op1=ALU.mult).then_inc(ev("x2n"), 1)
                dve.wait_ge(*at("x2n", k + 1))
                if k >= 1:
                    x_low(k - 1)
            x_low(KD - 1)
            for k in range(KD):
                stt(out=B2[:, k, :], in0=B2[:, k, :], scalar=pcol("final_g", k), in1=T[0], op0=ALU.mult, op1=ALU.mult).then_inc(ev("x2_sb"), 1)

            dve.wait_ge(*at("f_in", 32))
            dve.wait_ge(*at("f_e", 1))
            log1p(LS[:, 1, :], LS[:, 2, :], LS[:, 3, :], LS[:, 4, :])
            stt(out=LS[:, 0, :], in0=LS[:, 0, :], scalar=0.0, in1=LS[:, 4, :], op0=ALU.min, op1=ALU.subtract).then_inc(ev("lf_sb"), 1)

            def reverse(dst, src):
                for a, b in ((0, CTX), (CTX, ALL)):
                    step.link(V.tensor_copy(dst[32:32 + HEADS, a:b], src[32:32 + HEADS, a:b][:, ::-1]))

            dve.wait_ge(*at("x2_out", 16))
            step.link(V.memset(RZ, 1.0))
            step.link(V.memset(RZ.rearrange("p (c t) -> p c t", t=P)[:, :, 0:1], 0.0))
            dve.wait_ge(*at("rows_in", 64))
            reverse(RI, UN[0])
            reverse(RF, UN[1])
            step.link(V.tensor_tensor_scan(out=RB, data0=RZ, data1=RF, initial=0.0, op0=ALU.mult, op1=ALU.add))
            step.link(V.tensor_tensor(RI, RI, RB, ALU.subtract))
            step.link(V.memset(RZ, 0.0))

            def by_chunk(r):
                return r.rearrange("p (c t) -> p c t", t=P)

            step.link(V.tensor_copy(by_chunk(RZ)[:, 1:NCH, 0], by_chunk(RB)[:, 0:NCH - 1, P - 1]))
            step.link(V.tensor_tensor_scan(out=RM, data0=RZ, data1=RI, initial=0.0, op0=ALU.add, op1=ALU.max))
            step.link(V.memset(mprev[:], 0.0))
            step.link(V.tensor_tensor(mprev[:, 1:NCH], by_chunk(RB)[:, 0:NCH - 1, P - 1], by_chunk(RM)[:, 0:NCH - 1, P - 1], ALU.add))
            step.link(V.scalar_tensor_tensor(out=RF, in0=RB, scalar=-1.0, in1=RM, op0=ALU.mult, op1=ALU.subtract))
            step.link(V.tensor_tensor(by_chunk(RO), by_chunk(RI), by_chunk(RM)[:, :, P - 1:P].to_broadcast([36, NCH, P]), ALU.subtract))
            step.link(V.tensor_tensor(by_chunk(RZ), bc(mprev[:], P), by_chunk(RM), ALU.subtract))
            for q in range(5):
                reverse(UN[q], RQ[q])
            dve.sem_inc(ev("rows_sb"), 1)

            dve.wait_ge(*at("rows_out", 16 * 10))
            for s in range(2):
                dve.wait_ge(*at(f"proj_out{s}", 16 * STORES[s]))
            dve.wait_ge(*at("cols_ps", 1))
            V.tensor_copy(COLS, PS[1][:, 0:NCH * NCOL].rearrange("p (c n) -> p c n", n=NCOL)).then_inc(ev("cols_sb"), 1)
            for d in range(2):
                step.link(V.memset(M[d]["C"], 0.0))
                step.link(V.memset(M[d]["va"][:, :, DV:VW], 1.0))
            dve.sem_inc(ev("rec_zero"), 1)
            dve.wait_ge(*at("cols_sb", 1))
            dve.wait_ge(*at("ecol", 1))
            step.link(V.tensor_scalar(ECOL[:, :, 0:2 * HEADS], ECOL[:, :, 0:2 * HEADS], float(DK) ** 0.5, None, ALU.mult))
            DC = [PS[2][:, 512:512 + VW], PS[0][:, 512:512 + VW]]
            DEN = PS[0][:, SEQ - HEADS:SEQ]

            def col(cols, q, n, d):
                return cols[:, ds(chunk_of(n, d), 1), (2 * q + d) * HEADS:(2 * q + d + 1) * HEADS].rearrange("p a h -> p (a h)")

            def weigh(k, slot, d, seq):
                m, w = M[d]["slots"][slot], M[d]
                n, x, j, y = indices(k, slot, d)
                if seq:
                    dve.wait_ge(*at(f"chunk_in{d}{slot}", 32 * k + 32))
                    step.link(V.tensor_tensor(m["M"], m["M"], bc(col(COLS, 0, n, d), P), ALU.subtract))
                    stt(out=m["M"], in0=m["M"], scalar=0.0, in1=mask[d][:].rearrange("p (o t) -> p o t", o=1).to_broadcast([P, HEADS, P]), op0=ALU.max, op1=ALU.add).then_inc(ev("d_ok"), 1)
                dve.wait_ge(*at("t_ps", x + 1))
                V.tensor_tensor(w["kw"], PS[0][:, 0:HQ].rearrange("p (h n) -> p h n", h=HEADS), bc(col(ECOL, 1, n, d), P), ALU.mult).then_inc(ev("kw_ok"), 1)
                if seq:
                    dve.wait_ge(*at("s_ps", y + 1))
                    dve.wait_ge(*at("e_ok", y + 1))
                    V.tensor_tensor(w["p"], PS[2][:, 0:HQ].rearrange("p (h n) -> p h n", h=HEADS), m["M"], ALU.mult).then_inc(ev("p_ok"), 1)

            def heads(k, slot, d, seq):
                n, x, j, y = indices(k, slot, d)
                if seq:
                    dve.wait_ge(*at("den_ps", y + 1))
                    dve.wait_ge(*at(f"h_sb{d}", j))
                    r = rec_t[d][:]
                    step.link(stt(out=r, in0=DEN, scalar=-1.0, in1=col(ECOL, 0, n, d), op0=ALU.mult, op1=ALU.max))
                    step.link(V.tensor_tensor(r, DEN, r, ALU.max))
                    V.reciprocal(r, r).then_inc(ev("rec_ok"), 1)
                last = P - 1 if d == 0 else 0
                dve.wait_ge(*at("w_ok", x + 1))
                for h in range(HEADS):
                    dve.wait_ge(*at("dc_ps", HEADS * x + (h + 1)))
                    C = M[d]["C"][:, h, :]
                    stt(out=C, in0=C, scalar=M[d]["slots"][slot]["U"][:, h, last:last + 1], in1=DC[h % 2],
                        op0=ALU.mult, op1=ALU.add).then_inc(ev("c_ok"), 1)
                dve.wait_ge(*at("c_ok", HEADS * x + HEADS))
                dve.sem_inc(ev(f"chunk_free{d}"), 1)

            recurrence(dve, weigh, heads, step, 4 * 3)

            def read_sum(c, s, i):
                dve.wait_ge(*at(f"h_in{s}", 32 * i + 32))
                row = B1[:, ds(c, 1), :]
                V.tensor_tensor(row, row, B2[:, ds(c, 1), :], ALU.add).then_inc(ev("hs_ok"), 1)

            def read_norm(c, s, i):
                dve.wait_ge(*at("hrms", c + 1))
                step.link(V.reciprocal(small[:, 5, 0:HEADS], small[:, 4, 0:HEADS]))
                dve.wait_ge(*at("hs_ok", c + 1))
                if not isinstance(c, int) or c >= 2:
                    dve.wait_ge(*at("hT_ps", c + -1))
                V.tensor_tensor(HN[s].rearrange("p (h e) -> p h e", h=HEADS), B1[:, ds(c, 1), :].rearrange("p a (h e) -> p (a h) e", h=HEADS),
                                bc(small[:, 5, 0:HEADS], DV), ALU.mult).then_inc(ev("hn_ok"), 1)

            def read_gate(c, s):
                dve.wait_ge(*at("hT_ps", c + 1))
                dve.wait_ge(*at("gate_ok", c + 1))
                V.tensor_tensor(T[2 + s], PS[s][:], T[s], ALU.mult).then_inc(ev("yT_ok"), 1)
                dve.wait_ge(*at("yT_ok", c + 1))
                dve.sem_inc(ev(f"yT_free{s}"), 1)

            def read_low(c, s):
                dve.wait_ge(*at("xh_r", c + 1))
                V.tensor_tensor(XL[:, :, ds(P * c, P)], T[2 + s].rearrange("p (k t) -> p k t", k=KD),
                                XH[:, :, ds(P * c, P)].bitcast(F32), ALU.subtract).then_inc(ev("xl_r"), 1)
                dve.wait_ge(*at("xl_r", c + 1))

            read_sum(0, 0, 0)
            read_norm(0, 0, 0)
            read_sum(1, 1, 0)
            read_norm(1, 1, 0)
            with dve.Fori(0, NT // 2 - 1) as i:
                step.loop(i, 2)
                for s in range(2):
                    read_gate(2 * i + s, s)
                    read_sum(2 * i + s + 2, s, i + 1)
                    read_low(2 * i + s, s)
                    read_norm(2 * i + s + 2, s, i + 1)
            step.done(NT // 2 - 1)
            read_gate(NT - 2, 0)
            read_gate(NT - 1, 1)
            read_low(NT - 2, 0)
            read_low(NT - 1, 1)

            dve.wait_ge(*at("n2_sd", 1))
            step.link(V.reciprocal(T[6], T[6]))
            dve.wait_ge(*at("xssq_zero", 1))
            for k in range(KD):
                dve.wait_ge(*at("y_sb", KD))
                step.link(V.tensor_tensor(B1[:, k, :], B1[:, k, :], T[6], ALU.mult))
                dve.wait_ge(*at(f"x2_in{k % 2}", 16 * (k // 2 + 1)))
                stt(out=B2[:, k, :], in0=B1[:, k, :], scalar=SC[:, 6, k:k + 1], in1=T[k % 2], op0=ALU.mult, op1=ALU.add).then_inc(ev("x3_sb"), 1)
                dve.wait_ge(*at("xsq_ok", k + 1))
                V.tensor_tensor(T[5], T[5], T[2 + k % 2], ALU.add).then_inc(ev("xssq_ok"), 1)
                dve.wait_ge(*at("xssq_ok", k + 1))
            dve.sem_inc(ev("n2_done"), 1)
            dve.wait_ge(*at("n3_sd", 1))
            step.link(V.reciprocal(T[6], T[6]))

            def h2_low(k):
                dve.wait_ge(*at("xh_G6", k + 1))
                stt(out=XL[:, k, :], in0=T[2 + k % 2], scalar=ADA[:, 3 * KD + k, 0:1], in1=XH[:, k, :].bitcast(F32),
                    op0=ALU.add, op1=ALU.subtract).then_inc(ev("xl_G6"), 1)

            for k in range(KD):
                if k >= 2:
                    dve.wait_ge(*at("xl_G6", k - 1))
                stt(out=T[2 + k % 2], in0=B2[:, k, :], scalar=SC[:, 7, k:k + 1], in1=T[6], op0=ALU.mult, op1=ALU.mult).then_inc(ev("h2_t"), 1)
                dve.wait_ge(*at("h2_t", k + 1))
                if k >= 1:
                    h2_low(k - 1)
            h2_low(KD - 1)
            dve.wait_ge(*at("xl_G6", KD))

            def grid(t):
                return t.rearrange("p (r w) -> p r w", w=GRID)

            with dve.Fori(0, KF) as j:
                step.loop(j, 1)
                dve.wait_ge(*at("g_sb", 2 * j + 2))
                step.link(stt(out=grid(T[1])[:, :, 1:GRID], in0=grid(T[0])[:, :, 0:GRID - 1], scalar=pcol("ffn_conv_w", j),
                              in1=grid(T[1])[:, :, 1:GRID], op0=ALU.mult, op1=ALU.add))
                stt(out=grid(T[1])[:, :, 0:GRID - 1], in0=grid(T[0])[:, :, 1:GRID], scalar=pcol("ffn_conv_w", j + 2 * KF),
                    in1=grid(T[1])[:, :, 0:GRID - 1], op0=ALU.mult, op1=ALU.add).then_inc(ev("ffn_conv"), 1)
                b = (G6.T + 1) % 2
                dve.wait_ge(unit_used, 2 * j + (G6.U + 4))
                dve.wait_ge(*at("ffn_silu", j + 1))
                dve.wait_ge(*at("act_out", 16 * j))
                V.tensor_tensor(T[2], PS[b][:], T[3], ALU.mult).then_inc(ev("act_sb"), 1)
                dve.wait_ge(*at("act_sb", j + 1))
                dve.sem_inc(taken[b], 1)
            step.done(KF)

            n = 0
            for g, (k0, kc) in enumerate(down):
                for k in range(kc):
                    dve.wait_ge(*at("xh_G7", n + 1))
                    V.tensor_tensor(XL[:, k, :], T[4 + n % 2], XH[:, k, :].bitcast(F32), ALU.subtract).then_inc(ev("xl_G7"), 1)
                    n += 1

                def down_evac(t, s, i, ps, tk, g=g):
                    row = B1[:, ds(t, 1), :].rearrange("p a t -> p (a t)")
                    ins = V.tensor_copy(row, ps[:]) if g == 0 else V.tensor_tensor(row, ps[:], row, ALU.add)
                    ins.then_inc(ev("z_ok"), 1)
                    dve.wait_ge(*at("z_ok", t + (g * KD + 1)))
                    dve.sem_inc(tk, 1)

                tiles(G7[g], down_evac)
            dve.wait_ge(*at("n4_sd", 1))
            step.link(V.reciprocal(T[6], T[6]))
            for k in range(KD):
                step.link(V.tensor_tensor(B1[:, k, :], B1[:, k, :], T[6], ALU.mult))
                stt(out=B1[:, k, :], in0=B1[:, k, :], scalar=SC[:, 8, k:k + 1], in1=B2[:, k, :], op0=ALU.mult, op1=ALU.add).then_inc(ev("fin_ok"), 1)


_INS = ["x", "c", "norm_g", "mod_w", "mod_b", "w_in", "dw_w", "dw_b", "cln_g", "cln_b", "pw2_w", "pw2_b", "sc_w", "sc_b",
        "wr", "br", "wi", "bi", "lam", "w_out", "final_g", "c_2", "ctx_2", "c_ctx_2", "ada_w_2", "ada_b_2", "pre_mix_g_2",
        "post_mix_g_2", "pre_ffn_g_2", "post_ffn_g_2", "ffn_up_w_2", "ffn_conv_w_2", "ffn_conv_b_2", "ffn_down_w_2",
        "m_in_w_2", "m_in_b_2", "m_norm_g_2", "m_out_w_2"]


def kernel(**inputs):
    import numpy as _np
    import concourse.bacc as _bacc
    from concourse import mybir as _mybir
    from concourse.bass_utils import run_bass_kernel_spmd as _run

    nc = _bacc.Bacc("TRN2", target_bir_lowering=False, num_devices=1)
    arrays, args = {}, {}
    for name in _INS:
        a = _np.ascontiguousarray(inputs[name])
        arrays[f"in_{name}"] = a
        args[name] = nc.dram_tensor(f"in_{name}", a.shape, _mybir.dt.from_np(a.dtype), kind="ExternalInput").ap()
    shape = inputs["x"].shape
    out = nc.dram_tensor("out_dram", shape, _mybir.dt.float32, kind="ExternalOutput").ap()
    block_pair_kernel(nc, args, out)
    r = _run(nc, [arrays], core_ids=[0])
    return r.results[0]["out_dram"]
```

```python
from contextlib import ExitStack

import concourse.bass as bass
from concourse import mybir

F32 = mybir.dt.float32
F32R = mybir.dt.float32r
ALU = mybir.AluOpType
ACT = mybir.ActivationFunctionType
ds = bass.ds

P = 128
EPS = 1e-6
BIG = 1e30
GRID = 64


def block_pair_kernel(nc, A, out):
    x, ctx = A["x"][0], A["ctx_2"][0]
    SEQ, D = x.shape
    CTX = ctx.shape[0]
    KD = D // P
    NT = SEQ // P
    NC = CTX // P
    TAPS = A["dw_w"].shape[1]
    SHORT = A["sc_w"].shape[1]
    FFN = A["ffn_down_w_2"].shape[1]
    KF = FFN // P
    HEADS, DK, DV = 4, P, D // 4
    ALL = CTX + SEQ
    NCH = ALL // P
    HQ = HEADS * DK
    MP = A["m_in_w_2"].shape[2]
    GATE_ROW = MP - 4 * HEADS
    LRU_C = 8.0
    LOG1P_TERMS = 9
    VW = DV + 1

    mod_w, w_in, pw2_w, w_out = A["mod_w"][0], A["w_in"][0], A["pw2_w"][0], A["w_out"][0]
    ada_w, m_in_w, m_out_w = A["ada_w_2"][0], A["m_in_w_2"][0], A["m_out_w_2"][0]
    up_w, down_w = A["ffn_up_w_2"][0], A["ffn_down_w_2"][0]

    def dram(name, shape):
        return nc.dram_tensor(name, shape, F32).ap()

    xT_d = dram("xT_d", [D, SEQ])
    ctxT_d = dram("ctxT_d", [D, CTX])
    lru_d = dram("lru_d", [D, SEQ])
    cs_d = dram("cs_d", [D, SEQ])
    x2_d = dram("x2_d", [D, SEQ])
    proj_d = dram("proj_d", [MP, ALL])
    lf_d = dram("lf_d", [2 * HEADS, ALL])
    rows_d = dram("rows_d", [5 * 2 * HEADS, ALL])
    h_d = dram("h_d", [2, SEQ, D])
    act_d = dram("act_d", [FFN, SEQ])

    stage_rows, col, fill = [], {}, [0]

    def place(name, src, n):
        if fill[0] % P + n > P:
            fill[0] += P - fill[0] % P
        col[name] = fill[0]
        stage_rows.append((fill[0] // P, fill[0] % P, n, src))
        fill[0] += n

    def vec(a):
        return a.rearrange("(k p) -> k p", p=P)

    for name in ("norm_g", "mod_b", "dw_b", "cln_g", "cln_b", "pw2_b", "sc_b", "br", "bi", "lam"):
        place(name, vec(A[name][0]), A[name].shape[1] // P)
    place("c", vec(A["c"][0]), KD)
    place("sc_w", A["sc_w"][0].rearrange("t (k p) -> (t k) p", p=P), SHORT * KD)
    for name in ("pre_mix_g_2", "post_mix_g_2", "pre_ffn_g_2", "post_ffn_g_2", "m_norm_g_2", "ffn_conv_b_2", "ada_b_2"):
        place(name, vec(A[name][0]), A[name].shape[1] // P)
    place("c_2", vec(A["c_2"][0]), KD)
    place("final_g", vec(A["final_g"]), KD)
    dw = A["dw_w"][0].rearrange("t (k p) -> (t k) p", p=P)
    for t0 in range(0, TAPS, P // KD):
        n = min(P // KD, TAPS - t0) * KD
        place(f"dw_w{t0}", dw[t0 * KD:t0 * KD + n, :], n)
    place("ffn_conv_w", A["ffn_conv_w_2"][0].rearrange("t (k p) -> (t k) p", p=P), 3 * KF)
    place("m_in_b", vec(A["m_in_b_2"][0][0:GATE_ROW]), GATE_ROW // P)
    place("gate_b", vec(A["m_in_b_2"][0][MP - P:MP]), 1)
    place("c_ctx", vec(A["c_ctx_2"]), KD)
    NST = (fill[0] + P - 1) // P

    with ExitStack() as ctxs:
        def sb(name, shape, dt=F32):
            return ctxs.enter_context(nc.sbuf_tensor(name, shape, dt))

        def sem(name):
            return ctxs.enter_context(nc.semaphore(name))

        sems = {}

        shared = {}

        def share(total, *events):
            at_count = 0
            for name, n in events:
                shared[name] = (total, at_count)
                at_count += n

        share("x_high", ("xh_L1", KD), ("xh_G1", KD), ("xh_G2", KD), ("xh_G3", KD), ("xh_c", KD), ("xh_Gx", KD), ("xh_r", NT), ("xh_G6", KD), ("xh_G7", KF))
        share("x_low", ("xl_L1", KD), ("xl_G1", KD), ("xl_G2", KD), ("xl_G3", KD), ("xl_c", KD), ("xl_Gx", KD), ("xl_r", NT), ("xl_G6", KD), ("xl_G7", KF))
        share("dve_stage", *((n, 1) for n in ("stage_zero", "pv", "diag", "ctxn", "pj", "mod_ok", "sc_ok", "var_ok", "ln_diag", "n1_ms", "lf_sb", "rows_sb", "rec_zero", "n2_diag", "n2_done", "n4_diag")))
        share("pe_stage", *((n, 1) for n in ("stage_ps", "r_ps", "ctxT_ps", "mean_ps", "var_ps", "ln_r", "stat1_ps", "stat1_ps2", "stat2_ps", "n2_r", "stat4_ps", "n4_r")))
        share("act_stage", *((n, 1) for n in ("rms", "lam_e", "ln_sd", "n1_sd2", "n1_sd1", "f_e", "n2_sd", "n3_sd", "n4_sd")))
        for a, b, n in (("xsh", "w_ok", KD), ("xsl", "va_ok", KD), ("i_ok", "kw_ok", KD), ("r_ok", "t_ps", KD), ("th_ok", "e_ok", KD),
                        ("m2", "q2_ok", KD), ("mult_ok", "d_ok", KD), ("lx_sb", "s_ps", KD), ("ls_sb", "den_ps", KD), ("a_ok", "num_ps", KD),
                        ("xT_sb", "hs_ok", NT)):
            share(f"{a}_then_{b}", (a, n), (b, 0))
        share("pool_stage", ("msum_zero", 1), ("pads_zero", 2))

        def ev(name):
            name = shared.get(name, (name, 0))[0]
            if name not in sems:
                sems[name] = sem(name)
            return sems[name]

        BEGIN_AT_ONE = ("ada_used", "ada_summed", "cs_free0", "cs_free1", "res_free0", "res_free1", "msum_ok", "xs_ok",
                        "ri_ps", "lru_out", "lru_y", "vpad_ok", "cs_out", "proj_out0", "proj_out1", "h_out0", "h_out1",
                        "ffn_conv", "ffn_silu", "act_sb", 
                        "cs_sb", "ada_sb", "p_ok", "num_free", "yT_free0", "yT_free1", "low_sb0", "low_sb1", "act_out", "bx", "h_sb0", "h_sb1")

        def at(name, n):
            return ev(name), n + (1 if name in BEGIN_AT_ONE else shared.get(name, (name, 0))[1])

        XH = sb("XH", [P, KD, SEQ], F32R)
        XL = sb("XL", [P, KD, SEQ], F32R)
        XCH = sb("XCH", [P, KD, CTX], F32R)
        XCL = sb("XCL", [P, KD, CTX], F32R)
        raw = [sb(f"raw{s}", [P, KD, P]) for s in range(2)]
        wh = [sb(f"wh{s}", [P, KD, P], F32R) for s in range(2)]
        wl = [sb(f"wl{s}", [P, KD, P], F32R) for s in range(2)]
        B1 = sb("B1", [P, KD, SEQ])
        B2 = sb("B2", [P, KD, SEQ])
        VP = SEQ + 32
        LP = SEQ + 4
        SCR = sb("SCR", [P, VP + LP + 5 * SEQ])
        PV = sb("PV", [P, NST * P])
        NJ = TAPS + SHORT + 6
        PJ = sb("PJ", [P, KD, NJ])
        ident = sb("ident", [P, P])
        avg = sb("avg", [P, P])
        mask = [sb(f"mask{d}", [P, P]) for d in range(2)]
        CA = sb("CA", [P, KD, 4])
        MOD = sb("MOD", [P, 3 * KD])
        ADA = sb("ADA", [P, 6 * KD, 2])
        SC = sb("SC", [P, 9, KD])
        eps = sb("eps", [P, 1])
        ones = sb("ones", [P, 1])
        small = sb("small", [P, 6, 16])
        mprev = sb("mprev", [36, NCH])
        PJc = sb("PJc", [P, NJ])
        PJd = sb("PJd", [P, NJ])
        PJa = sb("PJa", [P, NJ])
        lam4 = sb("lam4", [P, 4, KD])
        rec_t = [sb(f"rec{d}", [P, HEADS]) for d in range(2)]
        PS = [ctxs.enter_context(nc.psum_tensor(f"PS{b}", [P, SEQ], F32)) for b in range(4)]

        vpad = SCR[:, 0:VP]
        lxpad = SCR[:, VP:VP + LP]
        T = [SCR[:, 0:SEQ], SCR[:, VP:VP + SEQ]] + [SCR[:, VP + LP + SEQ * n:VP + LP + SEQ * (n + 1)] for n in range(5)]
        LS = T[0][:, 0:5 * 2 * HEADS * ALL // P].rearrange("p (q w) -> p q w", q=5)
        b2 = B2[:].rearrange("p k t -> p (k t)")
        b1 = B1[:].rearrange("p k t -> p (k t)")

        ls_t, sg_t, vc_t, th_t, cs_t = (b2[:, n * D:(n + 1) * D] for n in range(3, 8))
        ada_t = b2[:, 0:3 * D].rearrange("p (k n) -> p k n", k=KD)
        HALF = 3 * P
        ada_acc = B1[:, KD - 1, 0:2 * HALF].rearrange("p (v n) -> p v n", v=2)
        CTX_STEPS = (2 * KD + 5) // 6
        xsH = XCH[:].rearrange("p k t -> p (k t)")[:, 0:SEQ]
        xsL = XCL[:].rearrange("p k t -> p (k t)")[:, 0:SEQ]
        PIECE = 4 * P
        PIECES = 3 * D // PIECE
        mod_in = [B1[:, 4 * h:4 * h + 4, :].rearrange("p a (b n) -> p (a b) n", n=PIECE) for h in range(2)]
        MOD_PS = PS[2][:, SEQ // 2:SEQ // 2 + 3 * KD]
        cn = B1[:, 4:6, :].rearrange("p a (b t) -> p (a b) t", t=CTX)
        xs_t, r_t, i_t, a_t, msum_t = T[2:7]
        ctx_t = SCR[:, VP + LP + 3 * SEQ:].rearrange("p (c d) -> p c d", c=NC)
        HN = T[4:6]

        def pcol(name, k=0):
            return PV[:, ds(k + col[name], 1)]

        def pvec(name, n):
            return PV[:, col[name]:col[name] + n]

        RF, RI, RB, RM, RZ, RO = (b2[0:36, ALL * n:ALL * (n + 1)] for n in range(6))
        UN = [b1[0:36, ALL * n:ALL * (n + 1)] for n in range(2, 6)] + [RB]
        stage = [b1[:, ALL * n:ALL * (n + 1)] for n in range(2)]
        RQ = [RI, RF, RO, RZ, RM]

        M = []
        for d, flat in enumerate((b1, b2)):
            m = {}

            def take(buf, off, *parts):
                for name, n, k in parts:
                    m[name] = buf[:, off:off + n].rearrange("p (k n) -> p k n", k=k)
                    off += n
                return off

            loaded = [("q", HQ, HEADS), ("k", HQ, HEADS), ("v", D, D // P), ("U", HQ, HEADS), ("M", HQ, HEADS)]
            n_loaded = sum(n for _, n, _ in loaded)
            m["slots"] = []
            for slot, (buf, off) in enumerate(((flat, 0), (SCR, d * n_loaded))):
                end = take(buf, off, *loaded)
                m["slots"].append({name: m[name] for name, _, _ in loaded} | {
                    "qkv": buf[:, off:off + 2 * HQ + D].rearrange("p (k n) -> p k n", n=P),
                    "kv": buf[:, off + HQ:off + 2 * HQ + D].rearrange("p (k n) -> p k n", n=P),
                    "UM": buf[:, off + 2 * HQ + D:end].rearrange("p (k n) -> p k n", n=P)})
            end = take(flat, n_loaded, ("kw", HQ, HEADS), ("va", HEADS * VW, HEADS), ("q2", HQ, HEADS), ("p", HQ, HEADS),
                       ("h", D, HEADS), ("C", HEADS * VW, HEADS))
            M.append(m)
        NCOL = 3 * 2 * HEADS
        COLS = b1[:, end:end + NCH * NCOL].rearrange("p (c n) -> p c n", n=NCOL)
        ECOL = b2[:, end:end + NCH * 4 * HEADS].rearrange("p (c n) -> p c n", n=4 * HEADS)
        ROWS = b2[0:NCOL, n_loaded + HQ:n_loaded + HQ + ALL]

        def chunk_of(n, d):
            if isinstance(n, int):
                return n if d == 0 else (NC - 1 - n if n < NC else NC + NCH - 1 - n)
            return n if d == 0 else n * -1 + (NC + NCH - 1)

        landed = [sem("landed0"), sem("landed1")]
        hi_done, lo_done, unit_used = sem("hi_done"), sem("lo_done"), sem("unit_used")
        taken = [sem("psum_taken0"), sem("psum_taken1")]
        gates_in = ev("gate_weights_landed")

        class Product:
            unit, tile = 0, 0

            def __init__(self, n, units=None, tiles=None):
                self.U, self.T, self.n = Product.unit, Product.tile, n
                Product.unit += units or n
                Product.tile += tiles or n
                self.end = Product.unit + 2

        L1 = Product(KD, 6 * KD, 4 * KD)
        G1a, G1b = Product(KD // 2), Product(KD // 2)
        G2, G3 = Product(KD), Product(KD)
        GxG, Gx = Product(1), Product(GATE_ROW // P)
        Q_TILES, KV_TILES = HQ // P, (HQ + D) // P
        PAIR = GxG.T % 2
        STORES = [(1 + Gx.n - n + 1) // 2 for n in range(2)]
        G5 = Product(KD)
        G6 = Product(2 * KF)
        down = [(k, min(KD, KF - k)) for k in range(0, KF, KD)]
        G7 = [Product(KD) for _ in down]
        LAST_UNIT = Product.unit

        def cols_of(w, k0, kc, c):
            return w[k0 * P:(k0 + kc) * P, :].rearrange("(k p) n -> p k n", p=P)[:, :, ds(c, P)]

        class Chain:

            def __init__(self, eng, name):
                self.eng, self.sem, self.base, self.i, self.n, self.k = eng, ev(name), 0, 0, 0, 0

            def loop(self, i, n):
                self.base, self.i, self.n, self.k = self.base + self.k, i, n, 0

            def done(self, times):
                assert self.k == self.n, (self.k, self.n)
                self.base, self.i, self.n, self.k = self.base + self.n * times, 0, 0, 0

            def sig(self, ins):
                self.k += 1
                ins.then_inc(self.sem, 1)

            def wait(self, back=0):
                self.eng.wait_ge(self.sem, self.i * self.n + (self.base + self.k - back))

            def link(self, ins):
                self.sig(ins)
                self.wait()

        def bc(a, n):
            return a.rearrange("p (h o) -> p h o", o=1).to_broadcast([a.shape[0], a.shape[1], n])

        def recurrence(eng, prepare, heads, step=None, steps=0):
            def pair(k, at4, seq, seq_next, more=True):
                nxt = at4 + 1
                if more:
                    prepare(k + nxt // 4, nxt % 4 // 2, nxt % 2, seq_next)
                heads(k, at4 // 2, at4 % 2, seq)

            assert NC == 2 and NT % 2 == 0
            prepare(0, 0, 0, False)
            for u in range(4):
                pair(0, u, False, u == 3)
            with eng.Fori(0, NT // 2 - 1) as i:
                if step:
                    step.loop(i, steps)
                for u in range(4):
                    pair(i + 1, u, True, True)
            if step:
                step.done(NT // 2 - 1)
            for u in range(4):
                pair(NCH // 2 - 1, u, True, True, u < 3)

        def indices(k, slot, d):
            n, x = 2 * k + slot, 4 * k + (2 * slot + d)
            return n, x, n + -NC, x + -2 * NC

        block = ctxs.enter_context(nc.Block())

        @block.sync
        def _(sp):
            def unit(U, slot, src, kc=KD, counted=False):
                sp.wait_ge(lo_done, U + 1)
                if counted:
                    sp.sem_inc(ev("sp_passed"), 1)
                sp.dma_start(raw[slot][:, 0:kc, :], src).then_inc(landed[slot], 16)

            for name in BEGIN_AT_ONE:
                sp.sem_inc(ev(name), 1)
            sp.wait_ge(*at("stage_zero", 1))
            for t, r, n, src in stage_rows:
                sp.dma_start(SCR[r:r + n, t * P:(t + 1) * P], src).then_inc(ev("stage_in"), 16)

            sp.wait_ge(*at("xT_ps", NT))
            sp.wait_ge(*at("rms", 1))
            for q in range(PIECES):
                if q >= 2:
                    sp.wait_ge(*at("mod_sum", q - 1))
                sp.dma_start(mod_in[q % 2], mod_w.rearrange("(k p) n -> p k n", p=P)[:, :, PIECE * q:PIECE * (q + 1)]).then_inc(ev(f"mod_in{q % 2}"), 16)
                if q == 1:
                    sp.wait_ge(*at("xT_sb", NT))
                    sp.dma_start(xT_d.rearrange("(k p) t -> p k t", p=P), B2[:]).then_inc(ev("xT_out"), 16)

            def l1_unit(j, pos):
                U = 6 * j + pos
                slot = pos % 2
                if pos == 2:
                    sp.wait_ge(lo_done, U + 1)
                    sp.dma_start(raw[0][:, 0:1, :], A["wr"][0][ds(j, 1)].rearrange("h d e -> d h e")).then_inc(landed[0], 16)
                    sp.dma_start(raw[0][:, 1:2, :], A["wi"][0][ds(j, 1)].rearrange("h d e -> d h e")).then_inc(gates_in, 16)
                else:
                    group = {0: 3, 1: 4, 3: 1, 4: 0, 5: 2}[pos]
                    unit(U, slot, cols_of(w_in, 0, KD, group * D + P * j), counted=group == 0)

            def ada_load(j, half):
                sp.wait_ge(*at("ada_summed", 2 * j + half))
                sp.dma_start(b2[:, 0:3 * D].rearrange("p (k n) -> p k n", k=KD),
                             ada_w.rearrange("(k p) n -> p k n", p=P)[:, :, ds(6 * P * j + 3 * P * half, 3 * P)]).then_inc(ev("ada_in"), 16)

            def l1_store(j):
                sp.wait_ge(*at("lru_y", j + 1))
                sp.dma_start(lru_d[ds(P * j, P), :], ls_t).then_inc(ev("lru_out"), 16)
                sp.wait_ge(*at("cs_sb", j + 1))
                sp.dma_start(cs_d[ds(P * j, P), :], cs_t).then_inc(ev("cs_out"), 16)

            def l1_loads(j, stores):
                l1_unit(j, 0)
                l1_unit(j, 1)
                if stores:
                    l1_store(j - 1)
                else:
                    sp.wait_ge(*at("ctxT_sb", 1))
                    sp.dma_start(ctxT_d.rearrange("(k p) t -> p k t", p=P),
                                 SCR[:, VP:VP + 2 * SEQ].rearrange("p (k t) -> p k t", k=KD)).then_inc(ev("ctxT_out"), 16)
                    sp.wait_ge(*at("xl_L1", KD))
                    sp.wait_ge(*at("xT_out", 16))
                l1_unit(j, 2)
                ada_load(j, 0)
                for pos in range(3, 6):
                    l1_unit(j, pos)
                ada_load(j, 1)

            l1_loads(0, False)
            with sp.Fori(1, KD) as j:
                l1_loads(j, True)
            for u in range(2):
                unit(G1a.U + u, u, cols_of(w_out, KD, KD, u * P))
            l1_store(KD - 1)

            for k in range(KD):
                sp.wait_ge(*at("lru_out", 16 * (k + 1)))
                if k >= 2:
                    sp.wait_ge(*at("xl_G1", k - 1))
                sp.dma_start(T[2 + k % 2], lru_d[k * P:(k + 1) * P, :]).then_inc(ev(f"lru_in{k % 2}"), 16)
            with sp.Fori(0, KD // 2 - 1) as i:
                for s in range(2):
                    unit(G1a.U + 2 + 2 * i + s, s, cols_of(w_out, KD, KD, 2 * P * i + (2 + s) * P))

            def cs_load(t, s, i):
                sp.wait_ge(*at(f"cs_free{s}", i))
                sp.dma_start(T[s], cs_d[ds(P * t, P), :]).then_inc(ev(f"cs_in{s}"), 16)

            sp.wait_ge(*at("cs_out", 16 * KD))
            sp.wait_ge(*at("conv_ok", KD))
            with sp.Fori(0, KD // 2) as i:
                for s in range(2):
                    unit(G2.U + 2 * i + s, s, cols_of(pw2_w, 0, KD, 2 * P * i + s * P))
                    cs_load(2 * i + s, s, i)

            for s in range(2):
                unit(G3.U + s, s, cols_of(w_out, 0, KD, s * P))
            sp.wait_ge(*at("ctxT_out", 16))
            sp.wait_ge(*at("xl_G3", KD))
            sp.dma_start(cn, ctxT_d.rearrange("(k p) t -> p k t", p=P)).then_inc(ev("ctx_in"), 16)
            for s in range(2):
                sp.wait_ge(*at(f"cs_free{s}", KD // 2))
                sp.wait_ge(*at("xT_out", 16))
                sp.dma_start(T[s], xT_d[s * P:(s + 1) * P, :]).then_inc(ev(f"res_in{s}"), 16)
            with sp.Fori(0, KD // 2 - 1) as i:
                for s in range(2):
                    unit(G3.U + 2 + 2 * i + s, s, cols_of(w_out, 0, KD, 2 * P * i + (2 + s) * P))
                    sp.wait_ge(*at(f"res_free{s}", i + 1))
                    sp.dma_start(T[s], xT_d[ds(2 * P * i + (2 + s) * P, P), :]).then_inc(ev(f"res_in{s}"), 16)

            def proj_unit(t, s):
                unit(GxG.U + t, (GxG.U + s) % 2, cols_of(m_in_w, 0, KD, MP - P if isinstance(t, int) and t == 0 else t * P + -P))

            def proj_store(t, s, ctx=False):
                sp.wait_ge(*at("proj_sb", t + 1))
                c0 = 0 if ctx else CTX
                dst, src = (proj_d[GATE_ROW:MP, c0:ALL], stage[s][P - 4 * HEADS:P, c0:ALL]) if isinstance(t, int) and t == 0 else \
                    (proj_d[ds(t * P + -P, P), c0:ALL], stage[s][:, c0:ALL])
                sp.dma_start(dst, src).then_inc(ev(f"proj_out{s}"), 16)

            for t in range(4):
                proj_unit(t, t % 2)
            proj_store(0, 0, True)
            for k in range(0, KD, 2):
                sp.wait_ge(*at("x2_sb", k + 2))
                sp.dma_start(x2_d.rearrange("(k p) t -> p k t", p=P)[:, k:k + 2, :], B2[:, k:k + 2, :]).then_inc(ev("x2_out"), 16)

            W = ALL // 16
            sp.wait_ge(*at("proj_out0", 16))
            for d in range(2):
                r = GATE_ROW + (2 * d + 1) * HEADS
                sp.dma_start(LS[64 * d:64 * d + 64, 0, :], proj_d[r:r + HEADS, :].rearrange("h (a w) -> (h a) w", w=W)).then_inc(ev("f_in"), 16)
            sp.wait_ge(*at("x2_out", 16 * KD // 2))
            sp.dma_start(RI[0:HEADS, :], proj_d[GATE_ROW:GATE_ROW + HEADS, :]).then_inc(ev("rows_in"), 16)
            sp.dma_start(UN[0][32:32 + HEADS, :], proj_d[GATE_ROW + 2 * HEADS:GATE_ROW + 3 * HEADS, :]).then_inc(ev("rows_in"), 16)
            proj_store(1, 1)
            for t in range(4, 6):
                proj_unit(t, t % 2)
                proj_store(t - 2, t % 2)
            sp.wait_ge(*at("lf_sb", 1))
            sp.dma_start(lf_d.rearrange("h (a w) -> (h a) w", w=W), LS[:, 0, :]).then_inc(ev("lf_out"), 16)
            sp.wait_ge(*at("lf_out", 16))
            sp.dma_start(RF[0:HEADS, :], lf_d[0:HEADS, :]).then_inc(ev("rows_in"), 16)
            sp.dma_start(UN[1][32:32 + HEADS, :], lf_d[HEADS:2 * HEADS, :]).then_inc(ev("rows_in"), 16)
            for t in range(6, Q_TILES + 3):
                proj_unit(t, t % 2)
                proj_store(t - 2, t % 2)

            first = Q_TILES + 1
            with sp.Fori(0, KV_TILES // 2) as i:
                for u in range(2):
                    s = (first + u) % 2
                    proj_unit(2 * i + (first + u + 2), s)
                    proj_store(2 * i + (first + u), s, True)
            first += KV_TILES
            with sp.Fori(0, KD // 2 - 1) as i:
                for u in range(2):
                    s = (first + u) % 2
                    proj_unit(2 * i + (first + u + 2), s)
                    proj_store(2 * i + (first + u), s)
            sp.wait_ge(*at("rows_sb", 1))
            for q, (f, b) in enumerate(zip(RQ, UN)):
                for d, r in enumerate((f[0:HEADS, :], b[32:32 + HEADS, :])):
                    row = (2 * q + d) * HEADS if q < 3 else NCOL + (2 * d + q - 3) * HEADS
                    sp.dma_start(rows_d[row:row + HEADS, :], r).then_inc(ev("rows_out"), 16)
            for t in range(Gx.n - 1, Gx.n + 1):
                unit(GxG.U + t + 2, (GxG.U + t) % 2, cols_of(m_out_w, 0, KD, (t - Gx.n + 1) * P))
                proj_store(t, t % 2)
            sp.wait_ge(*at("rows_out", 16 * 10))
            for s in range(2):
                sp.wait_ge(*at(f"proj_out{s}", 16 * STORES[s]))

            sp.dma_start(ROWS, rows_d[0:NCOL, :]).then_inc(ev("gate_rows_in"), 16)

            def chunk_load(n, d, slot, outputs=True):
                m = M[d]["slots"][slot]
                if not isinstance(n, int) or n >= 2:
                    sp.wait_ge(*at(f"chunk_free{d}", n + -1))
                c = chunk_of(n, d) * P
                r0 = 0 if outputs else HQ
                sp.dma_start(m["qkv" if outputs else "kv"],
                             proj_d[r0:2 * HQ + D, :].rearrange("(h p) t -> p h t", p=P)[:, :, ds(c, P)]).then_inc(ev(f"chunk_in{d}{slot}"), 16)
                r = NCOL + 2 * HEADS * d
                sp.dma_start(m["UM"], rows_d[r:r + 2 * HEADS, ds(c, P)].rearrange("(o h) t -> o h t", o=1)
                             .to_broadcast([P, 2 * HEADS, P])).then_inc(ev(f"chunk_in{d}{slot}"), 16)

            def h_store(j, d):
                sp.wait_ge(*at(f"h_sb{d}", j + 1))
                sp.dma_start(h_d[d][ds((chunk_of(j + NC, d) + -NC) * P, P), :], M[d]["h"].rearrange("p h e -> p (h e)")).then_inc(ev(f"h_out{d}"), 16)

            for n in range(4):
                for d in range(2):
                    chunk_load(n, d, n % 2, n >= NC)
            with sp.Fori(0, NT // 2 - 1) as i:
                for u in range(2):
                    for d in range(2):
                        h_store(2 * i + u, d)
                        chunk_load(2 * i + (u + NC + 2), d, u)
            for j in range(NT - 2, NT):
                for d in range(2):
                    h_store(j, d)

            def read_load(c, s):
                for d, B in enumerate((B1, B2)):
                    sp.dma_start(B[:, ds(c, 1), :], h_d[d].rearrange("(c p) e -> p c e", p=P)[:, ds(c, 1), :]).then_inc(ev(f"h_in{s}"), 16)

            for d in range(2):
                sp.wait_ge(*at(f"h_out{d}", 16 * NT))
                sp.wait_ge(*at(f"chunk_free{d}", NCH))
            for s in range(2):
                read_load(s, s)
            with sp.Fori(0, NT // 2 - 1) as i:
                for s in range(2):
                    sp.wait_ge(*at("hs_ok", 2 * i + s + 1))
                    read_load(2 * i + s + 2, s)
            with sp.Fori(0, (KD - 2) // 2) as i:
                for s in range(2):
                    unit(G5.U + 2 + 2 * i + s, (G5.U + s) % 2, cols_of(m_out_w, 0, KD, 2 * P * i + (2 + s) * P))
            for s in range(2):
                unit(G6.U + s, (G6.U + s) % 2, cols_of(up_w, 0, KD, FFN * (1 - s)))
            sp.wait_ge(*at("yT_ok", NT))
            for k in range(KD):
                if k >= 2:
                    sp.wait_ge(*at("x3_sb", k - 1))
                sp.dma_start(T[k % 2], x2_d[k * P:(k + 1) * P, :]).then_inc(ev(f"x2_in{k % 2}"), 16)
            def act_store(j):
                sp.wait_ge(*at("act_sb", j + 1))
                sp.dma_start(act_d[ds(P * j, P), :], T[2]).then_inc(ev("act_out"), 16)

            with sp.Fori(0, KF - 1) as j:
                unit(G6.U + 2 + 2 * j, G6.U % 2, cols_of(up_w, 0, KD, P * j + (FFN + P)))
                unit(G6.U + 3 + 2 * j, (G6.U + 1) % 2, cols_of(up_w, 0, KD, P * j + P))
                act_store(j)
            for s in range(2):
                unit(G7[0].U + s, (G7[0].U + s) % 2, cols_of(down_w, 0, KD, s * P))
            def act_load(n):
                sp.dma_start(T[4 + n % 2], act_d[n * P:(n + 1) * P, :]).then_inc(ev(f"act_in{n % 2}"), 16)

            sp.wait_ge(*at("act_out", 16 * (KF - 1)))
            for n in range(2):
                act_load(n)
            act_store(KF - 1)
            for g, (k0, kc) in enumerate(down):
                if g == 1:
                    sp.wait_ge(*at("act_out", 16 * KF))
                for n in range(max(k0, 2), k0 + kc):
                    sp.wait_ge(*at("xl_G7", n - 1))
                    act_load(n)
                with sp.Fori(0, (KD - 2) // 2) as i:
                    for s in range(2):
                        unit(G7[g].U + 2 + 2 * i + s, (G7[g].U + s) % 2, cols_of(down_w, k0, kc, 2 * P * i + (2 + s) * P), kc)
                if g + 1 < len(down):
                    for s in range(2):
                        unit(G7[g + 1].U + s, (G7[g + 1].U + s) % 2, cols_of(down_w, *down[g + 1], s * P), down[g + 1][1])
            with sp.Fori(0, NT // 2) as i:
                for s in range(2):
                    sp.wait_ge(*at("fin_sb", 2 * i + s + 1))
                    sp.dma_start(out[0][ds(2 * P * i + s * P, P), :], T[2 + s]).then_inc(ev(f"fin_out{s}"), 16)
            for s in range(2):
                sp.wait_ge(*at(f"fin_out{s}", 16 * NT // 2))

        @block.gpsimd
        def _(pool):
            step = Chain(pool, "pool_step")
            tt = nc.gpsimd.tensor_tensor

            def low(U, slot, kc=KD):
                pool.wait_ge(hi_done, U + 1)
                tt(wl[slot][:, 0:kc, :], raw[slot][:, 0:kc, :], wh[slot][:, 0:kc, :].bitcast(F32), ALU.subtract).then_inc(lo_done, 1)

            pool.sem_inc(lo_done, 2)
            nc.gpsimd.memset(ident[:], 0.0).then_inc(step.sem, 1)
            nc.gpsimd.memset(avg[:], 1.0 / D).then_inc(step.sem, 1)
            nc.gpsimd.memset(mask[0][:], 0.0).then_inc(step.sem, 1)
            nc.gpsimd.memset(mask[1][:], 0.0).then_inc(step.sem, 1)
            nc.gpsimd.memset(eps[:], EPS).then_inc(step.sem, 1)
            nc.gpsimd.memset(ones[:], 1.0).then_inc(step.sem, 1)
            step.k = 6
            step.wait()
            nc.gpsimd.affine_select(out=ident[:], in_=ident[:], compare_op=ALU.not_equal, fill=1.0, base=0,
                                    pattern=[[-1, P]], channel_multiplier=1).then_inc(ev("consts"), 1)
            nc.gpsimd.affine_select(out=mask[0][:], in_=mask[0][:], compare_op=ALU.is_ge, fill=BIG, base=0,
                                    pattern=[[1, P]], channel_multiplier=-1).then_inc(ev("consts"), 1)
            nc.gpsimd.affine_select(out=mask[1][:], in_=mask[1][:], compare_op=ALU.is_ge, fill=BIG, base=0,
                                    pattern=[[-1, P]], channel_multiplier=1).then_inc(ev("consts"), 1)

            low(0, 0)
            low(1, 1)
            pool.wait_ge(*at("xl_L1", KD))
            pool.wait_ge(*at("ctxT_out", 16))
            nc.gpsimd.memset(msum_t, 0.0).then_inc(ev("msum_zero"), 1)
            nc.gpsimd.memset(vpad[:, 0:TAPS - 1], 0.0).then_inc(ev("pads_zero"), 1)
            nc.gpsimd.memset(lxpad[:, 0:SHORT - 1], 0.0).then_inc(ev("pads_zero"), 1)

            def conv_sum(j):
                pool.wait_ge(*at("conv_ok", j + 1))
                pool.wait_ge(*at("msum_ok", j))
                pool.wait_ge(*at("msum_zero", 1))
                tt(msum_t, msum_t, B1[:, ds(j, 1), :].rearrange("p a t -> p (a t)"), ALU.add).then_inc(ev("msum_ok"), 1)

            def l1_pool(j, summed):
                U = 6 * j
                pool.wait_ge(*at("xsh", j + 1))
                tt(xsL, xs_t, xsH.bitcast(F32), ALU.subtract).then_inc(ev("xsl"), 1)
                low(U + 2, 0, 2)
                low(U + 3, 1)
                pool.wait_ge(*at("i_ok", j + 1))
                tt(i_t, i_t, xs_t, ALU.mult).then_inc(ev("ixs"), 1)
                low(U + 4, 0)
                pool.wait_ge(*at("th_ok", j + 1))
                tt(th_t, th_t, r_t, ALU.mult).then_inc(ev("m2"), 1)
                low(U + 5, 1)
                low(U + 6, 0)
                pool.wait_ge(*at("mult_ok", j + 1))
                tt(i_t, th_t, i_t, ALU.mult).then_inc(ev("bx"), 1)
                low(U + 7, 1)
                if summed:
                    conv_sum(j - 1)
                pool.wait_ge(*at("vc_ok", j + 1))
                pool.wait_ge(*at("pads_zero", 2))
                tt(vpad[:, TAPS - 1:TAPS - 1 + SEQ], vc_t, sg_t, ALU.mult).then_inc(ev("vpad_ok"), 1)

            l1_pool(0, False)
            with pool.Fori(1, KD) as j:
                l1_pool(j, True)

            for k in range(KD):
                pool.wait_ge(*at("xh_G1", k + 1))
                tt(XL[:, k, :], T[2 + k % 2], XH[:, k, :].bitcast(F32), ALU.subtract).then_inc(ev("xl_G1"), 1)

            def low_tiles(g, n=None):
                n = n or g.n
                if n >= 2:
                    with pool.Fori(0, n // 2) as i:
                        for s in range(2):
                            low(g.U + 1 + 2 * i + s, (g.U + 1 + s) % 2)
                if n % 2:
                    low(g.U + n, (g.U + n) % 2)

            low(G1a.U + 2, (G1a.U + 2) % 2)
            conv_sum(KD - 1)
            for i in range(2, 4):
                low(G1a.U + 1 + i, (G1a.U + 1 + i) % 2)
            low_tiles(G1b)
            low_tiles(G2)
            pool.wait_ge(*at("xl_G2", KD))
            nc.gpsimd.memset(T[4], 0.0).then_inc(ev("ssq_ok"), 1)
            nc.gpsimd.memset(T[6], 0.0).then_inc(ev("ssq_ok"), 1)

            def x1_sums(i, opened=False, n=2):
                for s in range(2):
                    if not opened:
                        low(G3.U + 1 + 2 * i + s, (G3.U + 1 + s) % 2)
                    if s == n:
                        return
                    pool.wait_ge(*at("sq_ok", 2 * i + s + 1))
                    pool.wait_ge(*at("ssq_ok", 2 * (2 * i + s) + 2))
                    tt(T[4], T[4], T[3], ALU.add).then_inc(ev("ssq_ok"), 1)
                    tt(T[6], T[6], T[5], ALU.add).then_inc(ev("ssq_ok"), 1)

            for u in range(1, 3):
                low(G3.U + u, (G3.U + u) % 2)
            x1_sums(0, True)
            with pool.Fori(1, KD // 2 - 1) as i:
                x1_sums(i)
            x1_sums(KD // 2 - 1, n=1)
            low_tiles(GxG)
            low_tiles(Gx)

            def q2(j, d, slot):
                m = M[d]["slots"][slot]
                pool.wait_ge(*at("w_ok", 2 * j + (2 * NC + d + 1)))
                pool.wait_ge(*at("dc_ps", HEADS * 2 * j + HEADS * (2 * NC + d - 1)))
                tt(M[d]["q2"], m["q"], m["U"], ALU.mult).then_inc(ev("q2_ok"), 1)

            with pool.Fori(0, NT // 2) as i:
                for u in range(2):
                    for d in range(2):
                        q2(2 * i + u, d, u)
            def read_low(c, s):
                pool.wait_ge(*at("xh_r", c + 1))
                tt(XL[:, :, ds(P * c, P)], T[2 + s].rearrange("p (k t) -> p k t", k=KD),
                   XH[:, :, ds(P * c, P)].bitcast(F32), ALU.subtract).then_inc(ev("xl_r"), 1)
                pool.wait_ge(*at("xl_r", c + 1))
                pool.sem_inc(ev(f"low_sb{s}"), 1)

            low(G5.U + 1, (G5.U + 1) % 2)
            with pool.Fori(0, NT // 2 - 1) as i:
                for s in range(2):
                    read_low(2 * i + s, s)
            read_low(NT - 2, 0)
            read_low(NT - 1, 1)
            pool.wait_ge(*at("yT_ok", NT))
            pool.wait_ge(*at("xl_r", NT))
            nc.gpsimd.memset(T[4], 0.0).then_inc(ev("yssq_ok"), 1)

            def y_sums(i, opened=False, n=2):
                for s in range(2):
                    if not opened:
                        low(G5.U + 1 + 2 * i + s, (G5.U + 1 + s) % 2)
                    if s == n:
                        return
                    pool.wait_ge(*at("ysq_ok", 2 * i + s + 1))
                    pool.wait_ge(*at("yssq_ok", 2 * i + s + 1))
                    tt(T[4], T[4], T[3], ALU.add).then_inc(ev("yssq_ok"), 1)

            low(G5.U + 2, G5.U % 2)
            y_sums(0, True)
            with pool.Fori(1, KD // 2 - 1) as i:
                y_sums(i)
            y_sums(KD // 2 - 1, n=1)
            low_tiles(G6)
            for g in range(len(down)):
                last = g == len(down) - 1
                if not last:
                    low_tiles(G7[g])
                else:
                    nc.gpsimd.memset(T[0], 0.0).then_inc(ev("zssq_ok"), 1)
                    for t in range(KD):
                        if t == 0:
                            for u in range(1, 3):
                                low(G7[g].U + u, (G7[g].U + u) % 2, down[g][1])
                        elif 2 <= t < KD - 1:
                            low(G7[g].U + 1 + t, (G7[g].U + 1 + t) % 2, down[g][1])
                        if t == KD - 1:
                            break
                        pool.wait_ge(*at("zsq_ok", t + 1))
                        pool.wait_ge(*at("zssq_ok", t + 1))
                        tt(T[0], T[0], T[3], ALU.add).then_inc(ev("zssq_ok"), 1)

        @block.scalar
        def _(act):
            step = Chain(act, "act_step")
            f = nc.scalar.activation

            def high(U, slot, kc=KD):
                act.wait_ge(landed[slot], U // 2 * 16 + 16)
                act.wait_ge(unit_used, U + 1)
                f(wh[slot][:, 0:kc, :], raw[slot][:, 0:kc, :], ACT.Copy).then_inc(hi_done, 1)

            def high_at(base, i, kc=KD):
                act.wait_ge(landed[base % 2], 16 * i + 16 * (base // 2 + 1))
                act.wait_ge(unit_used, 2 * i + (base + 1))
                f(wh[base % 2][:, 0:kc, :], raw[base % 2][:, 0:kc, :], ACT.Copy).then_inc(hi_done, 1)

            def second(g, kc=KD):
                high_at(g.U + 1, 0, kc)

            def tiles(g, evac, opened=True, kc=KD, kc_next=KD):
                def pair(i, first, kcs):
                    for s in range(2):
                        if not first:
                            high_at(g.U + 1 + s, i, kcs[s])
                        elif s == 0:
                            high_at(g.U + 2, i, kcs[s])
                        if evac:
                            act.wait_ge(unit_used, 2 * i + (g.U + s + 3))
                            evac(2 * i + s, PS[(g.T + s) % 2], taken[(g.T + s) % 2])

                pair(0, opened, (kc, kc))
                if g.n // 2 > 2:
                    with act.Fori(1, g.n // 2 - 1) as i:
                        pair(i, False, (kc, kc))
                pair(g.n // 2 - 1, False, (kc, kc_next))

            for c in range(NT // 2):
                act.dma_start(B1[:, 2 * c:2 * c + 2, :], x[2 * P * c:2 * P * (c + 1), :].rearrange("(c p) d -> p c d", p=P)).then_inc(ev(f"x_in{c}"), 16)
            act.dma_start(ctx_t, ctx.rearrange("(c p) d -> p c d", p=P)).then_inc(ev("ctx_tok"), 16)
            act.wait_ge(*at("consts", 3))
            for c in range(NT + NC):
                if c < NT:
                    act.wait_ge(*at(f"x_in{c // 2}", 16))
                else:
                    act.wait_ge(*at("ctx_tok", 16))
                step.link(f(PS[3][:], B1[:, c, :] if c < NT else ctx_t[:, c - NT, :], ACT.Square, accum_out=small[:, 0, c:c + 1]))
            f(small[:, 1, 0:NT + NC], small[:, 0, 0:NT + NC], ACT.Sqrt, scale=1.0 / D, bias=eps[:]).then_inc(ev("rms"), 1)

            act.wait_ge(*at("pv", 1))
            for n, name in enumerate(("c", "c", "c_2", "c_ctx")):
                f(CA[:, :, n], pvec(name, KD), ACT.Silu).then_inc(ev("ca"), 1)
            step.link(f(lam4[:, 0, :], pvec("lam", KD), ACT.Abs))
            f(lam4[:, 1, :], lam4[:, 0, :], ACT.Exp, scale=-1.0).then_inc(ev("lam_e"), 1)
            high(0, 0)
            second(L1)
            act.wait_ge(*at("mod_ok", 1))
            for k in range(KD):
                act.wait_ge(*at("h_t", k + 1))
                f(XH[:, k, :], T[5 + k % 2], ACT.Identity, bias=MOD[:, k:k + 1]).then_inc(ev("xh_L1"), 1)

            act.wait_ge(*at("pj", 1))
            act.wait_ge(*at("ctxT_out", 16))
            act.wait_ge(*at("xT_out", 16))

            def l1_act(j, opened=False):
                U = 6 * j
                def land(pos):
                    act.wait_ge(landed[pos % 2], 48 * j + 16 * (pos // 2 + 1))
                def hi(pos, kc=KD):
                    land(pos)
                    act.wait_ge(unit_used, U + pos + 1)
                    f(wh[pos % 2][:, 0:kc, :], raw[pos % 2][:, 0:kc, :], ACT.Copy).then_inc(hi_done, 1)

                step.link(f(PJa[:], PJ[:, ds(j, 1), :].rearrange("p a n -> p (a n)"), ACT.Copy))
                if not opened:
                    hi(1)
                act.wait_ge(unit_used, U + 3)
                act.wait_ge(*at("xs_ok", j))
                f(lxpad[:, SHORT - 1:SHORT - 1 + SEQ], PS[0][:], ACT.Copy).then_inc(ev("lx_sb"), 1)
                act.wait_ge(*at("lx_sb", j + 1))
                act.sem_inc(taken[0], 1)
                act.wait_ge(*at("xs_ok", j + 1))
                act.wait_ge(*at("ri_ps", j))
                f(xsH, xs_t, ACT.Copy).then_inc(ev("xsh"), 1)
                act.wait_ge(gates_in, 16 * j + 16)
                hi(2, 2)
                act.wait_ge(unit_used, U + 4)
                act.wait_ge(*at("lru_out", 16 * j))
                f(ls_t, PS[1][:], ACT.Silu).then_inc(ev("ls_sb"), 1)
                act.wait_ge(*at("ls_sb", j + 1))
                act.sem_inc(taken[1], 1)
                hi(3)
                act.wait_ge(*at("ri_ps", j + 1))
                act.wait_ge(*at("lru_y", j))
                f(r_t, PS[2][:], ACT.Sigmoid, bias=PJa[:, TAPS + SHORT + 2:TAPS + SHORT + 3]).then_inc(ev("r_ok"), 1)
                f(i_t, PS[3][:], ACT.Sigmoid, bias=PJa[:, TAPS + SHORT + 3:TAPS + SHORT + 4]).then_inc(ev("i_ok"), 1)
                hi(4)
                act.wait_ge(unit_used, U + 6)
                act.wait_ge(*at("vpad_ok", j))
                f(sg_t, PS[0][:], ACT.Sigmoid).then_inc(taken[0], 1)
                act.wait_ge(*at("r_ok", j + 1))
                f(th_t, r_t, ACT.Tanh, scale=PJa[:, TAPS + SHORT + 5:TAPS + SHORT + 6]).then_inc(ev("th_raw"), 1)
                f(a_t, r_t, ACT.Exp, scale=PJa[:, TAPS + SHORT + 4:TAPS + SHORT + 5]).then_inc(ev("a_ok"), 1)
                act.wait_ge(*at("a_ok", j + 1))
                act.wait_ge(*at("th_raw", j + 1))
                step.link(f(r_t, a_t, ACT.Square))
                f(r_t, r_t, ACT.Copy, bias=1.0).then_inc(ev("th_ok"), 1)
                hi(5)
                act.wait_ge(unit_used, U + 7)
                f(vc_t, PS[1][:], ACT.Copy).then_inc(ev("vc_ok"), 1)
                act.wait_ge(*at("vc_ok", j + 1))
                act.sem_inc(taken[1], 1)
                act.wait_ge(landed[0], 48 * j + 64)
                act.wait_ge(unit_used, U + 7)
                f(wh[0][:], raw[0][:], ACT.Copy).then_inc(hi_done, 1)
                act.wait_ge(*at("m2", j + 1))
                f(th_t, th_t, ACT.Sqrt).then_inc(ev("mult_ok"), 1)
                act.wait_ge(*at("cs_ps", j + 1))
                act.wait_ge(*at("cs_out", 16 * j))
                f(cs_t, PS[2][:], ACT.Silu).then_inc(ev("cs_sb"), 1)

            l1_act(0, True)
            with act.Fori(1, KD) as j:
                step.loop(j, 2)
                step.base -= 2
                l1_act(j)
            step.done(KD)

            second(G1a)
            for k in range(KD):
                act.wait_ge(*at(f"lru_in{k % 2}", 16 * (k // 2 + 1)))
                if k == 0:
                    act.wait_ge(unit_used, L1.end)
                f(XH[:, k, :], T[2 + k % 2], ACT.Copy).then_inc(ev("xh_G1"), 1)
            act.wait_ge(*at("vpad_ok", KD))
            act.wait_ge(*at("cs_out", 16 * KD))
            act.wait_ge(*at("ada_summed", 2 * KD))
            for g, k0 in ((G1a, 0), (G1b, KD // 2)):
                tiles(g, lambda t, ps, tk: f(B2[:, ds(t + k0, 1), :].rearrange("p a t -> p (a t)"), ps[:], ACT.Copy).then_inc(tk, 1), g is G1a)

            second(G2)
            act.wait_ge(*at("var_ps", 1))
            f(small[:, 1, 0:NT], PS[3][:, 0:NT], ACT.Sqrt, bias=eps[:]).then_inc(ev("ln_sd"), 1)
            for k in range(KD):
                act.wait_ge(*at("ln_t", k + 1))
                if k >= 2:
                    act.wait_ge(*at("xl_G2", k - 1))
                elif k == 1:
                    act.wait_ge(*at("ln_t", 2))
                step.link(f(T[2 + k % 2], B1[:, k, :], ACT.Silu, scale=pcol("cln_g", k), bias=pcol("cln_b", k)))
                if k == 0:
                    act.wait_ge(unit_used, G1b.end)
                f(XH[:, k, :], T[2 + k % 2], ACT.Copy).then_inc(ev("xh_G2"), 1)
            tiles(G2, None)
            second(G3)
            for k in range(KD):
                act.wait_ge(*at("yconv_ok", KD))
                act.wait_ge(unit_used, G2.end)
                f(XH[:, k, :], B1[:, k, :], ACT.Copy).then_inc(ev("xh_G3"), 1)
            def x1_squares(i, opened=False):
                if opened:
                    high_at(G3.U + 2, i)
                for s in range(2):
                    if not opened:
                        high_at(G3.U + 1 + s, i)
                    t = 2 * i + s
                    act.wait_ge(*at("x1_ok", t + 1))
                    act.wait_ge(*at("ssq_ok", 2 * t + 2))
                    x1 = B2[:, ds(t, 1), :].rearrange("p a t -> p (a t)")
                    f(T[3], x1, ACT.Square)
                    f(T[5], x1, ACT.Square, scale=pcol("final_g", t)).then_inc(ev("sq_ok"), 1)

            x1_squares(0, True)
            act.wait_ge(*at("ctx_in", 16))
            act.wait_ge(*at("sc_ok", 1))
            for k in range(KD):
                f(XCH[:, k, :], cn[:, k, :], ACT.Identity, scale=SC[:, 4, k:k + 1], bias=ADA[:, k, 1:2]).then_inc(ev("xh_c"), 1)
            with act.Fori(1, KD // 2) as i:
                x1_squares(i)

            high_at(Gx.U, 0)
            act.wait_ge(*at("n1_ms", 1))
            f(T[1], T[1], ACT.Sqrt).then_inc(ev("n1_sd2"), 1)
            act.wait_ge(*at("stat1_ps", 1))
            f(T[3], PS[2][:], ACT.Sqrt, bias=eps[:]).then_inc(ev("n1_sd1"), 1)
            for k in range(KD):
                act.wait_ge(*at("x2n", k + 1))
                f(XH[:, k, :], T[4 + k % 2], ACT.Identity, bias=ADA[:, k, 0:1]).then_inc(ev("xh_Gx"), 1)

            def proj(t, s, bias, ctx=False, fn=ACT.Identity, scale=None):
                b = (PAIR + s) % 2
                act.wait_ge(unit_used, t + (GxG.U + 3))
                act.wait_ge(*at(f"proj_out{s}", 8 * t + -8 * s))
                if ctx:
                    step.sig(f(stage[s][:, 0:CTX], PS[2 + s][:, 0:CTX], fn, bias=bias))
                step.sig(f(stage[s][:, CTX:ALL], PS[b][:], fn, bias=bias))
                step.wait()
                if scale is not None:
                    step.link(f(stage[s][:, CTX:ALL], stage[s][:, CTX:ALL], ACT.Copy, scale=scale))
                act.sem_inc(ev("proj_sb"), 1)
                act.sem_inc(taken[b], 1)

            def proj_pairs(first, n, ctx=False, fn=ACT.Identity):
                with act.Fori(0, n // 2) as i:
                    step.loop(i, 2 if fn == ACT.Identity and not ctx else 4)
                    for u in range(2):
                        high_at(GxG.U + first + u + 1, i)
                        proj(2 * i + (first + u), (first + u) % 2, pcol("m_in_b", 2 * i + (first + u - 1)), ctx, fn,
                             None if ctx else pcol("m_norm_g_2", 2 * i + u))
                step.done(n // 2)

            high_at(GxG.U + 2, 0)
            proj(0, 0, pcol("gate_b"), True)
            for t in range(1, Q_TILES + 1):
                if t >= 2:
                    high_at(GxG.U + t + 1, 0)
                proj(t, t % 2, pcol("m_in_b", t - 1))
                if t == 3:
                    act.wait_ge(*at("f_in", 32))
                    step.link(f(LS[:, 1, :], LS[:, 0, :], ACT.Abs))
                    f(LS[:, 1, :], LS[:, 1, :], ACT.Exp, scale=-1.0).then_inc(ev("f_e"), 1)
            proj_pairs(Q_TILES + 1, KV_TILES, True)
            proj_pairs(Q_TILES + KV_TILES + 1, KD, False, ACT.Sigmoid)

            act.wait_ge(*at("cols_sb", 1))
            f(ECOL, COLS[:, :, 2 * HEADS:NCOL], ACT.Exp).then_inc(ev("ecol"), 1)

            def weights(k, slot, d, seq):
                m = M[d]["slots"][slot]
                n, x, j, y = indices(k, slot, d)
                act.wait_ge(*at(f"chunk_in{d}{slot}", 32 * k + 32))
                f(m["U"], m["U"], ACT.Exp).then_inc(ev("w_ok"), 1)
                if seq:
                    act.wait_ge(*at("d_ok", y + 1))
                    f(m["M"], m["M"], ACT.Exp, scale=-1.0).then_inc(ev("e_ok"), 1)
                act.wait_ge(*at("t_ps", x + 1))
                act.wait_ge(*at("rec_zero", 1))
                f(M[d]["va"][:, :, 0:DV], PS[1][:].rearrange("p (h e) -> p h e", h=HEADS), ACT.Copy).then_inc(ev("va_ok"), 1)

            def heads(k, slot, d, seq):
                if not seq:
                    return
                n, x, j, y = indices(k, slot, d)
                act.wait_ge(*at("rec_ok", y + 1))
                act.wait_ge(*at(f"h_out{d}", 16 * j))
                for h in range(HEADS):
                    act.wait_ge(*at("num_ps", HEADS * y + (h // 2 * 2 + 2)))
                    f(M[d]["h"][:, h, :], PS[3][:, DV * h:DV * (h + 1)], ACT.Copy, scale=rec_t[d][:, h:h + 1]).then_inc(ev("num_free"), 1)
                act.wait_ge(*at("num_free", HEADS * y + HEADS))
                act.sem_inc(ev(f"h_sb{d}"), 1)

            recurrence(act, weights, heads)

            def read_ssq(c, s):
                act.wait_ge(*at("hs_ok", c + 1))
                if not isinstance(c, int) or c >= 2:
                    act.wait_ge(*at("hn_ok", c + -1))
                for h in range(HEADS):
                    e = slice(h * DV, (h + 1) * DV)
                    ins = f(B2[:, ds(c, 1), e].rearrange("p a e -> p (a e)"), B1[:, ds(c, 1), e].rearrange("p a e -> p (a e)"), ACT.Square,
                            accum_out=small[:, 3, HEADS * s + h:HEADS * s + h + 1])
                step.link(ins)
                f(small[:, 4, HEADS * s:HEADS * (s + 1)], small[:, 3, HEADS * s:HEADS * (s + 1)], ACT.Sqrt, scale=1.0 / DV, bias=eps[:]).then_inc(ev("hrms"), 1)

            def gate_load(c, s):
                act.dma_start(T[s].rearrange("p (k t) -> p k t", k=KD),
                              proj_d[GATE_ROW - D:GATE_ROW, :].rearrange("(k p) t -> p k t", p=P)[:, :, ds(P * c + CTX, P)]).then_inc(ev(f"o_in{s}"), 16)

            def read_high(c, s, load=True):
                act.wait_ge(*at("yT_ok", c + 1))
                if load:
                    gate_load(c + 2, s)
                f(XH[:, :, ds(P * c, P)], T[2 + s].rearrange("p (k t) -> p k t", k=KD), ACT.Copy).then_inc(ev("xh_r"), 1)

            for d in range(2):
                act.wait_ge(*at(f"chunk_free{d}", NCH))
            gate_load(0, 0)
            gate_load(1, 1)
            second(G5)
            for c in range(3):
                read_ssq(c, c % 2)
            with act.Fori(0, NT // 2 - 2) as i:
                step.loop(i, 2)
                for s in range(2):
                    read_high(2 * i + s, s)
                    read_ssq(2 * i + s + 3, 1 - s)
            step.done(NT // 2 - 2)
            read_high(NT - 4, 0)
            read_ssq(NT - 1, 1)
            read_high(NT - 3, 1)
            read_high(NT - 2, 0, False)
            read_high(NT - 1, 1, False)

            def y_tiles(i, opened=False):
                if opened:
                    high_at(G5.U + 2, i)
                for s in range(2):
                    if not opened:
                        high_at(G5.U + 1 + s, i)
                    t = 2 * i + s
                    b = (G5.T + s) % 2
                    act.wait_ge(unit_used, 2 * i + (G5.U + s + 3))
                    f(B1[:, ds(t, 1), :].rearrange("p a t -> p (a t)"), PS[b][:], ACT.Copy).then_inc(ev("y_sb"), 1)
                    act.wait_ge(*at("yssq_ok", t + 1))
                    f(T[3], PS[b][:], ACT.Square).then_inc(ev("ysq_ok"), 1)
                    act.wait_ge(*at("y_sb", t + 1))
                    act.wait_ge(*at("ysq_ok", t + 1))
                    act.sem_inc(taken[b], 1)

            y_tiles(0, True)
            with act.Fori(1, KD // 2) as i:
                y_tiles(i)
            second(G6)
            act.wait_ge(*at("stat2_ps", 1))
            f(small[:, 1, 0:NT], PS[2][:, 0:NT], ACT.Sqrt, bias=eps[:]).then_inc(ev("n2_sd"), 1)
            for k in range(KD):
                act.wait_ge(*at("x3_sb", k + 1))
                if k >= 2:
                    act.wait_ge(*at("xsq_used", k - 1))
                f(T[2 + k % 2], B2[:, k, :], ACT.Square).then_inc(ev("xsq_ok"), 1)
            act.wait_ge(*at("xsq_used", KD))
            act.wait_ge(*at("n2_done", 1))
            f(T[6], PS[3][:], ACT.Sqrt, bias=eps[:]).then_inc(ev("n3_sd"), 1)
            for k in range(KD):
                act.wait_ge(*at("h2_t", k + 1))
                if k == 0:
                    act.wait_ge(unit_used, G5.end)
                f(XH[:, k, :], T[2 + k % 2], ACT.Identity, bias=ADA[:, 3 * KD + k, 0:1]).then_inc(ev("xh_G6"), 1)
            def ffn_tile(j, opened=False):
                high_at(G6.U + 2 if opened else G6.U + 1, j)
                b = G6.T % 2
                act.wait_ge(unit_used, 2 * j + (G6.U + 3))
                act.wait_ge(*at("ffn_conv", j))
                act.wait_ge(*at("ffn_silu", j))
                f(T[0], PS[b][:], ACT.Copy).then_inc(ev("g_sb"), 1)
                f(T[1], PS[b][:], ACT.Identity, scale=pcol("ffn_conv_w", j + KF), bias=pcol("ffn_conv_b_2", j)).then_inc(ev("g_sb"), 1)
                act.wait_ge(*at("g_sb", 2 * j + 2))
                act.sem_inc(taken[b], 1)
                if not opened:
                    high_at(G6.U + 2, j)
                act.wait_ge(*at("ffn_conv", j + 1))
                act.wait_ge(*at("act_sb", j))
                f(T[3], T[1], ACT.Silu).then_inc(ev("ffn_silu"), 1)

            ffn_tile(0, True)
            with act.Fori(1, KF) as j:
                ffn_tile(j)
            n = 0
            for g, (k0, kc) in enumerate(down):
                second(G7[g], kc)
                for k in range(kc):
                    act.wait_ge(*at(f"act_in{n % 2}", 16 * (n // 2 + 1)))
                    if k == 0:
                        act.wait_ge(unit_used, (G6 if g == 0 else G7[g - 1]).end)
                    f(XH[:, k, :], T[4 + n % 2], ACT.Copy).then_inc(ev("xh_G7"), 1)
                    n += 1
                if g < len(down) - 1:
                    tiles(G7[g], None, True, kc, down[g + 1][1])
                else:
                    for t in range(KD):
                        if t == 0:
                            high_at(G7[g].U + 2, 0, kc)
                        elif 2 <= t < KD - 1:
                            high_at(G7[g].U + 1 + t, 0, kc)
                        act.wait_ge(*at("z_ok", (g + 1) * KD - KD + t + 1))
                        act.wait_ge(*at("zssq_ok", t + 1))
                        f(T[3], B1[:, t, :], ACT.Square).then_inc(ev("zsq_ok"), 1)
            act.wait_ge(*at("stat4_ps", 1))
            f(small[:, 1, 0:NT], PS[2][:, 0:NT], ACT.Sqrt, bias=eps[:]).then_inc(ev("n4_sd"), 1)
            for t in range(NT):
                act.wait_ge(*at("out_ps", t + 1))
                if t >= 2:
                    act.wait_ge(*at(f"fin_out{t % 2}", 16 * (t // 2)))
                f(T[2 + t % 2], PS[t % 2][:], ACT.Copy).then_inc(ev("fin_sb"), 1)

        @block.tensor
        def _(pe):
            mm = nc.tensor.matmul

            def product(ps, w, kc, X, n):
                XHt, XLt = X
                step_n = min(n, 512)
                total, seen = 3 * kc, 0
                for k in range(kc):
                    for W, Y in ((wh[w], XHt), (wl[w], XHt), (wh[w], XLt)):
                        for c in range(0, n, step_n):
                            last = mm(ps[:, c:c + step_n], W[:, k, :], Y[:, k, c:c + step_n], start=(seen == 0), stop=(seen == total - 1))
                        seen += 1
                return last

            def tile(U, slot, ps, tk, nth, kc=KD, X=(XH, XL), n=SEQ):
                pe.wait_ge(lo_done, U + 3)
                pe.wait_ge(tk, nth + 1)
                product(ps, slot, kc, X, n).then_inc(unit_used, 1)

            def opening(g, ready, kc=KD, before=0):
                pe.wait_ge(lo_done, g.U + 4)
                for s in range(2):
                    pe.wait_ge(taken[(g.T + s) % 2], (g.T + s) // 2 + 1)
                for k in range(kc):
                    pe.wait_ge(*at(ready, before + k + 1))
                    for s in range(2):
                        w, ps = (g.U + s) % 2, PS[(g.T + s) % 2]
                        for n, (W, Y) in enumerate(((wh[w], XH), (wl[w], XH), (wh[w], XL))):
                            for c in range(0, SEQ, 512):
                                last = mm(ps[:, c:c + 512], W[:, k, :], Y[:, k, c:c + 512], start=(k == 0 and n == 0), stop=(k == kc - 1 and n == 2))
                        if k == kc - 1:
                            last.then_inc(unit_used, 1)

            def tiles(g, opened=True, **kw):
                with pe.Fori(1 if opened else 0, g.n // 2) as i:
                    for s in range(2):
                        b = (g.T + s) % 2
                        tile(2 * i + (g.U + s), (g.U + s) % 2, PS[b], taken[b], i + (g.T + s) // 2, **kw)

            def stat(ps, *srcs, event):
                for c in range(0, SEQ, 512):
                    for n, src in enumerate(srcs):
                        last = mm(ps[:, c:c + 512], avg[:], src[:, c:c + 512], start=(n == 0), stop=(n == len(srcs) - 1))
                last.then_inc(ev(event), 1)

            def token_stat(ps, *srcs, sums, diag, event):
                for c in range(NT):
                    for n, src in enumerate(srcs):
                        last = mm(ps[:, c:c + 1], src[:, P * c:P * (c + 1)], avg[:, 0:1], start=(n == 0), stop=(n == len(srcs) - 1))
                last.then_inc(ev(sums), 1)
                pe.wait_ge(*at(diag, 1))
                stat(ps, T[6], event=event)

            pe.sem_inc(unit_used, 2)
            pe.sem_inc(taken[0], 1)
            pe.sem_inc(taken[1], 1)
            pe.wait_ge(*at("consts", 3))
            for c in range(NT):
                if c % 2 == 0:
                    pe.wait_ge(*at(f"x_in{c // 2}", 16))
                if c >= 2:
                    pe.wait_ge(*at("xT_sb", c - 1))
                for k in range(KD):
                    last = nc.tensor.transpose(PS[c % 2][:, k * P:(k + 1) * P], B1[:, c, k * P:(k + 1) * P], ident[:])
                last.then_inc(ev("xT_ps"), 1)
            pe.wait_ge(*at("stage_in", 16 * len(stage_rows)))
            for t in range(NST):
                last = nc.tensor.transpose(PS[2][:, t * P:(t + 1) * P], SCR[:, t * P:(t + 1) * P], ident[:])
            last.then_inc(ev("stage_ps"), 1)
            pe.wait_ge(*at("diag", 1))
            for c in range(2):
                last = mm(PS[3][:, 512 * c:512 * c + 512], avg[:], T[3][:, 512 * c:512 * c + 512], start=True, stop=True)
            last.then_inc(ev("r_ps"), 1)
            pe.wait_ge(*at("ctxn", 1))
            pe.wait_ge(*at("xT_sb", NT))
            for c in range(NC):
                for k in range(KD):
                    last = nc.tensor.transpose(PS[c][:, k * P:(k + 1) * P], ctx_t[:, c, k * P:(k + 1) * P], ident[:])
            last.then_inc(ev("ctxT_ps"), 1)
            pe.wait_ge(*at("pv", 1))
            for q in range(PIECES):
                pe.wait_ge(*at("mod_sum", q + 1))
                for c in range(4):
                    last = mm(MOD_PS[:, 4 * q + c:4 * q + c + 1], T[4][:, PIECE * (q % 2) + c * P:PIECE * (q % 2) + (c + 1) * P], ones[:], start=True, stop=True)
                last.then_inc(ev("mod_sum_used"), 1)

            def ada(j, half):
                pe.wait_ge(*at("ada_summed", 2 * j + (half + 1)))
                for c in range(3):
                    for v in range(2):
                        last = mm(PS[3][:, 512 * half + 2 * c + v:512 * half + 2 * c + v + 1], ada_acc[:, v, c * P:(c + 1) * P], ones[:], start=True, stop=True)
                last.then_inc(ev("ada_used"), 1)

            def l1_pe(j, opened=False):
                U = 6 * j
                if not opened:
                    tile(U, 0, PS[0], taken[0], 2 * j)
                    tile(U + 1, 1, PS[1], taken[1], 2 * j)
                    ada(j + -1, 1)
                pe.wait_ge(lo_done, U + 2 + 3)
                pe.wait_ge(*at("xsl", j + 1))
                pe.wait_ge(*at("cs_sb", j))
                pe.wait_ge(*at("ada_sb", j))
                for c, ps in enumerate((PS[2], PS[3])):
                    for n, (W, Y) in enumerate(((wh[0], xsH), (wl[0], xsH), (wh[0], xsL))):
                        for h in range(0, SEQ, 512):
                            last = mm(ps[:, h:h + 512], W[:, c, :], Y[:, h:h + 512], start=(n == 0), stop=(n == 2))
                last.then_inc(unit_used, 1)
                pe.wait_ge(unit_used, U + 5)
                pe.sem_inc(ev("ri_ps"), 1)
                tile(U + 3, 1, PS[0], taken[0], 2 * j + 1)
                pe.wait_ge(*at("i_ok", j + 1))
                ada(j, 0)
                tile(U + 4, 0, PS[1], taken[1], 2 * j + 1)
                pe.wait_ge(lo_done, U + 5 + 3)
                pe.wait_ge(*at("r_ok", j + 1))
                product(PS[2], 1, KD, (XH, XL), SEQ).then_inc(unit_used, 1)
                pe.wait_ge(unit_used, U + 8)
                pe.sem_inc(ev("cs_ps"), 1)

            opening(L1, "xl_L1")
            l1_pe(0, True)
            with pe.Fori(1, KD) as j:
                l1_pe(j)
            ada(KD - 1, 1)

            opening(G1a, "xl_G1")
            tiles(G1a)
            pe.wait_ge(*at("msum_ok", KD))
            pe.wait_ge(*at("cs_sb", KD))
            stat(PS[2], msum_t, event="mean_ps")
            tiles(G1b, False)
            pe.wait_ge(*at("var_ok", 1))
            pe.wait_ge(*at("ada_sb", KD))
            token_stat(PS[3], T[5], sums="var_ps", diag="ln_diag", event="ln_r")
            opening(G2, "xl_G2")
            tiles(G2)
            opening(G3, "xl_G3")
            tiles(G3)
            pe.wait_ge(*at("ssq_ok", 2 * KD))
            pe.wait_ge(*at("sq_ok", KD))
            stat(PS[2], T[4], T[3], event="stat1_ps")
            stat(PS[3], T[6], T[5], event="stat1_ps2")

            def ctx_product(s, w):
                return product(PS[2 + s][:, 0:CTX], w, KD, (XCH, XCL), CTX)

            pe.wait_ge(lo_done, GxG.U + 3)
            pe.wait_ge(*at("xl_c", KD))
            pe.wait_ge(*at("n1_sd1", 1))
            pe.wait_ge(*at("n1_ms", 1))
            ctx_product(0, GxG.U % 2)
            opening(GxG, "xl_Gx")
            for t in range(2, Q_TILES + 1):
                tile(GxG.U + t, (GxG.U + t) % 2, PS[(GxG.T + t) % 2], taken[(GxG.T + t) % 2], (GxG.T + t) // 2)

            def proj_pairs(first, n, ctx):
                with pe.Fori(0, n // 2) as i:
                    for u in range(2):
                        t = first + u
                        b, w = (GxG.T + t) % 2, (GxG.U + t) % 2
                        if ctx:
                            pe.wait_ge(lo_done, 2 * i + (GxG.U + t + 3))
                            pe.wait_ge(taken[b], i + ((GxG.T + t) // 2 + 1))
                            ctx_product(t % 2, w)
                        tile(2 * i + (GxG.U + t), w, PS[b], taken[b], i + (GxG.T + t) // 2)

            proj_pairs(Q_TILES + 1, KV_TILES, True)
            proj_pairs(Q_TILES + KV_TILES + 1, KD, False)

            DC = [PS[2][:, 512:512 + VW], PS[0][:, 512:512 + VW]]
            DEN = PS[0][:, SEQ - HEADS:SEQ]

            pe.wait_ge(taken[0], (G5.T + 1) // 2 + 1)
            pe.wait_ge(taken[1], G5.T // 2 + 1)
            pe.wait_ge(*at("gate_rows_in", 16))
            for c in range(NCH):
                last = nc.tensor.transpose(PS[1][:, NCOL * c:NCOL * (c + 1)], ROWS[:, P * c:P * (c + 1)], ident[0:NCOL, 0:NCOL])
            last.then_inc(ev("cols_ps"), 1)

            def transposes(k, slot, d, seq):
                m = M[d]["slots"][slot]
                n, x, j, y = indices(k, slot, d)
                pe.wait_ge(*at(f"chunk_in{d}{slot}", 32 * k + 32))
                if isinstance(x, int) and x == 0:
                    pe.wait_ge(*at("cols_sb", 1))
                pe.wait_ge(*at("kw_ok", x))
                for h in range(HEADS):
                    nc.tensor.transpose(PS[0][:, h * P:(h + 1) * P], m["k"][:, h, :], ident[:])
                pe.wait_ge(*at("va_ok", x))
                for h in range(D // P):
                    last = nc.tensor.transpose(PS[1][:, h * P:(h + 1) * P], m["v"][:, h, :], ident[:])
                last.then_inc(ev("t_ps"), 1)
                if seq:
                    if not (isinstance(y, int) and y == 0):
                        pe.wait_ge(*at("p_ok", y))
                    for h in range(HEADS):
                        last = mm(PS[2][:, h * P:(h + 1) * P], m["k"][:, h, :], m["q"][:, h, :], start=True, stop=True)
                    last.then_inc(ev("s_ps"), 1)

            def heads(k, slot, d, seq):
                m = M[d]
                n, x, j, y = indices(k, slot, d)
                pe.wait_ge(*at("va_ok", x + 1))
                pe.wait_ge(*at("kw_ok", x + 1))
                if seq:
                    pe.wait_ge(*at("p_ok", y + 1))
                    pe.wait_ge(*at("q2_ok", y + 1))
                    pe.wait_ge(*at("c_ok", HEADS * x))
                    for h in range(HEADS):
                        mm(DEN[:, h:h + 1], m["p"][:, h, :], m["va"][:, h, DV:VW], start=True, stop=False)
                        last = mm(DEN[:, h:h + 1], m["q2"][:, h, :], m["C"][:, h, DV:VW], start=False, stop=True)
                    last.then_inc(ev("den_ps"), 1)
                    pe.wait_ge(*at("num_free", HEADS * y))
                for h in range(HEADS):
                    if seq:
                        num = PS[3][:, DV * h:DV * (h + 1)]
                        mm(num, m["p"][:, h, :], m["va"][:, h, 0:DV], start=True, stop=False)
                        mm(num, m["q2"][:, h, :], m["C"][:, h, 0:DV], start=False, stop=True).then_inc(ev("num_ps"), 1)
                    if h >= 2:
                        pe.wait_ge(*at("c_ok", HEADS * x + (h - 1)))
                    elif not seq:
                        pe.wait_ge(*at("c_ok", HEADS * x))
                    elif h == 1:
                        pe.wait_ge(*at("rec_ok", y + 1))
                    mm(DC[h % 2], m["kw"][:, h, :], m["va"][:, h, :], start=True, stop=True).then_inc(ev("dc_ps"), 1)

            recurrence(pe, transposes, heads)
            pe.wait_ge(*at("c_ok", HEADS * 2 * NCH))
            pe.wait_ge(*at("kw_ok", 2 * NCH))
            with pe.Fori(0, NT // 2) as i:
                for s in range(2):
                    c = 2 * i + s
                    pe.wait_ge(*at("hn_ok", c + 1))
                    pe.wait_ge(*at(f"yT_free{s}", i))
                    for k in range(KD):
                        last = nc.tensor.transpose(PS[s][:, k * P:(k + 1) * P],
                                                   HN[s][:, k * P:(k + 1) * P], ident[:])
                    last.then_inc(ev("hT_ps"), 1)
            half = SEQ // 2
            pe.wait_ge(lo_done, G5.U + 4)
            for c in range(2):
                pe.wait_ge(*at("xl_r", (c + 1) * NT // 2))
                for s in range(2):
                    if c == 0:
                        pe.wait_ge(*at(f"yT_free{(G5.T + s) % 2}", NT // 2))
                    w, ps = (G5.U + s) % 2, PS[(G5.T + s) % 2]
                    for k in range(KD):
                        for n, (W, Y) in enumerate(((wh[w], XH), (wl[w], XH), (wh[w], XL))):
                            last = mm(ps[:, half * c:half * (c + 1)], W[:, k, :], Y[:, k, half * c:half * (c + 1)],
                                      start=(k == 0 and n == 0), stop=(k == KD - 1 and n == 2))
                    if c == 1:
                        last.then_inc(unit_used, 1)
            tiles(G5)
            pe.wait_ge(*at("yssq_ok", KD))
            pe.wait_ge(*at("ysq_ok", KD))
            token_stat(PS[2], T[4], T[3], sums="stat2_ps", diag="n2_diag", event="n2_r")
            for k in range(KD):
                pe.wait_ge(*at("xsq_ok", k + 1))
                for c in range(2):
                    last = mm(PS[3][:, 512 * c:512 * c + 512], avg[:], T[2 + k % 2][:, 512 * c:512 * c + 512], start=(k == 0), stop=(k == KD - 1))
                last.then_inc(ev("xsq_used"), 1)
            opening(G6, "xl_G6")
            tiles(G6)
            for g, (k0, kc) in enumerate(down):
                opening(G7[g], "xl_G7", kc, k0)
                tiles(G7[g], kc=kc)
            pe.wait_ge(*at("zssq_ok", KD))
            pe.wait_ge(*at("zsq_ok", KD))
            token_stat(PS[2], T[0], T[3], sums="stat4_ps", diag="n4_diag", event="n4_r")
            for t in range(NT):
                pe.wait_ge(*at("fin_ok", KD * (1 + t // (NT // 2))))
                if t >= 2:
                    pe.wait_ge(*at("fin_sb", t - 1))
                for k in range(KD):
                    last = nc.tensor.transpose(PS[t % 2][:, k * P:(k + 1) * P], B1[:, k, t * P:(t + 1) * P], ident[:])
                last.then_inc(ev("out_ps"), 1)

        @block.vector
        def _(dve):
            step = Chain(dve, "dve_step")
            V = nc.vector

            def log1p(e, s, z, p):
                step.link(V.tensor_scalar(s, e, 2.0, None, ALU.add))
                step.link(V.reciprocal(s, s))
                step.link(V.tensor_tensor(s, e, s, ALU.mult))
                step.link(V.tensor_tensor(z, s, s, ALU.mult))
                n = LOG1P_TERMS
                step.link(V.tensor_scalar(p, z, 1.0 / (2 * n + 1), 1.0 / (2 * n - 1), ALU.mult, ALU.add))
                for t in range(n - 2, -1, -1):
                    step.link(V.tensor_tensor(p, p, z, ALU.mult))
                    step.link(V.tensor_scalar(p, p, 1.0 / (2 * t + 1), None, ALU.add))
                step.link(V.scalar_tensor_tensor(out=p, in0=s, scalar=2.0, in1=p, op0=ALU.mult, op1=ALU.mult))

            V.memset(SCR[:, 0:NST * P], 0.0).then_inc(ev("stage_zero"), 1)
            for c in range(NT):
                dve.wait_ge(*at("xT_ps", c + 1))
                V.tensor_copy(B2[:, :, c * P:(c + 1) * P], PS[c % 2][:].rearrange("p (k t) -> p k t", k=KD)).then_inc(ev("xT_sb"), 1)
            dve.wait_ge(*at("stage_ps", 1))
            V.tensor_copy(PV[:], PS[2][:, 0:NST * P]).then_inc(ev("pv"), 1)
            dve.wait_ge(*at("rms", 1))
            dve.wait_ge(*at("consts", 3))
            def diagonals(dst, n, event):
                step.link(V.reciprocal(small[:, 2, 0:n], small[:, 1, 0:n]))
                step.link(V.tensor_scalar(small[:, 3, 0:NT], small[:, 2, 0:NT], float(D), None, ALU.mult))
                V.tensor_tensor(dst.rearrange("p (c t) -> p c t", t=P), ident[:].rearrange("p (o t) -> p o t", o=1).to_broadcast([P, NT, P]),
                                bc(small[:, 3, 0:NT], P), ALU.mult).then_inc(ev(event), 1)

            diagonals(T[3], NT + NC, "diag")
            for c in range(NC):
                step.sig(V.tensor_scalar(ctx_t[:, c, :], ctx_t[:, c, :], small[:, 2, NT + c:NT + c + 1], None, ALU.mult))
            step.wait()
            dve.sem_inc(ev("ctxn"), 1)

            def mod_sum(q):
                dve.wait_ge(*at(f"mod_in{q % 2}", 16 * (q // 2 + 1)))
                if q >= 2:
                    dve.wait_ge(*at("mod_sum_used", q - 1))
                o = T[4][:, PIECE * (q % 2):PIECE * (q % 2 + 1)]
                step.link(V.tensor_scalar(o, mod_in[q % 2][:, 0, :], CA[:, 0, 0:1], None, ALU.mult))
                for k in range(1, KD):
                    ins = V.scalar_tensor_tensor(out=o, in0=mod_in[q % 2][:, k, :], scalar=CA[:, k, 0:1], in1=o, op0=ALU.mult, op1=ALU.add)
                    if k < KD - 1:
                        step.link(ins)
                ins.then_inc(ev("mod_sum"), 1)

            dve.wait_ge(*at("ctxT_ps", 1))
            for c in range(NC):
                step.sig(V.tensor_copy(SCR[:, VP:VP + 2 * SEQ].rearrange("p (k t) -> p k t", k=KD)[:, :, c * P:(c + 1) * P],
                                       PS[c][:].rearrange("p (k t) -> p k t", k=KD)))
            step.wait()
            dve.sem_inc(ev("ctxT_sb"), 1)

            dve.wait_ge(*at("pv", 1))
            dve.wait_ge(*at("lam_e", 1))
            log1p(lam4[:, 1, :], lam4[:, 0, :], lam4[:, 2, :], lam4[:, 3, :])
            step.link(V.tensor_scalar(lam4[:, 0, :], pvec("lam", KD), -1.0, 0.0, ALU.mult, ALU.max))
            step.link(V.tensor_tensor(lam4[:, 0, :], lam4[:, 0, :], lam4[:, 3, :], ALU.add))
            step.sig(V.tensor_scalar(PJ[:, :, TAPS + SHORT + 4], lam4[:, 0, :], -LRU_C, None, ALU.mult))
            step.sig(V.tensor_scalar(PJ[:, :, TAPS + SHORT + 5], lam4[:, 0, :], LRU_C, None, ALU.mult))
            for t0 in range(0, TAPS, P // KD):
                n = min(P // KD, TAPS - t0)
                step.sig(V.tensor_copy(PJ[:, :, t0:t0 + n], pvec(f"dw_w{t0}", n * KD).rearrange("p (t k) -> p k t", k=KD)))
            step.sig(V.tensor_copy(PJ[:, :, TAPS], pvec("dw_b", KD)))
            step.sig(V.tensor_copy(PJ[:, :, TAPS + 1:TAPS + 1 + SHORT], pvec("sc_w", SHORT * KD).rearrange("p (t k) -> p k t", k=KD)))
            for n, name in enumerate(("sc_b", "br", "bi")):
                step.sig(V.tensor_copy(PJ[:, :, TAPS + SHORT + 1 + n], pvec(name, KD)))
            step.wait()
            dve.sem_inc(ev("pj"), 1)
            dve.wait_ge(*at("ca", 4))
            for q in range(PIECES):
                mod_sum(q)
            dve.wait_ge(*at("mod_sum_used", PIECES))
            step.link(V.tensor_tensor(MOD[:], MOD_PS, pvec("mod_b", 3 * KD), ALU.add))
            step.sig(V.scalar_tensor_tensor(out=SC[:, 0, :], in0=MOD[:, KD:2 * KD], scalar=1.0, in1=pvec("norm_g", KD), op0=ALU.add, op1=ALU.mult))
            step.sig(V.tensor_scalar(SC[:, 1, :], MOD[:, 2 * KD:3 * KD], 1.0, None, ALU.add))
            step.wait()
            dve.sem_inc(ev("mod_ok"), 1)
            dve.wait_ge(*at("r_ps", 1))

            def h_low(k):
                dve.wait_ge(*at("xh_L1", k + 1))
                V.scalar_tensor_tensor(out=XL[:, k, :], in0=T[5 + k % 2], scalar=MOD[:, k:k + 1], in1=XH[:, k, :].bitcast(F32),
                                       op0=ALU.add, op1=ALU.subtract).then_inc(ev("xl_L1"), 1)

            for k in range(KD):
                if k >= 2:
                    dve.wait_ge(*at("xl_L1", k - 1))
                V.scalar_tensor_tensor(out=T[5 + k % 2], in0=B2[:, k, :], scalar=SC[:, 0, k:k + 1], in1=PS[3][:], op0=ALU.mult, op1=ALU.mult).then_inc(ev("h_t"), 1)
                if k >= 1:
                    h_low(k - 1)
            h_low(KD - 1)

            def short_conv(j):
                step.link(V.tensor_copy(PJd[:, TAPS:NJ], PJ[:, ds(j, 1), TAPS:NJ].rearrange("p a n -> p (a n)")))
                dve.wait_ge(*at("lx_sb", j + 1))
                dve.wait_ge(*at("pads_zero", 2))
                dve.wait_ge(*at("bx", j))
                step.link(V.tensor_scalar(xs_t, lxpad[:, 0:SEQ], PJd[:, TAPS + 1:TAPS + 2], PJd[:, TAPS + SHORT + 1:TAPS + SHORT + 2],
                                          ALU.mult, ALU.add))
                for t in range(1, SHORT):
                    ins = V.scalar_tensor_tensor(out=xs_t, in0=lxpad[:, t:t + SEQ], scalar=PJd[:, TAPS + 1 + t:TAPS + 2 + t],
                                                 in1=xs_t, op0=ALU.mult, op1=ALU.add)
                    if t < SHORT - 1:
                        step.link(ins)
                ins.then_inc(ev("xs_ok"), 1)

            def conv(j):
                step.link(V.tensor_copy(PJc[:], PJ[:, ds(j, 1), :].rearrange("p a n -> p (a n)")))
                dve.wait_ge(*at("vpad_ok", j + 1))
                o = B1[:, ds(j, 1), :].rearrange("p a t -> p (a t)")
                step.link(V.tensor_scalar(o, vpad[:, 0:SEQ], PJc[:, 0:1], PJc[:, TAPS:TAPS + 1], ALU.mult, ALU.add))
                for t in range(1, TAPS):
                    ins = V.scalar_tensor_tensor(out=o, in0=vpad[:, t:t + SEQ], scalar=PJc[:, t:t + 1], in1=o, op0=ALU.mult, op1=ALU.add)
                    if t < TAPS - 1:
                        step.link(ins)
                ins.then_inc(ev("conv_ok"), 1)

            def lru(j):
                dve.wait_ge(*at("bx", j + 1))
                dve.wait_ge(*at("a_ok", j + 1))
                step.link(V.tensor_tensor_scan(out=r_t, data0=a_t, data1=i_t, initial=0.0, op0=ALU.mult, op1=ALU.add))
                dve.wait_ge(*at("ls_sb", j + 1))
                V.tensor_tensor(ls_t, r_t, ls_t, ALU.mult).then_inc(ev("lru_y"), 1)

            def ada_sum(j, half, both):
                dve.wait_ge(*at("ada_in", 32 * j + 16 * (half + 1)))
                dve.wait_ge(*at("ada_used", 2 * j + half))
                for v in range(1 if both else 0, -1, -1):
                    o = ada_acc[:, v, :]
                    step.link(V.tensor_scalar(o, ada_t[:, 0, :], CA[:, 0, 2 + v:3 + v], None, ALU.mult))
                    for k in range(1, KD):
                        ins = V.scalar_tensor_tensor(out=o, in0=ada_t[:, k, :], scalar=CA[:, k, 2 + v:3 + v], in1=o, op0=ALU.mult, op1=ALU.add)
                        if v or k < KD - 1:
                            step.link(ins)
                ins.then_inc(ev("ada_summed"), 1)

            def ada_copy(j):
                dve.wait_ge(*at("ada_used", 2 * j + 2))
                for half in range(2):
                    ins = V.tensor_copy(ADA[:, ds(6 * j + 3 * half, 3), :], PS[3][:, 512 * half:512 * half + 6].rearrange("p (c t) -> p c t", t=2))
                ins.then_inc(ev("ada_sb"), 1)

            short_conv(0)
            ada_sum(0, 0, True)
            lru(0)
            for first, end, both in ((1, CTX_STEPS + 1, True), (CTX_STEPS + 1, KD, False)):
                n = 1 + (SHORT - 1) + 1 + (TAPS - 1) + 1 + 2 * (KD * (2 if both else 1) - 1)
                with dve.Fori(first, end) as j:
                    step.loop(j, n)
                    step.base -= first * n
                    ada_sum(j + -1, 1, both)
                    short_conv(j)
                    ada_copy(j + -1)
                    ada_sum(j, 0, both)
                    conv(j + -1)
                    lru(j)
                step.base += first * n
                step.done(end - first)
            ada_sum(KD - 1, 1, False)
            ada_copy(KD - 1)

            dve.wait_ge(*at("ada_sb", KD))
            step.sig(V.tensor_tensor(ADA[:, :, 0], ADA[:, :, 0], pvec("ada_b_2", 6 * KD), ALU.add))
            step.sig(V.tensor_tensor(ADA[:, 0:2 * KD, 1], ADA[:, 0:2 * KD, 1], pvec("ada_b_2", 2 * KD), ALU.add))
            step.wait()
            stt = V.scalar_tensor_tensor
            step.link(stt(out=SC[:, 4, :], in0=ADA[:, KD:2 * KD, 1], scalar=1.0, in1=pvec("pre_mix_g_2", KD), op0=ALU.add, op1=ALU.mult))
            step.link(stt(out=SC[:, 5, :], in0=ADA[:, KD:2 * KD, 0], scalar=1.0, in1=pvec("pre_mix_g_2", KD), op0=ALU.add, op1=ALU.mult))
            step.link(V.tensor_tensor(SC[:, 5, :], SC[:, 5, :], pvec("final_g", KD), ALU.mult))
            step.link(V.tensor_tensor(SC[:, 6, :], ADA[:, 2 * KD:3 * KD, 0], pvec("post_mix_g_2", KD), ALU.mult))
            step.link(stt(out=SC[:, 7, :], in0=ADA[:, 4 * KD:5 * KD, 0], scalar=1.0, in1=pvec("pre_ffn_g_2", KD), op0=ALU.add, op1=ALU.mult))
            step.link(V.tensor_tensor(SC[:, 8, :], ADA[:, 5 * KD:6 * KD, 0], pvec("post_ffn_g_2", KD), ALU.mult))
            dve.sem_inc(ev("sc_ok"), 1)

            conv(KD - 1)
            dve.wait_ge(*at("mean_ps", 1))
            dve.wait_ge(*at("msum_ok", KD))
            for k in range(KD):
                step.link(V.tensor_tensor(B1[:, k, :], B1[:, k, :], PS[2][:], ALU.subtract))
                if k == 0:
                    step.link(V.tensor_tensor(T[5], B1[:, 0, :], B1[:, 0, :], ALU.mult))
                else:
                    step.link(V.tensor_tensor(T[4], B1[:, k, :], B1[:, k, :], ALU.mult))
                    step.link(V.tensor_tensor(T[5], T[5], T[4], ALU.add))
            dve.sem_inc(ev("var_ok"), 1)
            dve.wait_ge(*at("ln_sd", 1))
            diagonals(T[6], NT, "ln_diag")
            dve.wait_ge(*at("ln_r", 1))

            def ln_low(k):
                dve.wait_ge(*at("xh_G2", k + 1))
                V.tensor_tensor(XL[:, k, :], T[2 + k % 2], XH[:, k, :].bitcast(F32), ALU.subtract).then_inc(ev("xl_G2"), 1)

            for k in range(KD):
                V.tensor_tensor(B1[:, k, :], B1[:, k, :], PS[3][:], ALU.mult).then_inc(ev("ln_t"), 1)
                if k >= 1:
                    ln_low(k - 1)
            ln_low(KD - 1)

            def tiles(g, evac, n=None, first=0, end=None):
                end = end or g.n // 2

                def pair(i):
                    for s in range(2):
                        b = (g.T + s) % 2
                        dve.wait_ge(unit_used, 2 * i + (g.U + s + 3))
                        evac(2 * i + s, s, i, PS[b], taken[b])

                if end - first == 1:
                    pair(first)
                    return
                with dve.Fori(first, end) as i:
                    if n:
                        step.loop(i, 2 * n)
                        step.base -= 2 * n * first
                    pair(i)
                if n:
                    step.base += 2 * n * first
                    step.done(end - first)

            def g2(t, s, i, ps, tk):
                dve.wait_ge(*at(f"cs_in{s}", 16 * i + 16))
                stt(out=B1[:, ds(t, 1), :].rearrange("p a t -> p (a t)"), in0=ps[:], scalar=pcol("pw2_b", t), in1=T[s],
                    op0=ALU.add, op1=ALU.mult).then_inc(ev("yconv_ok"), 1)
                dve.wait_ge(*at("yconv_ok", t + 1))
                dve.sem_inc(tk, 1)
                dve.sem_inc(ev(f"cs_free{s}"), 1)

            dve.wait_ge(*at("xl_G2", KD))
            tiles(G2, g2)
            for k in range(KD):
                dve.wait_ge(*at("xh_G3", k + 1))
                V.tensor_tensor(XL[:, k, :], B1[:, k, :], XH[:, k, :].bitcast(F32), ALU.subtract).then_inc(ev("xl_G3"), 1)

            def g3(t, s, i, ps, tk):
                row = B2[:, ds(t, 1), :].rearrange("p a t -> p (a t)")
                step.link(V.tensor_tensor(T[2], ps[:], row, ALU.add))
                dve.sem_inc(tk, 1)
                dve.wait_ge(*at(f"res_in{s}", 16 * i + 16))
                stt(out=row, in0=T[2], scalar=SC[:, 1, :][:, ds(t, 1)], in1=T[s], op0=ALU.mult, op1=ALU.add).then_inc(ev("x1_ok"), 1)
                dve.wait_ge(*at("x1_ok", t + 1))
                dve.sem_inc(ev(f"res_free{s}"), 1)

            tiles(G3, g3, 1, 0, 1)
            dve.wait_ge(*at("ctx_in", 16))
            for k in range(KD):
                tmp = T[2][:, 0:CTX]
                step.link(V.tensor_scalar(tmp, cn[:, k, :], SC[:, 4, k:k + 1], ADA[:, k, 1:2], ALU.mult, ALU.add))
                dve.wait_ge(*at("xh_c", k + 1))
                V.tensor_tensor(XCL[:, k, :], tmp, XCH[:, k, :].bitcast(F32), ALU.subtract).then_inc(ev("xl_c"), 1)
                dve.wait_ge(*at("xl_c", k + 1))
            tiles(G3, g3, 1, 1)

            dve.wait_ge(*at("stat1_ps", 1))
            step.link(V.tensor_scalar(T[1], PS[2][:], EPS, EPS, ALU.add, ALU.mult))
            dve.wait_ge(*at("stat1_ps2", 1))
            step.link(V.tensor_tensor(T[1], T[1], PS[3][:], ALU.add))
            dve.sem_inc(ev("n1_ms"), 1)
            dve.wait_ge(*at("n1_sd2", 1))
            step.link(V.reciprocal(T[1], T[1]))

            def x_low(k):
                dve.wait_ge(*at("xh_Gx", k + 1))
                stt(out=XL[:, k, :], in0=T[4 + k % 2], scalar=ADA[:, k, 0:1], in1=XH[:, k, :].bitcast(F32), op0=ALU.add, op1=ALU.subtract).then_inc(ev("xl_Gx"), 1)

            for k in range(KD):
                if k >= 2:
                    dve.wait_ge(*at("xl_Gx", k - 1))
                stt(out=T[4 + k % 2], in0=B2[:, k, :], scalar=SC[:, 5, k:k + 1], in1=T[1], op0=ALU.mult, op1=ALU.mult).then_inc(ev("x2n"), 1)
                dve.wait_ge(*at("x2n", k + 1))
                if k >= 1:
                    x_low(k - 1)
            x_low(KD - 1)
            dve.wait_ge(*at("n1_sd1", 1))
            step.link(V.reciprocal(T[0], T[3]))
            for k in range(KD):
                stt(out=B2[:, k, :], in0=B2[:, k, :], scalar=pcol("final_g", k), in1=T[0], op0=ALU.mult, op1=ALU.mult).then_inc(ev("x2_sb"), 1)

            dve.wait_ge(*at("f_in", 32))
            dve.wait_ge(*at("f_e", 1))
            log1p(LS[:, 1, :], LS[:, 2, :], LS[:, 3, :], LS[:, 4, :])
            stt(out=LS[:, 0, :], in0=LS[:, 0, :], scalar=0.0, in1=LS[:, 4, :], op0=ALU.min, op1=ALU.subtract).then_inc(ev("lf_sb"), 1)

            def reverse(dst, src):
                for a, b in ((0, CTX), (CTX, ALL)):
                    step.link(V.tensor_copy(dst[32:32 + HEADS, a:b], src[32:32 + HEADS, a:b][:, ::-1]))

            dve.wait_ge(*at("x2_out", 16 * KD // 2))
            step.link(V.memset(RZ, 1.0))
            step.link(V.memset(RZ.rearrange("p (c t) -> p c t", t=P)[:, :, 0:1], 0.0))
            dve.wait_ge(*at("rows_in", 64))
            reverse(RI, UN[0])
            reverse(RF, UN[1])
            step.link(V.tensor_tensor_scan(out=RB, data0=RZ, data1=RF, initial=0.0, op0=ALU.mult, op1=ALU.add))
            step.link(V.tensor_tensor(RI, RI, RB, ALU.subtract))
            step.link(V.memset(RZ, 0.0))

            def by_chunk(r):
                return r.rearrange("p (c t) -> p c t", t=P)

            step.link(V.tensor_copy(by_chunk(RZ)[:, 1:NCH, 0], by_chunk(RB)[:, 0:NCH - 1, P - 1]))
            step.link(V.tensor_tensor_scan(out=RM, data0=RZ, data1=RI, initial=0.0, op0=ALU.add, op1=ALU.max))
            step.link(V.memset(mprev[:], 0.0))
            step.link(V.tensor_tensor(mprev[:, 1:NCH], by_chunk(RB)[:, 0:NCH - 1, P - 1], by_chunk(RM)[:, 0:NCH - 1, P - 1], ALU.add))
            step.link(V.scalar_tensor_tensor(out=RF, in0=RB, scalar=-1.0, in1=RM, op0=ALU.mult, op1=ALU.subtract))
            step.link(V.tensor_tensor(by_chunk(RO), by_chunk(RI), by_chunk(RM)[:, :, P - 1:P].to_broadcast([36, NCH, P]), ALU.subtract))
            step.link(V.tensor_tensor(by_chunk(RZ), bc(mprev[:], P), by_chunk(RM), ALU.subtract))
            for q in range(5):
                reverse(UN[q], RQ[q])
            dve.sem_inc(ev("rows_sb"), 1)

            dve.wait_ge(*at("rows_out", 16 * 10))
            for s in range(2):
                dve.wait_ge(*at(f"proj_out{s}", 16 * STORES[s]))
            dve.wait_ge(*at("cols_ps", 1))
            V.tensor_copy(COLS, PS[1][:, 0:NCH * NCOL].rearrange("p (c n) -> p c n", n=NCOL)).then_inc(ev("cols_sb"), 1)
            for d in range(2):
                step.link(V.memset(M[d]["C"], 0.0))
                step.link(V.memset(M[d]["va"][:, :, DV:VW], 1.0))
            dve.sem_inc(ev("rec_zero"), 1)
            dve.wait_ge(*at("cols_sb", 1))
            dve.wait_ge(*at("ecol", 1))
            step.link(V.tensor_scalar(ECOL[:, :, 0:2 * HEADS], ECOL[:, :, 0:2 * HEADS], float(DK) ** 0.5, None, ALU.mult))
            DC = [PS[2][:, 512:512 + VW], PS[0][:, 512:512 + VW]]
            DEN = PS[0][:, SEQ - HEADS:SEQ]

            def col(cols, q, n, d):
                return cols[:, ds(chunk_of(n, d), 1), (2 * q + d) * HEADS:(2 * q + d + 1) * HEADS].rearrange("p a h -> p (a h)")

            def weigh(k, slot, d, seq):
                m, w = M[d]["slots"][slot], M[d]
                n, x, j, y = indices(k, slot, d)
                if seq:
                    dve.wait_ge(*at(f"chunk_in{d}{slot}", 32 * k + 32))
                    step.link(V.tensor_tensor(m["M"], m["M"], bc(col(COLS, 0, n, d), P), ALU.subtract))
                    stt(out=m["M"], in0=m["M"], scalar=0.0, in1=mask[d][:].rearrange("p (o t) -> p o t", o=1).to_broadcast([P, HEADS, P]), op0=ALU.max, op1=ALU.add).then_inc(ev("d_ok"), 1)
                dve.wait_ge(*at("t_ps", x + 1))
                V.tensor_tensor(w["kw"], PS[0][:, 0:HQ].rearrange("p (h n) -> p h n", h=HEADS), bc(col(ECOL, 1, n, d), P), ALU.mult).then_inc(ev("kw_ok"), 1)
                if seq:
                    dve.wait_ge(*at("s_ps", y + 1))
                    dve.wait_ge(*at("e_ok", y + 1))
                    V.tensor_tensor(w["p"], PS[2][:, 0:HQ].rearrange("p (h n) -> p h n", h=HEADS), m["M"], ALU.mult).then_inc(ev("p_ok"), 1)

            def heads(k, slot, d, seq):
                n, x, j, y = indices(k, slot, d)
                if seq:
                    dve.wait_ge(*at("den_ps", y + 1))
                    dve.wait_ge(*at(f"h_sb{d}", j))
                    r = rec_t[d][:]
                    step.link(stt(out=r, in0=DEN, scalar=-1.0, in1=col(ECOL, 0, n, d), op0=ALU.mult, op1=ALU.max))
                    step.link(V.tensor_tensor(r, DEN, r, ALU.max))
                    V.reciprocal(r, r).then_inc(ev("rec_ok"), 1)
                last = P - 1 if d == 0 else 0
                dve.wait_ge(*at("w_ok", x + 1))
                for h in range(HEADS):
                    dve.wait_ge(*at("dc_ps", HEADS * x + (h + 1)))
                    C = M[d]["C"][:, h, :]
                    stt(out=C, in0=C, scalar=M[d]["slots"][slot]["U"][:, h, last:last + 1], in1=DC[h % 2],
                        op0=ALU.mult, op1=ALU.add).then_inc(ev("c_ok"), 1)
                dve.wait_ge(*at("c_ok", HEADS * x + HEADS))
                dve.sem_inc(ev(f"chunk_free{d}"), 1)

            recurrence(dve, weigh, heads, step, 4 * 3)

            def read_sum(c, s, i):
                dve.wait_ge(*at(f"h_in{s}", 32 * i + 32))
                row = B1[:, ds(c, 1), :]
                V.tensor_tensor(row, row, B2[:, ds(c, 1), :], ALU.add).then_inc(ev("hs_ok"), 1)

            def read_norm(c, s, i):
                dve.wait_ge(*at("hrms", c + 1))
                step.link(V.reciprocal(small[:, 5, HEADS * s:HEADS * (s + 1)], small[:, 4, HEADS * s:HEADS * (s + 1)]))
                dve.wait_ge(*at("hs_ok", c + 1))
                if not isinstance(c, int) or c >= 2:
                    dve.wait_ge(*at("hT_ps", c + -1))
                V.tensor_tensor(HN[s].rearrange("p (h e) -> p h e", h=HEADS), B1[:, ds(c, 1), :].rearrange("p a (h e) -> p (a h) e", h=HEADS),
                                bc(small[:, 5, HEADS * s:HEADS * (s + 1)], DV), ALU.mult).then_inc(ev("hn_ok"), 1)

            def read_gate(c, s, i):
                dve.wait_ge(*at("hT_ps", c + 1))
                dve.wait_ge(*at(f"o_in{s}", 16 * i + 16))
                dve.wait_ge(*at(f"low_sb{s}", i))
                V.tensor_tensor(T[2 + s], PS[s][:], T[s], ALU.mult).then_inc(ev("yT_ok"), 1)
                dve.wait_ge(*at("yT_ok", c + 1))
                dve.sem_inc(ev(f"yT_free{s}"), 1)

            read_sum(0, 0, 0)
            read_sum(1, 1, 0)
            read_norm(0, 0, 0)
            read_sum(2, 0, 1)
            read_norm(1, 1, 0)
            with dve.Fori(0, NT // 2 - 2) as i:
                step.loop(i, 2)
                for s in range(2):
                    read_gate(2 * i + s, s, i)
                    read_norm(2 * i + s + 2, s, i + 1)
                    read_sum(2 * i + s + 3, 1 - s, i + (1 + s))
            step.done(NT // 2 - 2)
            last = NT // 2 - 1
            read_gate(NT - 4, 0, last - 1)
            read_norm(NT - 2, 0, last)
            read_sum(NT - 1, 1, last)
            read_gate(NT - 3, 1, last - 1)
            read_norm(NT - 1, 1, last)
            read_gate(NT - 2, 0, last)
            read_gate(NT - 1, 1, last)

            dve.wait_ge(*at("n2_sd", 1))
            diagonals(T[6], NT, "n2_diag")
            dve.wait_ge(*at("n2_r", 1))
            for k in range(KD):
                dve.wait_ge(*at("y_sb", KD))
                step.link(V.tensor_tensor(B1[:, k, :], B1[:, k, :], PS[2][:], ALU.mult))
                dve.wait_ge(*at(f"x2_in{k % 2}", 16 * (k // 2 + 1)))
                stt(out=B2[:, k, :], in0=B1[:, k, :], scalar=SC[:, 6, k:k + 1], in1=T[k % 2], op0=ALU.mult, op1=ALU.add).then_inc(ev("x3_sb"), 1)
            dve.sem_inc(ev("n2_done"), 1)
            dve.wait_ge(*at("n3_sd", 1))
            step.link(V.reciprocal(T[6], T[6]))

            def h2_low(k):
                dve.wait_ge(*at("xh_G6", k + 1))
                stt(out=XL[:, k, :], in0=T[2 + k % 2], scalar=ADA[:, 3 * KD + k, 0:1], in1=XH[:, k, :].bitcast(F32),
                    op0=ALU.add, op1=ALU.subtract).then_inc(ev("xl_G6"), 1)

            for k in range(KD):
                if k >= 2:
                    dve.wait_ge(*at("xl_G6", k - 1))
                stt(out=T[2 + k % 2], in0=B2[:, k, :], scalar=SC[:, 7, k:k + 1], in1=T[6], op0=ALU.mult, op1=ALU.mult).then_inc(ev("h2_t"), 1)
                dve.wait_ge(*at("h2_t", k + 1))
                if k >= 1:
                    h2_low(k - 1)
            h2_low(KD - 1)
            dve.wait_ge(*at("xl_G6", KD))

            def grid(t):
                return t.rearrange("p (r w) -> p r w", w=GRID)

            with dve.Fori(0, KF) as j:
                step.loop(j, 1)
                dve.wait_ge(*at("g_sb", 2 * j + 2))
                step.link(stt(out=grid(T[1])[:, :, 1:GRID], in0=grid(T[0])[:, :, 0:GRID - 1], scalar=pcol("ffn_conv_w", j),
                              in1=grid(T[1])[:, :, 1:GRID], op0=ALU.mult, op1=ALU.add))
                stt(out=grid(T[1])[:, :, 0:GRID - 1], in0=grid(T[0])[:, :, 1:GRID], scalar=pcol("ffn_conv_w", j + 2 * KF),
                    in1=grid(T[1])[:, :, 0:GRID - 1], op0=ALU.mult, op1=ALU.add).then_inc(ev("ffn_conv"), 1)
                b = (G6.T + 1) % 2
                dve.wait_ge(unit_used, 2 * j + (G6.U + 4))
                dve.wait_ge(*at("ffn_silu", j + 1))
                dve.wait_ge(*at("act_out", 16 * j))
                V.tensor_tensor(T[2], PS[b][:], T[3], ALU.mult).then_inc(ev("act_sb"), 1)
                dve.wait_ge(*at("act_sb", j + 1))
                dve.sem_inc(taken[b], 1)
            step.done(KF)

            n = 0
            for g, (k0, kc) in enumerate(down):
                for k in range(kc):
                    dve.wait_ge(*at("xh_G7", n + 1))
                    V.tensor_tensor(XL[:, k, :], T[4 + n % 2], XH[:, k, :].bitcast(F32), ALU.subtract).then_inc(ev("xl_G7"), 1)
                    n += 1

                def down_evac(t, s, i, ps, tk, g=g):
                    row = B1[:, ds(t, 1), :].rearrange("p a t -> p (a t)")
                    ins = V.tensor_copy(row, ps[:]) if g == 0 else V.tensor_tensor(row, ps[:], row, ALU.add)
                    ins.then_inc(ev("z_ok"), 1)
                    dve.wait_ge(*at("z_ok", t + (g * KD + 1)))
                    dve.sem_inc(tk, 1)

                tiles(G7[g], down_evac)
            dve.wait_ge(*at("n4_sd", 1))
            diagonals(T[6], NT, "n4_diag")
            dve.wait_ge(*at("n4_r", 1))
            for c in range(2):
                half = slice(c * SEQ // 2, (c + 1) * SEQ // 2)
                for k in range(KD):
                    step.link(V.tensor_tensor(B1[:, k, half], B1[:, k, half], PS[2][:, half], ALU.mult))
                    stt(out=B1[:, k, half], in0=B1[:, k, half], scalar=SC[:, 8, k:k + 1], in1=B2[:, k, half], op0=ALU.mult, op1=ALU.add).then_inc(ev("fin_ok"), 1)


_INS = ["x", "c", "norm_g", "mod_w", "mod_b", "w_in", "dw_w", "dw_b", "cln_g", "cln_b", "pw2_w", "pw2_b", "sc_w", "sc_b",
        "wr", "br", "wi", "bi", "lam", "w_out", "final_g", "c_2", "ctx_2", "c_ctx_2", "ada_w_2", "ada_b_2", "pre_mix_g_2",
        "post_mix_g_2", "pre_ffn_g_2", "post_ffn_g_2", "ffn_up_w_2", "ffn_conv_w_2", "ffn_conv_b_2", "ffn_down_w_2",
        "m_in_w_2", "m_in_b_2", "m_norm_g_2", "m_out_w_2"]


def kernel(**inputs):
    import numpy as _np
    import concourse.bacc as _bacc
    from concourse import mybir as _mybir
    from concourse.bass_utils import run_bass_kernel_spmd as _run

    nc = _bacc.Bacc("TRN2", target_bir_lowering=False, num_devices=1)
    arrays, args = {}, {}
    for name in _INS:
        a = _np.ascontiguousarray(inputs[name])
        arrays[f"in_{name}"] = a
        args[name] = nc.dram_tensor(f"in_{name}", a.shape, _mybir.dt.from_np(a.dtype), kind="ExternalInput").ap()
    shape = inputs["x"].shape
    out = nc.dram_tensor("out_dram", shape, _mybir.dt.float32, kind="ExternalOutput").ap()
    block_pair_kernel(nc, args, out)
    r = _run(nc, [arrays], core_ids=[0])
    return r.results[0]["out_dram"]
```
